# Optimizing a Trainium2 kernel written in Bass

```python
import jax
import jax.numpy as jnp
from jax import lax
import numpy as np

D_MODEL = 1024
BATCH = 1
SEQ = 256
DEPTH = 2

CTX_LEN = 256
GRID_W = 64
HEAD_DIM = 64
ROPE_THETA = 10000.0
QBLK = 128
EPS = 1e-6

A_HEADS = (D_MODEL // 2) // HEAD_DIM
A_KV_HEADS = A_HEADS // 4
A_WIDTH = A_HEADS * HEAD_DIM
B_WIDTH = D_MODEL - A_WIDTH
CONV_WIDTH = 31
AB_IN = A_WIDTH + 2 * A_KV_HEADS * HEAD_DIM + 2 * B_WIDTH

C_HEADS = (D_MODEL // 2) // HEAD_DIM
C_KV_HEADS = C_HEADS // 4
C_WIDTH = C_HEADS * HEAD_DIM
WINDOW = 128
D_WIDTH = D_MODEL - C_WIDTH
POOL_SIZES = (2, 4, 8, 16)
POOL_GROUP_WIDTH = D_WIDTH // len(POOL_SIZES)
CD_IN = C_WIDTH + 2 * C_KV_HEADS * HEAD_DIM + D_WIDTH

N_EXPERT_GROUPS = 4
EXPERTS_PER_GROUP = 8
N_EXPERTS = N_EXPERT_GROUPS * EXPERTS_PER_GROUP
TOP_K_INNER = 2
D_EXPERT = D_MODEL // 2
MOE_BLOCK = 128


def _rmsnorm(x, g):
    xf = x.astype(jnp.float32)
    y = xf * lax.rsqrt(jnp.mean(xf * xf, axis=-1, keepdims=True) + EPS)
    return (y * g.astype(jnp.float32)).astype(x.dtype)

def _modulate(h, shift, scale):
    return h * (1 + scale) + shift

def _rope_tables(n_lat):
    rows = n_lat // GRID_W
    row = jnp.repeat(jnp.arange(rows, dtype=jnp.float32), GRID_W)
    col = jnp.tile(jnp.arange(GRID_W, dtype=jnp.float32), rows)
    n_freq = HEAD_DIM // 4
    inv = ROPE_THETA ** (-jnp.arange(n_freq, dtype=jnp.float32) / n_freq)
    ang = jnp.concatenate([row[:, None] * inv, col[:, None] * inv], axis=-1)
    return jnp.cos(ang), jnp.sin(ang)

def _rope(x, cos, sin):
    half = HEAD_DIM // 2
    x1, x2 = x[..., :half], x[..., half:]
    c = cos.astype(x.dtype)
    s = sin.astype(x.dtype)
    return jnp.concatenate([x1 * c - x2 * s, x2 * c + x1 * s], axis=-1)

def _heads(t, n):
    b, s, _ = t.shape
    return t.reshape(b, s, n, HEAD_DIM).transpose(0, 2, 1, 3)

def _group(q, n_kv):
    b, h, s, d = q.shape
    return q.reshape(b, n_kv, h // n_kv, s, d)

def _merge(o):
    b, k, g, s, d = o.shape
    return o.transpose(0, 3, 1, 2, 4).reshape(b, s, k * g * d)

def _attend(q, k, v, mask, sink):
    s = jnp.einsum('bkgqd,bksd->bkgqs', q, k).astype(jnp.float32) * (HEAD_DIM ** -0.5)
    if mask is not None:
        s = jnp.where(mask, s, -jnp.inf)
    if sink is None:
        p = jax.nn.softmax(s, axis=-1)
    else:
        sk = jnp.broadcast_to(sink.astype(jnp.float32)[None, :, :, None, None], s.shape[:-1] + (1,))
        p = jax.nn.softmax(jnp.concatenate([s, sk], axis=-1), axis=-1)[..., :-1]
    return jnp.einsum('bkgqs,bksd->bkgqd', p.astype(v.dtype), v)

def _dense_attn_blocks(q, k, v):
    b, hk, g, s, d = q.shape
    nb = s // QBLK
    qb = jnp.moveaxis(q.reshape(b, hk, g, nb, QBLK, d), 3, 0)
    ob = lax.map(lambda qi: _attend(qi, k, v, None, None), qb)
    return jnp.moveaxis(ob, 0, 3).reshape(b, hk, g, s, d)

def _window_attn_blocks(q, k_lat, v_lat, k_ctx, v_ctx, sink):
    b, hk, g, s, d = q.shape
    nb = s // QBLK
    span = QBLK + 2 * WINDOW
    n_ctx = k_ctx.shape[2]
    pad = ((0, 0), (0, 0), (WINDOW, WINDOW), (0, 0))
    kp = jnp.pad(k_lat, pad)
    vp = jnp.pad(v_lat, pad)
    qb = jnp.moveaxis(q.reshape(b, hk, g, nb, QBLK, d), 3, 0)
    r = jnp.arange(QBLK)
    j = jnp.arange(span)
    ctx_mask = jnp.ones((QBLK, n_ctx), dtype=bool)

    def block(args):
        qi, i = args
        start = i * QBLK
        kw = lax.dynamic_slice_in_dim(kp, start, span, axis=2)
        vw = lax.dynamic_slice_in_dim(vp, start, span, axis=2)
        qpos = start + r
        kpos = start - WINDOW + j
        band = (jnp.abs(qpos[:, None] - kpos[None, :]) <= WINDOW) & ((kpos >= 0) & (kpos < s))[None, :]
        mask = jnp.concatenate([ctx_mask, band], axis=1)
        return _attend(qi, jnp.concatenate([k_ctx, kw], axis=2), jnp.concatenate([v_ctx, vw], axis=2), mask, sink)

    ob = lax.map(block, (qb, jnp.arange(nb)))
    return jnp.moveaxis(ob, 0, 3).reshape(b, hk, g, s, d)

def _conv_module(u, conv_w, conv_b, ln_g, ln_b):
    a, gate = jnp.split(u, 2, axis=-1)
    glu = a * jax.nn.sigmoid(gate)
    y = lax.conv_general_dilated(glu, conv_w[:, None, :], window_strides=(1,),
                                 padding=[(CONV_WIDTH // 2, CONV_WIDTH // 2)],
                                 dimension_numbers=('NWC', 'WIO', 'NWC'),
                                 feature_group_count=B_WIDTH) + conv_b
    yf = y.astype(jnp.float32)
    mu = jnp.mean(yf, axis=-1, keepdims=True)
    var = jnp.mean((yf - mu) ** 2, axis=-1, keepdims=True)
    yn = ((yf - mu) * lax.rsqrt(var + EPS) * ln_g.astype(jnp.float32) + ln_b.astype(jnp.float32)).astype(u.dtype)
    return jax.nn.silu(yn)

def _pool_mixer(u, pool_w, pool_scale):
    b, s, _ = u.shape
    uf = u.astype(jnp.float32)
    cs = jnp.pad(jnp.cumsum(uf, axis=1), ((0, 0), (1, 0), (0, 0)))
    t = jnp.arange(s)
    outs = []
    for gi, w in enumerate(POOL_SIZES):
        lo_c, hi_c = gi * POOL_GROUP_WIDTH, (gi + 1) * POOL_GROUP_WIDTH
        lo = jnp.clip(t - w // 2, 0, s)
        hi = jnp.clip(t - w // 2 + w, 0, s)
        csg = cs[..., lo_c:hi_c]
        mean = (jnp.take(csg, hi, axis=1) - jnp.take(csg, lo, axis=1)) / (hi - lo).astype(jnp.float32)[None, :, None]
        outs.append(mean - uf[..., lo_c:hi_c])
    p = jnp.stack(outs, axis=2).astype(u.dtype)
    y = jnp.einsum('bsgc,gcd->bsgd', p, pool_w).reshape(b, s, D_WIDTH)
    return y * pool_scale

def _mixer_ab(hx, hc, w_in, w_out, q_g, k_g, conv_w, conv_b, ln_g, ln_b, cos, sin, ctx_out):
    kvw = A_KV_HEADS * HEAD_DIM
    o_k, o_v, o_u = A_WIDTH, A_WIDTH + kvw, A_WIDTH + 2 * kvw
    px = hx @ w_in
    qx = _rope(_rmsnorm(_heads(px[..., :o_k], A_HEADS), q_g), cos, sin)
    kx = _rope(_rmsnorm(_heads(px[..., o_k:o_v], A_KV_HEADS), k_g), cos, sin)
    vx = _heads(px[..., o_v:o_u], A_KV_HEADS)
    if ctx_out:
        pc = hc @ w_in
        kvc = pc[..., o_k:o_u]
    else:
        kvc = hc @ w_in[:, o_k:o_u]
    kc = _rmsnorm(_heads(kvc[..., :kvw], A_KV_HEADS), k_g)
    vc = _heads(kvc[..., kvw:], A_KV_HEADS)
    ox = _dense_attn_blocks(_group(qx, A_KV_HEADS), jnp.concatenate([kc, kx], axis=2), jnp.concatenate([vc, vx], axis=2))
    bx = _conv_module(px[..., o_u:], conv_w, conv_b, ln_g, ln_b)
    yx = jnp.concatenate([_merge(ox), bx], axis=-1) @ w_out
    if not ctx_out:
        return yx, None
    qc = _rmsnorm(_heads(pc[..., :o_k], A_HEADS), q_g)
    oc = _attend(_group(qc, A_KV_HEADS), kc, vc, None, None)
    bc = _conv_module(pc[..., o_u:], conv_w, conv_b, ln_g, ln_b)
    yc = jnp.concatenate([_merge(oc), bc], axis=-1) @ w_out
    return yx, yc

def _mixer_cd(hx, hc, w_in, w_out, q_g, k_g, sink, pool_w, pool_scale, cos, sin, ctx_out):
    kvw = C_KV_HEADS * HEAD_DIM
    o_k, o_v, o_u = C_WIDTH, C_WIDTH + kvw, C_WIDTH + 2 * kvw
    sink_g = sink.reshape(C_KV_HEADS, C_HEADS // C_KV_HEADS)
    px = hx @ w_in
    qx = _rope(_rmsnorm(_heads(px[..., :o_k], C_HEADS), q_g), cos, sin)
    kx = _rope(_rmsnorm(_heads(px[..., o_k:o_v], C_KV_HEADS), k_g), cos, sin)
    vx = _heads(px[..., o_v:o_u], C_KV_HEADS)
    if ctx_out:
        pc = hc @ w_in
        kvc = pc[..., o_k:o_u]
    else:
        kvc = hc @ w_in[:, o_k:o_u]
    kc = _rmsnorm(_heads(kvc[..., :kvw], C_KV_HEADS), k_g)
    vc = _heads(kvc[..., kvw:], C_KV_HEADS)
    ox = _window_attn_blocks(_group(qx, C_KV_HEADS), kx, vx, kc, vc, sink_g)
    dx = _pool_mixer(px[..., o_u:], pool_w, pool_scale)
    yx = jnp.concatenate([_merge(ox), dx], axis=-1) @ w_out
    if not ctx_out:
        return yx, None
    qc = _rmsnorm(_heads(pc[..., :o_k], C_HEADS), q_g)
    oc = _attend(_group(qc, C_KV_HEADS), kc, vc, None, sink_g)
    dc = _pool_mixer(pc[..., o_u:], pool_w, pool_scale)
    yc = jnp.concatenate([_merge(oc), dc], axis=-1) @ w_out
    return yx, yc

def _moe(h, grp_w, grp_b, exp_w, exp_b, w_gate, w_up, w_down):
    n_tok, d = h.shape
    tok_idx = jnp.arange(n_tok)
    g_logits = (h @ grp_w).astype(jnp.float32) + grp_b.astype(jnp.float32)
    g_sel = jnp.argmax(g_logits, axis=-1)
    g_w = jax.nn.softmax(g_logits, axis=-1)[tok_idx, g_sel]
    e_logits = ((h @ exp_w).astype(jnp.float32) + exp_b.astype(jnp.float32)).reshape(n_tok, N_EXPERT_GROUPS, EXPERTS_PER_GROUP)[tok_idx, g_sel]
    e_p, e_i = lax.top_k(jax.nn.softmax(e_logits, axis=-1), TOP_K_INNER)
    wts = (g_w[:, None] * e_p / jnp.sum(e_p, axis=-1, keepdims=True)).reshape(-1)
    eid = (g_sel[:, None] * EXPERTS_PER_GROUP + e_i).reshape(-1).astype(jnp.int32)
    n_asg = n_tok * TOP_K_INNER
    flat_tok = jnp.repeat(tok_idx, TOP_K_INNER).astype(jnp.int32)
    order = jnp.argsort(eid)
    se, stok, sw = eid[order], flat_tok[order], wts[order]
    counts = jnp.bincount(eid, length=N_EXPERTS).astype(jnp.int32)
    padded = (counts + MOE_BLOCK - 1) // MOE_BLOCK * MOE_BLOCK
    start = jnp.cumsum(counts) - counts
    pend = jnp.cumsum(padded)
    dest = (pend - padded)[se] + jnp.arange(n_asg, dtype=jnp.int32) - start[se]
    n_blk = -(-(n_asg + N_EXPERTS * (MOE_BLOCK - 1)) // MOE_BLOCK)
    cap = n_blk * MOE_BLOCK
    buf_tok = jnp.full((cap,), n_tok, jnp.int32).at[dest].set(stok)
    buf_w = jnp.zeros((cap,), h.dtype).at[dest].set(sw.astype(h.dtype))
    blk_e = jnp.minimum(jnp.searchsorted(pend, jnp.arange(n_blk, dtype=jnp.int32) * MOE_BLOCK, side='right'), N_EXPERTS - 1)
    h_pad = jnp.concatenate([h, jnp.zeros((1, d), h.dtype)], axis=0)

    def run(args):
        tok, wt, e = args
        xb = h_pad[tok]
        hid = jax.nn.silu(xb @ w_gate[e]) * (xb @ w_up[e])
        return (hid @ w_down[e]) * wt[:, None]

    ys = lax.map(run, (buf_tok.reshape(n_blk, MOE_BLOCK), buf_w.reshape(n_blk, MOE_BLOCK), blk_e))
    out = jnp.zeros((n_tok + 1, d), h.dtype).at[buf_tok].add(ys.reshape(cap, d))
    return out[:n_tok]

def first_inputs(seed: int = 0) -> dict:
    key = jax.random.key(seed)
    keys = jax.random.split(key, 48)
    counter = iter(range(48))

    def nrm(shape, scale):
        return jax.random.normal(keys[next(counter)], shape, jnp.float32) * scale

    n_even = (DEPTH + 1) // 2
    n_odd = DEPTH // 2
    dm = D_MODEL
    return {
        'x': nrm((BATCH, SEQ, dm), 1.0),
        'c': nrm((BATCH, dm), 1.0),
        'ctx': nrm((BATCH, CTX_LEN, dm), 1.0),
        'c_ctx': nrm((dm,), 1.0),
        'mod_w': nrm((DEPTH, dm, 6 * dm), 0.5 * dm ** -0.5),
        'mod_b': nrm((DEPTH, 6 * dm), 0.02),
        'ln1_g': 1.0 + nrm((DEPTH, dm), 0.02),
        'ln2_g': 1.0 + nrm((DEPTH, dm), 0.02),
        'w_in_ab': nrm((n_even, dm, AB_IN), dm ** -0.5),
        'w_out_ab': nrm((n_even, A_WIDTH + B_WIDTH, dm), dm ** -0.5),
        'q_norm_a': 1.0 + nrm((n_even, HEAD_DIM), 0.02),
        'k_norm_a': 1.0 + nrm((n_even, HEAD_DIM), 0.02),
        'conv_w': nrm((n_even, CONV_WIDTH, B_WIDTH), CONV_WIDTH ** -0.5),
        'conv_b': nrm((n_even, B_WIDTH), 0.02),
        'conv_ln_g': 1.0 + nrm((n_even, B_WIDTH), 0.02),
        'conv_ln_b': nrm((n_even, B_WIDTH), 0.02),
        'w_in_cd': nrm((n_odd, dm, CD_IN), dm ** -0.5),
        'w_out_cd': nrm((n_odd, C_WIDTH + D_WIDTH, dm), dm ** -0.5),
        'q_norm_c': 1.0 + nrm((n_odd, HEAD_DIM), 0.02),
        'k_norm_c': 1.0 + nrm((n_odd, HEAD_DIM), 0.02),
        'sink_c': nrm((n_odd, C_HEADS), 0.5),
        'pool_w': nrm((n_odd, len(POOL_SIZES), POOL_GROUP_WIDTH, POOL_GROUP_WIDTH), POOL_GROUP_WIDTH ** -0.5),
        'pool_scale': 1.0 + nrm((n_odd, D_WIDTH), 0.02),
        'rt_grp_w': nrm((DEPTH, dm, N_EXPERT_GROUPS), dm ** -0.5),
        'rt_grp_b': nrm((DEPTH, N_EXPERT_GROUPS), 0.01),
        'rt_exp_w': nrm((DEPTH, dm, N_EXPERTS), dm ** -0.5),
        'rt_exp_b': nrm((DEPTH, N_EXPERTS), 0.01),
        'ex_gate': nrm((DEPTH, N_EXPERTS, dm, D_EXPERT), dm ** -0.5),
        'ex_up': nrm((DEPTH, N_EXPERTS, dm, D_EXPERT), dm ** -0.5),
        'ex_down': nrm((DEPTH, N_EXPERTS, D_EXPERT, dm), D_EXPERT ** -0.5),
    }

def first_block(x, c, ctx, c_ctx, mod_w, mod_b, ln1_g, ln2_g,
              w_in_ab, w_out_ab, q_norm_a, k_norm_a, conv_w, conv_b, conv_ln_g, conv_ln_b,
              w_in_cd, w_out_cd, q_norm_c, k_norm_c, sink_c, pool_w, pool_scale,
              rt_grp_w, rt_grp_b, rt_exp_w, rt_exp_b, ex_gate, ex_up, ex_down):
    b, s, dm = x.shape
    cos, sin = _rope_tables(s)
    for i in range(DEPTH):
        last = i == DEPTH - 1
        li = i // 2
        mod = jax.nn.silu(c) @ mod_w[i] + mod_b[i]
        modc = jax.nn.silu(c_ctx) @ mod_w[i] + mod_b[i]
        sh1, sc1, g1, sh2, sc2, g2 = jnp.split(mod[:, None, :], 6, axis=-1)
        sh1c, sc1c, g1c, sh2c, sc2c, g2c = jnp.split(modc[None, None, :], 6, axis=-1)
        hx = _modulate(_rmsnorm(x, ln1_g[i]), sh1, sc1)
        hc = _modulate(_rmsnorm(ctx, ln1_g[i]), sh1c, sc1c)
        if i % 2 == 0:
            yx, yc = _mixer_ab(hx, hc, w_in_ab[li], w_out_ab[li], q_norm_a[li], k_norm_a[li],
                               conv_w[li], conv_b[li], conv_ln_g[li], conv_ln_b[li], cos, sin, not last)
        else:
            yx, yc = _mixer_cd(hx, hc, w_in_cd[li], w_out_cd[li], q_norm_c[li], k_norm_c[li],
                               sink_c[li], pool_w[li], pool_scale[li], cos, sin, not last)
        x = x + g1 * yx
        hx = _modulate(_rmsnorm(x, ln2_g[i]), sh2, sc2)
        if last:
            ox = _moe(hx.reshape(b * s, dm), rt_grp_w[i], rt_grp_b[i], rt_exp_w[i], rt_exp_b[i],
                      ex_gate[i], ex_up[i], ex_down[i]).reshape(b, s, dm)
            x = x + g2 * ox
        else:
            ctx = ctx + g1c * yc
            hc = _modulate(_rmsnorm(ctx, ln2_g[i]), sh2c, sc2c)
            n_ctx = ctx.shape[1]
            tokens = jnp.concatenate([hc, hx], axis=1).reshape(-1, dm)
            out = _moe(tokens, rt_grp_w[i], rt_grp_b[i], rt_exp_w[i], rt_exp_b[i],
                       ex_gate[i], ex_up[i], ex_down[i]).reshape(b, n_ctx + s, dm)
            ctx = ctx + g2c * out[:, :n_ctx]
            x = x + g2 * out[:, n_ctx:]
    return x


HGRN_WIDTH = D_MODEL // 2
HGRN_HEAD_DIM = 128
HGRN_HEADS = HGRN_WIDTH // HGRN_HEAD_DIM
HGRN_CHUNK = 64
HGRN_PROJ = 4 * HGRN_WIDTH
RWKV_WIDTH = D_MODEL // 2
RWKV_HEAD_DIM = 64
RWKV_HEADS = RWKV_WIDTH // RWKV_HEAD_DIM
RWKV_DECAY_LORA = 64
RWKV_AAA_LORA = 64
RWKV_GATE_LORA = 128
RWKV_LN_EPS = 64e-5
RWKV_PROJ = 3 * RWKV_WIDTH + RWKV_DECAY_LORA + RWKV_AAA_LORA + RWKV_GATE_LORA
AR_PROJ = HGRN_PROJ + RWKV_PROJ
ATTN_HEADS = 8
ATTN_HEAD_DIM = D_MODEL // ATTN_HEADS
MOBA_BLOCK = 256
MOBA_TOPK = 3
MOBA_QCHUNK = 64
D_FF = 4 * D_MODEL
PLE_DIM = 256
N_EVEN = (DEPTH + 1) // 2
N_ODD = DEPTH // 2
NORM_EPS = 1e-6


def rms_norm(x, g, eps=NORM_EPS):
    xf = x.astype(jnp.float32)
    y = xf * lax.rsqrt(jnp.mean(xf * xf, axis=-1, keepdims=True) + eps)
    return (y * g.astype(jnp.float32)).astype(x.dtype)

def head_layer_norm(y, w, b, eps=RWKV_LN_EPS):
    yf = y.astype(jnp.float32)
    mu = jnp.mean(yf, axis=-1, keepdims=True)
    var = jnp.mean(jnp.square(yf - mu), axis=-1, keepdims=True)
    return (yf - mu) * lax.rsqrt(var + eps) * w + b

def rotary(x, pos):
    half = x.shape[-1] // 2
    inv_freq = jnp.power(ROPE_THETA, -jnp.arange(half, dtype=jnp.float32) / half)
    ang = pos.astype(jnp.float32)[:, None] * inv_freq[None, :]
    cos = jnp.cos(ang)[None, :, None, :]
    sin = jnp.sin(ang)[None, :, None, :]
    xf = x.astype(jnp.float32)
    x1, x2 = xf[..., :half], xf[..., half:]
    return jnp.concatenate([x1 * cos - x2 * sin, x2 * cos + x1 * sin], axis=-1).astype(x.dtype)

def token_shift(u):
    return jnp.pad(u[:, :-1], ((0, 0), (1, 0), (0, 0)))

def hgrn2_chunked(q, k, v, log_f):
    B, H, S, dk = q.shape
    dv = v.shape[-1]
    C = HGRN_CHUNK
    n = S // C

    def to_chunks(t):
        return t.reshape(B, H, n, C, t.shape[-1]).transpose(2, 0, 1, 3, 4)

    causal = jnp.tril(jnp.ones((C, C), dtype=bool))

    def step(state, inp):
        qc, kc, vc, gc = inp
        b = jnp.cumsum(gc, axis=2)
        o_inter = jnp.einsum('bhtk,bhkv->bhtv', qc * jnp.exp(b), state)
        diff = jnp.where(causal[None, None, :, :, None],
                         b[:, :, :, None, :] - b[:, :, None, :, :], -jnp.inf)
        scores = jnp.einsum('bhtk,bhsk,bhtsk->bhts', qc, kc, jnp.exp(diff))
        o_intra = jnp.einsum('bhts,bhsv->bhtv', scores, vc)
        b_last = b[:, :, -1:, :]
        state = (state * jnp.exp(b_last)[:, :, 0, :, None]
                 + jnp.einsum('bhsk,bhsv->bhkv', kc * jnp.exp(b_last - b), vc))
        return state, o_inter + o_intra

    state0 = jnp.zeros((B, H, dk, dv), jnp.float32)
    _, o = lax.scan(step, state0, (to_chunks(q), to_chunks(k), to_chunks(v), to_chunks(log_f)))
    return o.transpose(1, 2, 0, 3, 4).reshape(B, H, S, dv)

def rwkv7_scan(r, decay, k, v, kk, a):
    B, S, H, N = r.shape

    def step(state, inp):
        r_t, w_t, k_t, v_t, kk_t, a_t = inp
        sa = jnp.einsum('bhvk,bhk->bhv', state, -kk_t)
        state = (state * w_t[:, :, None, :]
                 + sa[..., None] * (kk_t * a_t)[:, :, None, :]
                 + v_t[..., None] * k_t[:, :, None, :])
        return state, jnp.einsum('bhvk,bhk->bhv', state, r_t)

    xs = (r.transpose(1, 0, 2, 3), decay.transpose(1, 0, 2, 3), k.transpose(1, 0, 2, 3),
          v.transpose(1, 0, 2, 3), kk.transpose(1, 0, 2, 3), a.transpose(1, 0, 2, 3))
    state0 = jnp.zeros((B, H, N, N), jnp.float32)
    _, y = lax.scan(step, state0, xs)
    return y.transpose(1, 0, 2, 3)

def hgrn_rwkv_mixer(h, w_in, w_out, lb, onorm, mu, w0, w2, a0, a2, g2, k_k, k_a, r_k, ln_w, ln_b):
    B, S, _ = h.shape
    u = (h @ w_in).astype(jnp.float32)
    hq, hf, hi, hg, ur = jnp.split(u, [HGRN_WIDTH, 2 * HGRN_WIDTH, 3 * HGRN_WIDTH, HGRN_PROJ], axis=-1)

    def heads(t, n_heads):
        return t.reshape(B, S, n_heads, -1).transpose(0, 2, 1, 3)

    f = lb + (1.0 - lb) * jax.nn.sigmoid(hf)
    o_a = hgrn2_chunked(heads(jax.nn.silu(hq), HGRN_HEADS), heads(1.0 - f, HGRN_HEADS),
                        heads(hi, HGRN_HEADS), heads(jnp.log(f), HGRN_HEADS))
    o_a = rms_norm(o_a.transpose(0, 2, 1, 3), onorm.reshape(HGRN_HEADS, HGRN_HEAD_DIM))
    o_a = o_a.reshape(B, S, HGRN_WIDTH) * jax.nn.silu(hg)

    ur = ur + (token_shift(ur) - ur) * mu
    r, k, v, wd, ad, gd = jnp.split(
        ur, [RWKV_WIDTH, 2 * RWKV_WIDTH, 3 * RWKV_WIDTH, 3 * RWKV_WIDTH + RWKV_DECAY_LORA,
             3 * RWKV_WIDTH + RWKV_DECAY_LORA + RWKV_AAA_LORA], axis=-1)
    w = -jax.nn.softplus(-(w0 + jnp.tanh(wd) @ w2)) - 0.5
    decay = jnp.exp(-jnp.exp(w))
    a = jax.nn.sigmoid(a0 + ad @ a2)
    g = jax.nn.sigmoid(gd) @ g2
    kk = (k * k_k).reshape(B, S, RWKV_HEADS, RWKV_HEAD_DIM)
    kk = kk / jnp.maximum(jnp.sqrt(jnp.sum(kk * kk, axis=-1, keepdims=True)), 1e-12)
    k = k * (1.0 + (a - 1.0) * k_a)

    def rh(t):
        return t.reshape(B, S, RWKV_HEADS, RWKV_HEAD_DIM)

    r4, k4, v4 = rh(r), rh(k), rh(v)
    y = rwkv7_scan(r4, rh(decay), k4, v4, kk, rh(a))
    y = head_layer_norm(y, ln_w.reshape(RWKV_HEADS, RWKV_HEAD_DIM),
                        ln_b.reshape(RWKV_HEADS, RWKV_HEAD_DIM))
    bonus = jnp.sum(r4 * k4 * r_k.reshape(RWKV_HEADS, RWKV_HEAD_DIM), axis=-1, keepdims=True) * v4
    o_b = (y + bonus).reshape(B, S, RWKV_WIDTH) * g

    o = jnp.concatenate([o_a, o_b], axis=-1).astype(h.dtype)
    return o @ w_out

def moba_attention(q, k, v):
    B, H, S, Dh = q.shape
    nb = -(-S // MOBA_BLOCK)
    pad = nb * MOBA_BLOCK - S
    kb = jnp.pad(k, ((0, 0), (0, 0), (0, pad), (0, 0))).reshape(B, H, nb, MOBA_BLOCK, Dh)
    vb = jnp.pad(v, ((0, 0), (0, 0), (0, pad), (0, 0))).reshape(B, H, nb, MOBA_BLOCK, Dh)
    scale = Dh ** -0.5
    q_blk = jnp.arange(S) // MOBA_BLOCK
    n_sel = min(MOBA_TOPK, nb - 1)
    if n_sel > 0:
        k_mean = jnp.mean(kb.astype(jnp.float32), axis=3)
        gate = jnp.einsum('bhsd,bhnd->bhsn', q.astype(jnp.float32), k_mean)
        past = jnp.arange(nb)[None, :] < q_blk[:, None]
        gate = jnp.where(past, gate, -jnp.inf)
        _, sel = lax.top_k(gate, n_sel)
    else:
        sel = jnp.zeros((B, H, S, 0), jnp.int32)
    valid = jnp.arange(n_sel)[None, :] < q_blk[:, None]

    qc_size = MOBA_QCHUNK
    nc = S // qc_size
    q_chunks = q.reshape(B, H, nc, qc_size, Dh).transpose(2, 0, 1, 3, 4)
    sel_chunks = sel.reshape(B, H, nc, qc_size, n_sel).transpose(2, 0, 1, 3, 4)
    valid_chunks = valid.reshape(nc, qc_size, n_sel)
    bi = jnp.arange(B)[:, None, None]
    hi = jnp.arange(H)[None, :, None]

    def attend_chunk(inp):
        c, qc, sel_c, valid_c = inp
        q_pos = c * qc_size + jnp.arange(qc_size)
        own = (c * qc_size) // MOBA_BLOCK
        k_own = lax.dynamic_index_in_dim(kb, own, axis=2, keepdims=False)
        v_own = lax.dynamic_index_in_dim(vb, own, axis=2, keepdims=False)
        k_pos = own * MOBA_BLOCK + jnp.arange(MOBA_BLOCK)
        s_own = jnp.einsum('bhqd,bhkd->bhqk', qc, k_own).astype(jnp.float32) * scale
        scores = [jnp.where(k_pos[None, :] <= q_pos[:, None], s_own, -jnp.inf)]
        for j in range(n_sel):
            k_sel = kb[bi, hi, sel_c[..., j]]
            s = jnp.einsum('bhqd,bhqkd->bhqk', qc, k_sel).astype(jnp.float32) * scale
            scores.append(jnp.where(valid_c[:, j][:, None], s, -jnp.inf))
        probs = jax.nn.softmax(jnp.concatenate(scores, axis=-1), axis=-1).astype(vb.dtype)
        out = jnp.einsum('bhqk,bhkd->bhqd', probs[..., :MOBA_BLOCK], v_own)
        for j in range(n_sel):
            v_sel = vb[bi, hi, sel_c[..., j]]
            p_j = probs[..., (j + 1) * MOBA_BLOCK:(j + 2) * MOBA_BLOCK]
            out = out + jnp.einsum('bhqk,bhqkd->bhqd', p_j, v_sel)
        return out

    o = lax.map(attend_chunk, (jnp.arange(nc), q_chunks, sel_chunks, valid_chunks))
    return o.transpose(1, 2, 0, 3, 4).reshape(B, H, S, Dh)

def moba_mixer(h, w_qkv, w_o, q_gain, k_gain, pos):
    B, S, D = h.shape
    q, k, v = jnp.split(h @ w_qkv, 3, axis=-1)
    q = q.reshape(B, S, ATTN_HEADS, ATTN_HEAD_DIM)
    k = k.reshape(B, S, ATTN_HEADS, ATTN_HEAD_DIM)
    v = v.reshape(B, S, ATTN_HEADS, ATTN_HEAD_DIM)
    q = rotary(rms_norm(q, q_gain), pos)
    k = rotary(rms_norm(k, k_gain), pos)
    o = moba_attention(q.transpose(0, 2, 1, 3), k.transpose(0, 2, 1, 3), v.transpose(0, 2, 1, 3))
    return o.transpose(0, 2, 1, 3).reshape(B, S, D) @ w_o

def second_inputs(seed: int = 0) -> dict:
    key = jax.random.key(seed)
    ks = iter(jax.random.split(key, 40))

    def normal(shape, scale):
        return jax.random.normal(next(ks), shape, jnp.float32) * scale

    def gain(shape):
        return 1.0 + normal(shape, 0.05)

    D = D_MODEL
    mix_w = HGRN_WIDTH + RWKV_WIDTH
    return {
        'x': normal((BATCH, SEQ, D), 1.0),
        'p': normal((DEPTH, BATCH, SEQ, PLE_DIM), 1.0),
        'attn_norm': gain((DEPTH, D)),
        'mlp_norm': gain((DEPTH, D)),
        'w_in_ar': normal((N_EVEN, D, AR_PROJ), D ** -0.5),
        'w_out_ar': normal((N_EVEN, mix_w, D), mix_w ** -0.5),
        'hgrn_lb': normal((DEPTH + 1, HGRN_WIDTH), 0.5),
        'hgrn_onorm': gain((N_EVEN, HGRN_WIDTH)),
        'rwkv_mu': jax.random.uniform(next(ks), (N_EVEN, RWKV_PROJ), jnp.float32),
        'rwkv_w0': jax.random.uniform(next(ks), (N_EVEN, RWKV_WIDTH), jnp.float32, -3.0, 1.0),
        'rwkv_w2': normal((N_EVEN, RWKV_DECAY_LORA, RWKV_WIDTH), 0.1 * RWKV_DECAY_LORA ** -0.5),
        'rwkv_a0': normal((N_EVEN, RWKV_WIDTH), 0.5),
        'rwkv_a2': normal((N_EVEN, RWKV_AAA_LORA, RWKV_WIDTH), 0.1 * RWKV_AAA_LORA ** -0.5),
        'rwkv_g2': normal((N_EVEN, RWKV_GATE_LORA, RWKV_WIDTH), RWKV_GATE_LORA ** -0.5),
        'rwkv_kk': 0.85 + normal((N_EVEN, RWKV_WIDTH), 0.05),
        'rwkv_ka': 1.0 + normal((N_EVEN, RWKV_WIDTH), 0.05),
        'rwkv_rk': normal((N_EVEN, RWKV_WIDTH), 0.1),
        'rwkv_ln_w': gain((N_EVEN, RWKV_WIDTH)),
        'rwkv_ln_b': normal((N_EVEN, RWKV_WIDTH), 0.02),
        'w_qkv': normal((N_ODD, D, 3 * D), D ** -0.5),
        'w_o_attn': normal((N_ODD, D, D), D ** -0.5),
        'q_norm': gain((N_ODD, ATTN_HEAD_DIM)),
        'k_norm': gain((N_ODD, ATTN_HEAD_DIM)),
        'w_up': normal((DEPTH, D, D_FF), D ** -0.5),
        'w_down': normal((DEPTH, D_FF, D), D_FF ** -0.5),
        'ple_proj': normal((DEPTH, PLE_DIM, D), PLE_DIM ** -0.5),
        'ple_norm': gain((DEPTH, D)),
        'ple_gate': normal((DEPTH, D, D), D ** -0.5),
    }

def second_block(x, p, attn_norm, mlp_norm, w_in_ar, w_out_ar, hgrn_lb, hgrn_onorm,
              rwkv_mu, rwkv_w0, rwkv_w2, rwkv_a0, rwkv_a2, rwkv_g2, rwkv_kk, rwkv_ka, rwkv_rk,
              rwkv_ln_w, rwkv_ln_b, w_qkv, w_o_attn, q_norm, k_norm, w_up, w_down,
              ple_proj, ple_norm, ple_gate):
    S = x.shape[1]
    pos = jnp.arange(S)
    lb_all = jnp.cumsum(jax.nn.softmax(hgrn_lb.astype(jnp.float32), axis=0), axis=0)
    for l in range(DEPTH):
        h = rms_norm(x, attn_norm[l])
        if l % 2 == 0:
            e = l // 2
            mix = hgrn_rwkv_mixer(h, w_in_ar[e], w_out_ar[e], lb_all[l], hgrn_onorm[e],
                                  rwkv_mu[e], rwkv_w0[e], rwkv_w2[e], rwkv_a0[e], rwkv_a2[e],
                                  rwkv_g2[e], rwkv_kk[e], rwkv_ka[e], rwkv_rk[e],
                                  rwkv_ln_w[e], rwkv_ln_b[e])
        else:
            o = l // 2
            mix = moba_mixer(h, w_qkv[o], w_o_attn[o], q_norm[o], k_norm[o], pos)
        x = x + mix.astype(x.dtype)
        h = rms_norm(x, mlp_norm[l])
        x = x + jnp.square(jax.nn.relu(h @ w_up[l])) @ w_down[l]
        ple = rms_norm(p[l] @ ple_proj[l], ple_norm[l])
        x = x + ple * jax.nn.sigmoid(x @ ple_gate[l])
    return x


def setup_inputs(seed=0):
    out = dict(first_inputs(seed))
    for name, value in second_inputs(seed + 1).items():
        if name != "x":
            out[name + "_2"] = value
    return out


def reference(
    x, c, ctx, c_ctx, mod_w, mod_b, ln1_g, ln2_g, w_in_ab, w_out_ab, q_norm_a, k_norm_a, conv_w,
    conv_b, conv_ln_g, conv_ln_b, w_in_cd, w_out_cd, q_norm_c, k_norm_c, sink_c, pool_w,
    pool_scale, rt_grp_w, rt_grp_b, rt_exp_w, rt_exp_b, ex_gate, ex_up, ex_down, p_2,
    attn_norm_2, mlp_norm_2, w_in_ar_2, w_out_ar_2, hgrn_lb_2, hgrn_onorm_2, rwkv_mu_2,
    rwkv_w0_2, rwkv_w2_2, rwkv_a0_2, rwkv_a2_2, rwkv_g2_2, rwkv_kk_2, rwkv_ka_2, rwkv_rk_2,
    rwkv_ln_w_2, rwkv_ln_b_2, w_qkv_2, w_o_attn_2, q_norm_2, k_norm_2, w_up_2, w_down_2,
    ple_proj_2, ple_norm_2, ple_gate_2,
):
    x = first_block(
        x, c, ctx, c_ctx, mod_w, mod_b, ln1_g, ln2_g, w_in_ab, w_out_ab, q_norm_a, k_norm_a,
        conv_w, conv_b, conv_ln_g, conv_ln_b, w_in_cd, w_out_cd, q_norm_c, k_norm_c, sink_c,
        pool_w, pool_scale, rt_grp_w, rt_grp_b, rt_exp_w, rt_exp_b, ex_gate, ex_up, ex_down,
    )
    return second_block(
        x, p_2, attn_norm_2, mlp_norm_2, w_in_ar_2, w_out_ar_2, hgrn_lb_2, hgrn_onorm_2,
        rwkv_mu_2, rwkv_w0_2, rwkv_w2_2, rwkv_a0_2, rwkv_a2_2, rwkv_g2_2, rwkv_kk_2, rwkv_ka_2,
        rwkv_rk_2, rwkv_ln_w_2, rwkv_ln_b_2, w_qkv_2, w_o_attn_2, q_norm_2, k_norm_2, w_up_2,
        w_down_2, ple_proj_2, ple_norm_2, ple_gate_2,
    )


_drawn_inputs = setup_inputs


def setup_inputs(seed=0):
    import zlib

    import numpy as np

    out = dict(_drawn_inputs(seed))
    spreads = {}
    factors = {'ln1_g': 5.782,
     'q_norm_a': 8.0,
     'k_norm_a': 8.0,
     'conv_b': 4.134,
     'conv_ln_g': 4.976,
     'conv_ln_b': 5.574,
     'q_norm_c': 8.0,
     'k_norm_c': 8.0,
     'sink_c': 8.0,
     'pool_scale': 7.378,
     'rt_grp_b': 23.633,
     'rt_exp_b': 17.955,
     'hgrn_lb_2': 10.117,
     'hgrn_onorm_2': 16.802,
     'rwkv_w2_2': 39.844,
     'rwkv_a2_2': 4.577,
     'rwkv_kk_2': 200.0,
     'rwkv_ka_2': 3.124,
     'rwkv_ln_w_2': 18.529,
     'rwkv_ln_b_2': 49.417,
     'q_norm_2': 42.744,
     'k_norm_2': 48.271,
     'ple_norm_2': 27.156,
     'ln2_g': 3.194,
     'mlp_norm_2': 3.914,
     'rwkv_rk_2': 3.243}
    for name, (base, spread) in spreads.items():
        noise = np.random.default_rng([zlib.crc32(name.encode()), seed]).standard_normal(out[name].shape)
        drawn = base * np.exp(spread * noise) if base else spread * noise
        out[name] = jnp.asarray(drawn.astype(out[name].dtype))
    for name, factor in factors.items():
        out[name] = (out[name] * factor).astype(out[name].dtype)
    return out
```

```python
from contextlib import ExitStack

import numpy as np
import concourse.bass as bass
from concourse import mybir

P = 128
F32 = mybir.dt.float32
I32 = mybir.dt.int32
ALU = mybir.AluOpType
ACT = mybir.ActivationFunctionType
AX = mybir.AxisListType

D = 1024
KC = D // P
SEQ = 256
NX = SEQ // P
FFN = 4 * D
NEXP, NGRP = 32, 4
EPG = NEXP // NGRP
DE = D // 2
HALF = D // 2
HC = HALF // P
TAPS = 31
HD = 64
CH = 16
NCH = P // CH
EPS = 1e-6
LN_EPS = 64e-5
BIG = 1e30
LOW = -87.0
PANEL = 4096
HEAD2 = 128
PLE = 256


def pack(entries):
    at, off = {}, 0
    for name, width in entries:
        at[name] = (off, width)
        off += width
    return at, off


CONSTS, NCONST = pack([
    ("ident", P), ("ones", P), ("before", P), ("pair_ones", P), ("chunk_before_st", P),
    ("chunk_before_ts", P), ("chunk_upto_st", P), ("chunk_of", NCH), ("restart", SEQ),
    ("cos", 4 * 32), ("sin", 4 * 32), ("cos2", NX * 64), ("sin2", NX * 64),
    ("eye_pair", 64), ("expert", NEXP), ("group", NEXP), ("token", 4), ("rowsel", 2 * P),
])
TABLES, NTABLE = pack([("band", NX * 512), ("pool", NX * 4 * SEQ), ("causal", NX * SEQ)])
COLS, NCOL = pack([
    ("ln1_0", KC), ("ln1_1", KC), ("ln2_0", KC), ("ln2_1", KC), ("cond", 2 * KC),
    ("conv_w", HC * TAPS), ("conv_b", HC), ("conv_g", HC), ("conv_lb", HC), ("pool_scale", HC),
    ("an_0", KC), ("an_1", KC), ("mn_0", KC), ("mn_1", KC), ("lb", 3 * HC), ("onorm", HC),
    ("mu", 14), ("w0", HC), ("a0", HC), ("kk", HC), ("ka", HC), ("rk", HC), ("lnw", HC), ("lnb", HC),
])
ROWS, NROW = pack([
    ("qa", HD), ("ka", HD), ("qc", HD), ("kc", HD), ("q2", HEAD2), ("k2", HEAD2), ("sink", 8),
    ("rtb_0", NGRP + NEXP), ("rtb_1", NGRP + NEXP),
])


class Signal:

    def __init__(self, sem):
        self.sem, self.sent, self.seen = sem, 0, {}

    def wait(self, eng, n=1):
        self.seen[eng.engine] = self.seen.get(eng.engine, 0) + n
        eng.wait_ge(self.sem, self.seen[eng.engine])


class Steps:

    def __init__(self, eng, order):
        self.eng, self.order = eng, order

    def __call__(self, ins, signal=None):
        s = signal or self.order
        ins.then_inc(s.sem, 1)
        s.sent += 1
        self.eng.wait_ge(s.sem, s.sent)


class Banks:

    def __init__(self, banks, full, freed):
        self.banks, self.full, self.freed = banks, full, freed
        self.filling = self.taking = 0

    def claim(self, pe):
        n = self.filling
        self.filling += 1
        if n >= len(self.banks):
            pe.wait_ge(self.freed.sem, n - len(self.banks) + 1)
        return self.banks[n % len(self.banks)]

    def settled(self, pe):
        if self.filling:
            pe.wait_ge(self.freed.sem, self.filling)

    def take(self, eng):
        n = self.taking
        self.taking += 1
        eng.wait_ge(self.full.sem, n + 1)
        return self.banks[n % len(self.banks)]


def build_program(nc, d):
    with ExitStack() as ctx:
        def signal(name):
            return Signal(ctx.enter_context(nc.semaphore(name)))

        WORK1 = 12800
        FIX = NCONST + NCOL + NROW + 2 * (3 * KC * 2) + 48 * 2 + 64
        RING, GATES, WORK = 0, 6 * PANEL, 6 * PANEL + 4096
        X = WORK + WORK1
        HT = X + 4096
        CONST = HT + 4096
        TOTAL = CONST + FIX
        big = ctx.enter_context(nc.sbuf_tensor("big", [P, TOTAL], F32))
        bigi = ctx.enter_context(nc.sbuf_tensor("bigi", [P, 24], I32))
        zeros_i = ctx.enter_context(nc.sbuf_tensor("zeros_i", [P, P], I32))[:, :]
        ibuf = ctx.enter_context(nc.sbuf_tensor("ibuf", [P, 8], mybir.dt.uint32))[:, :]
        expert_ids = ctx.enter_context(nc.sbuf_tensor("expert_ids", [P, NEXP + 8], I32))[:, :]
        pool_passed = ctx.enter_context(nc.semaphore("pool_passed"))
        psum = [ctx.enter_context(nc.psum_tensor(f"bank{i}", [P, 512], F32)) for i in range(8)]

        def view(off, *dims, p0=0, p1=P):
            n = int(np.prod(dims))
            ap = big[p0:p1, off:off + n]
            names = "abcd"[:len(dims)]
            if len(dims) > 1:
                ap = ap.rearrange(f"p ({' '.join(names)}) -> p {' '.join(names)}",
                                  **dict(zip(names[1:], dims[1:])))
            return ap

        class Space:

            def __init__(self, off, size):
                self.off, self.end = off, off + size

            def take(self, *dims):
                o = self.off
                self.off += int(np.prod(dims))
                assert self.off <= self.end, (self.off, self.end)
                return view(o, *dims)

        fixed = Space(CONST, FIX)
        const_sb, col_sb, row_sb = fixed.take(NCONST), fixed.take(NCOL), fixed.take(NROW)
        mod_col = fixed.take(48, 2)
        norm_a = fixed.take(2, KC, 2)
        small = fixed.take(96 + 32)

        def const(name, *dims):
            o, w = CONSTS[name]
            return view(CONST + o, *(dims or (w,)))

        def col(name, *dims):
            o, w = COLS[name]
            return view(CONST + NCONST + o, *(dims or (w,)))

        def row(name):
            o, w = ROWS[name]
            return row_sb[:, o:o + w]

        x = view(X, 4, D)
        hT = view(HT, KC, 512)
        gates = view(GATES, 4, D)
        ident = const("ident")
        ones = const("ones")

        loaded = signal("params_loaded")
        panel_full = [signal(f"panel_full{i}") for i in range(6)]
        panel_used = signal("panel_used")
        dve_banks = Banks(psum[0:4], signal("dve_bank_full"), signal("dve_bank_freed"))
        act_banks = Banks(psum[4:7], signal("act_bank_full"), signal("act_bank_freed"))
        dve_to_pe = signal("dve_result_for_pe")
        dve_to_act = signal("dve_result_for_act")
        dve_to_pool = signal("dve_result_for_pool")
        dve_to_sp = signal("dve_result_for_sp")
        act_to_dve = signal("act_result_for_dve")
        act_to_pe = signal("act_result_for_pe")
        act_to_pool = signal("act_result_for_pool")
        pool_to_dve = signal("pool_result_for_dve")
        pool_to_pe = signal("pool_result_for_pe")
        stage_loaded = signal("stage_table_loaded")
        pe_done = signal("pe_loop_done")
        out_written = signal("out_written")

        block = ctx.enter_context(nc.Block())

        panels = []
        slot_owner = {}
        ring = {"n": 6, "next": 0, "moe": 0}
        panel_at = [0]
        slot_uses = {}

        def add_panel(src, *dims):
            s = ring["next"] % ring["n"]
            ring["next"] += 1
            slot_uses[s] = slot_uses.get(s, 0) + 1
            panels.append((s, view(RING + s * PANEL, *dims), src, slot_owner.get(s), slot_uses[s], ring["moe"]))
            slot_owner[s] = len(panels) - 1
            return len(panels) - 1

        def load_panel(n):
            s, dst, src, before, _, moe = panels[n]
            sp = nc.sync
            if before is not None:
                sp.wait_ge(panel_used.sem, before + 1)
            if moe:
                sp.wait_ge(pe_done.sem, moe)
            sp.dma_start(dst, src).then_inc(panel_full[s].sem, 16)

        stage_at = {}

        def load_table(name, *pairs):
            for dst, src in pairs:
                sp.dma_start(dst, src).then_inc(stage_loaded.sem, 16)
                stage_loaded.sent += 16
            stage_at[name] = stage_loaded.sent

        def table_in(eng, name):
            eng.wait_ge(stage_loaded.sem, stage_at[name])

        def open_panel(pe, n):
            s, dst, _, _, use, _ = panels[n]
            pe.wait_ge(panel_full[s].sem, 16 * use)
            return dst

        def krows(w, n0=None, n1=None):
            v = w.rearrange("(c p) n -> p c n", p=P)
            return v if n0 is None else v[:, :, n0:n1]

        pe, dve, act, pool, sp = nc.tensor, nc.vector, nc.scalar, nc.gpsimd, nc.sync
        V = Steps(dve, signal("dve_order"))
        A = Steps(act, signal("act_order"))
        G = Steps(pool, signal("pool_order"))

        def tell(steps, sig):
            steps.eng.sem_inc(sig.sem, 1)
            sig.sent += 1

        def bcast(ap, *dims):
            return ap.broadcast_to([ap.shape[0], *dims])

        def mid(ap, n):
            return ap.unsqueeze(1).broadcast_to([ap.shape[0], n, ap.shape[1]])

        def last(ap, n):
            return ap.unsqueeze(len(ap.shape)).broadcast_to([*ap.shape, n])

        def mm(out, lhsT, rhs, start, stop):
            return pe.matmul(out, lhsT, rhs, start=start, stop=stop, skip_group_check=True)

        def stt(out, in0, scalar, in1, op0=ALU.mult, op1=ALU.add):
            return dve.scalar_tensor_tensor(out=out, in0=in0, scalar=scalar, in1=in1, op0=op0, op1=op1)

        def product(bank, cols, pairs, banks):
            for i, (w, m) in enumerate(pairs):
                ins = mm(bank, w, m, i == 0, i == len(pairs) - 1)
            return ins

        def full(banks, ins):
            ins.then_inc(banks.full.sem, 1)

        def used(ins_panel):
            pass

        def load_stage():
            def sp_part():
                items = [(const_sb, d["consts"]), (col_sb, d["cols"]), (row_sb, d["rows"]),
                         (x[:, 0:2, :], d["ctx"].rearrange("a (t p) n -> p (a t) n", p=P)),
                         (x[:, 2:4, :], d["x"].rearrange("a (t p) n -> p (a t) n", p=P))]
                for dst, src in items:
                    sp.dma_start(dst, src).then_inc(loaded.sem, 16)
                loaded.sent = 16 * len(items)

            def wait_all(eng):
                eng.wait_ge(loaded.sem, 16 * 5)
            return dict(sp=sp_part, pe=lambda: wait_all(pe), dve=lambda: wait_all(dve),
                        act=lambda: wait_all(act), pool=lambda: wait_all(pool))

        def mod_stage(i):
            work = Space(WORK, WORK1)
            mod_row, mod_b = work.take(6 * D), work.take(6 * D)
            cond = view(GATES, KC, 2)
            tmp = view(GATES + 64, KC, 2)
            raw = col("cond", KC, 2)
            first = [add_panel(krows(d["mod_w"][i], 512 * n, 512 * n + 512), KC, 512) for n in range(12)]

            def sp_part():
                if i:
                    stage_in_dve(sp)
                load_table(f"mod_b{i}", (mod_b[0:2, :], d["mod_b"][i]))
                for n in first:
                    load_panel(n)

            def act_part():
                if i:
                    dve_to_act.wait(act)
                A(act.activation(tmp, raw, ACT.Exp, scale=-1.0))
                tell(A, act_to_dve)

            def dve_part():
                if i:
                    tell(V, dve_to_sp)
                    tell(V, dve_to_act)
                act_to_dve.wait(dve)
                V(dve.tensor_scalar(tmp, tmp, 1.0, None, ALU.add))
                V(dve.reciprocal(tmp, tmp))
                V(dve.tensor_tensor(cond, raw, tmp, ALU.mult))
                tell(V, dve_to_pe)
                table_in(dve, f"mod_b{i}")
                for n in range(12):
                    b = dve_banks.take(dve)
                    c = slice(512 * n, 512 * n + 512)
                    V(dve.tensor_tensor(mod_row[0:2, c], b[0:2, :], mod_b[0:2, c], ALU.add), dve_banks.freed)
                b = dve_banks.take(dve)
                V(dve.tensor_copy(mod_col, b[:, 0:96].rearrange("p (n r) -> p n r", r=2)), dve_banks.freed)
                for k, at in enumerate((8, 32)):
                    V(stt(norm_a[:, k], mod_col[:, at:at + KC, :], 1.0,
                          last(col(f"ln{k + 1}_{i}"), 2), ALU.add, ALU.mult))
                for g in range(4):
                    for h in range(2):
                        b = dve_banks.take(dve)
                        V(dve.tensor_copy(gates[:, g, 512 * h:512 * h + 512], b[:, :]), dve_banks.freed)

            def pe_part():
                dve_to_pe.wait(pe)
                for n in first:
                    w = open_panel(pe, n)
                    b = dve_banks.claim(pe)
                    for c in range(KC):
                        ins = mm(b[0:2, :], cond[:, c, :], w[:, c, :], c == 0, c == KC - 1)
                    full(dve_banks, ins)
                    pe_used(n)
                dve_banks.settled(pe)
                b = dve_banks.claim(pe)
                for n in range(48):
                    ins = mm(b[:, 2 * n:2 * n + 2], mod_row[0:2, P * n:P * n + P], ident[0:2, 0:2], True, True)
                full(dve_banks, ins)
                for g in range(4):
                    at = (2 if g < 2 else 5) * D
                    for h in range(2):
                        b = dve_banks.claim(pe)
                        r = g % 2
                        full(dve_banks, mm(b[:, :], const("rowsel", 2, P)[0:2, r, :],
                                           mod_row[0:2, at + 512 * h:at + 512 * h + 512], True, True))
            return dict(sp=sp_part, act=act_part, dve=dve_part, pe=pe_part)

        def stage_in_dve(eng):
            dve_to_sp.wait(eng)

        def pe_used(n):
            b = psum[7]
            mm(b[0:2, 0:2], ident[0:2, 0:2], ident[0:2, 0:2], True, True).then_inc(panel_used.sem, 1)
            panel_used.sent += 1
            assert panel_used.sent == n + 1

        def norm_stage(tiles, gain, shift=None, first_tile=0):
            ssq, rstd = small[:, 0:4], small[:, 4:8]
            junk = view(WORK + WORK1 - 3072, D)
            xn = view(WORK + WORK1 - 2048, 2, D)

            def dve_part():
                for k, t in enumerate(tiles):
                    V(dve.tensor_tensor(junk, x[:, t, :], x[:, t, :], ALU.mult))
                    V(dve.tensor_reduce(ssq[:, k:k + 1], junk, AX.X, ALU.add))
                n = len(tiles)
                V(dve.tensor_scalar(ssq[:, 0:n], ssq[:, 0:n], 1.0 / D, EPS, ALU.mult, ALU.add))
                tell(V, dve_to_act)
                act_to_dve.wait(dve)
                for k, t in enumerate(tiles):
                    if k >= 2:
                        dve.wait_ge(dve_banks.full.sem, dve_banks.taking)
                    V(dve.tensor_scalar(xn[:, k % 2, :], x[:, t, :], rstd[:, k:k + 1], None, ALU.mult))
                    tell(V, dve_to_pe)
                    for h in range(2):
                        b = dve_banks.take(dve)
                        for j in range(4):
                            c = 4 * h + j
                            s = None if shift is None else shift(c, t)
                            o = (t - first_tile) * P
                            ins = dve.tensor_scalar(hT[:, c, o:o + P], b[:, P * j:P * j + P], gain(c, t), s,
                                                    ALU.mult, *([ALU.add] if s is not None else []))
                            V(ins, dve_banks.freed if j == 3 else None)

            def act_part():
                dve_to_act.wait(act)
                n = len(tiles)
                A(act.activation(rstd[:, 0:n], ssq[:, 0:n], ACT.Ln))
                A(act.activation(rstd[:, 0:n], rstd[:, 0:n], ACT.Exp, scale=-0.5))
                tell(A, act_to_dve)

            def pe_part():
                for k, t in enumerate(tiles):
                    dve_to_pe.wait(pe)
                    for h in range(2):
                        b = dve_banks.claim(pe)
                        for j in range(4):
                            c = 4 * h + j
                            ins = pe.transpose(b[:, P * j:P * j + P], xn[:, k % 2, P * c:P * c + P], ident)
                        full(dve_banks, ins)
                dve_banks.settled(pe)
            return dict(dve=dve_part, act=act_part, pe=pe_part)

        def rows_of_panel(n, tiles, width, lhs, banks=None):
            banks = banks or dve_banks
            w = open_panel(pe, n)
            kc = w.shape[1]
            for t in tiles:
                b = banks.claim(pe)
                for c in range(kc):
                    ins = mm(b[:, 0:width], lhs(c, t), w[:, c, :], c == 0, c == kc - 1)
                full(banks, ins)
            pe_used(n)

        def cols_of_panel(n, nblocks, ntok, off=0, banks=None):
            banks = banks or dve_banks
            w = open_panel(pe, n)
            for j in range(nblocks):
                b = banks.claim(pe)
                for c in range(KC):
                    ins = mm(b[:, 0:ntok], w[:, c, P * j:P * j + P], hT[:, c, off:off + ntok], c == 0, c == KC - 1)
                full(banks, ins)
            pe_used(n)

        def ht(c, t):
            return hT[:, c, P * t:P * t + P]

        def silu_parts(dst, src, e, n_extra=None):
            V(dve.tensor_scalar(e, e, 1.0, None, ALU.add))
            V(dve.reciprocal(e, e))
            V(dve.tensor_tensor(dst, src, e, ALU.mult))

        def exp_of(act_out, act_in, scale=1.0, func=ACT.Exp):
            dve_to_act.wait(act)
            A(act.activation(act_out, act_in, func, scale=scale))
            tell(A, act_to_dve)

        def ask_act():
            tell(V, dve_to_act)
            act_to_dve.wait(dve)

        def residual_dve(tiles, gate_of):
            tmp = view(WORK + WORK1 - 512, 512)
            for h in range(2):
                for t in tiles:
                    b = dve_banks.take(dve)
                    c = slice(512 * h, 512 * h + 512)
                    if gate_of is None:
                        V(dve.tensor_tensor(x[:, t, c], x[:, t, c], b[:, :], ALU.add), dve_banks.freed)
                    else:
                        V(dve.tensor_tensor(tmp, b[:, :], gate_of(t)[:, c], ALU.mult), dve_banks.freed)
                        V(dve.tensor_tensor(x[:, t, c], x[:, t, c], tmp, ALU.add))

        def attention(units, hd, q_of, k_of, v_of, o_of, scale, mask_of, sink_of, buf):
            s_sb, p_sb, pT = buf["s"], buf["p"], buf["pT"]
            nmax, den, rec = small[:, 8:10], small[:, 10:12], small[:, 12:14]

            def scores(n):
                h, t, nk = units[n]
                b = act_banks.claim(pe)
                full(act_banks, mm(b[:, 0:P * nk], q_of(h, t), k_of(h, nk), True, True))

            def pe_part():
                scores(0)
                for n, (h, t, nk) in enumerate(units):
                    if n + 1 < len(units):
                        scores(n + 1)
                    act_to_pe.wait(pe)
                    b = dve_banks.claim(pe)
                    for j in range(nk):
                        ins = pe.transpose(b[:, P * j:P * j + P], p_sb[:, n % 2, P * j:P * j + P], ident)
                    full(dve_banks, ins)
                    dve_banks.settled(pe)
                    b = dve_banks.claim(pe)
                    for j in range(nk):
                        ins = mm(b[:, 0:hd], pT[:, n % 2, P * j:P * j + P], v_of(h, j), j == 0, j == nk - 1)
                    full(dve_banks, ins)
                dve_banks.settled(pe)

            def highest(n):
                h, t, nk = units[n]
                at = attention_marks[id(units)][1] + n
                dve.wait_ge(act_banks.full.sem, at + 1)
                b = act_banks.banks[at % len(act_banks.banks)]
                m = nmax[:, n % 2:n % 2 + 1]
                if mask_of is None:
                    V(dve.tensor_reduce(m, b[:, 0:P * nk], AX.X, ALU.max))
                    V(dve.tensor_scalar(m, m, -scale, None, ALU.mult))
                else:
                    s = s_sb[:, n % 2, 0:P * nk]
                    V(stt(s, b[:, 0:P * nk], scale, mask_of(t, nk)))
                    V(dve.tensor_reduce(m, s, AX.X, ALU.max))
                    if sink_of is None:
                        V(dve.tensor_scalar(m, m, -1.0, None, ALU.mult))
                    else:
                        V(dve.tensor_scalar(m, m, sink_of(h), -1.0, ALU.max, ALU.mult))
                tell(V, dve_to_act)

            def dve_part():
                highest(0)
                for n, (h, t, nk) in enumerate(units):
                    if n + 1 < len(units):
                        highest(n + 1)
                    b = dve_banks.take(dve)
                    V(dve.tensor_copy(pT[:, n % 2, 0:P * nk], b[:, 0:P * nk]), dve_banks.freed)
                    k = slice(n % 2, n % 2 + 1)
                    act_to_dve.wait(dve)
                    if sink_of is not None:
                        V(dve.tensor_tensor(den[:, k], den[:, k], small[:, 14 + n % 2:15 + n % 2], ALU.add))
                    V(dve.reciprocal(rec[:, k], den[:, k]))
                    b = dve_banks.take(dve)
                    V(dve.tensor_scalar(o_of(h, t), b[:, 0:hd], rec[:, k], None, ALU.mult), dve_banks.freed)

            def act_part():
                for n, (h, t, nk) in enumerate(units):
                    k = slice(n % 2, n % 2 + 1)
                    dve_to_act.wait(act)
                    b = act_banks.take(act)
                    if n >= 2:
                        act.wait_ge(dve_banks.freed.sem, freed0[0] + 2 * (n - 1))
                    if mask_of is None:
                        A(act.activation(p_sb[:, n % 2, 0:P * nk], b[:, 0:P * nk], ACT.Exp, bias=nmax[:, k],
                                         scale=scale, accum_out=den[:, k]), act_banks.freed)
                    else:
                        if sink_of is not None:
                            A(act.activation(small[:, 14 + n % 2:15 + n % 2], sink_of(h), ACT.Exp, bias=nmax[:, k]))
                        A(act.activation(p_sb[:, n % 2, 0:P * nk], s_sb[:, n % 2, 0:P * nk], ACT.Exp,
                                         bias=nmax[:, k], accum_out=den[:, k]), act_banks.freed)
                    tell(A, act_to_pe)
                    tell(A, act_to_dve)
            freed0 = [0]

            def dve_whole():
                dve_part()

            def act_whole():
                freed0[0] = attention_marks[id(units)][0]
                act_part()

            def pe_whole():
                attention_marks[id(units)] = (dve_banks.filling, act_banks.filling)
                pe_part()
            return dict(pe=pe_whole, act=act_whole, dve=dve_whole)

        attention_marks = {}

        def head_norm_rope(src, heads, gain_of, cos, sin, hd, tmp, rope=True):
            n = len(heads)
            h0, h1 = heads[0], heads[-1] + 1
            v = src[:, h0:h1, :]
            sq = tmp[:, 0:n * hd].rearrange("p (h e) -> p h e", e=hd)
            ss = small[:, 16:16 + n]
            V(dve.tensor_tensor(sq, v, v, ALU.mult))
            V(dve.tensor_reduce(ss, sq, AX.X, ALU.add))
            V(dve.tensor_scalar(ss, ss, 1.0 / hd, EPS, ALU.mult, ALU.add))
            ask_act()
            V(dve.tensor_tensor(v, v, last(ss, hd), ALU.mult))
            for a, b_, g in gain_of:
                V(dve.tensor_tensor(src[:, a:b_, :], src[:, a:b_, :], mid(g, b_ - a), ALU.mult))
            if not rope:
                return
            hf = hd // 2
            x1, x2 = v[:, :, 0:hf], v[:, :, hf:hd]
            t1 = tmp[:, 0:n * hf].rearrange("p (h e) -> p h e", e=hf)
            t2 = tmp[:, n * hf:2 * n * hf].rearrange("p (h e) -> p h e", e=hf)
            t3 = tmp[:, 2 * n * hf:3 * n * hf].rearrange("p (h e) -> p h e", e=hf)
            c, s = mid(cos, n), mid(sin, n)
            V(dve.tensor_tensor(t1, x1, s, ALU.mult))
            V(dve.tensor_tensor(t2, x2, s, ALU.mult))
            V(dve.tensor_tensor(x1, x1, c, ALU.mult))
            V(dve.tensor_tensor(x2, x2, c, ALU.mult))
            V(dve.tensor_tensor(x1, x1, t2, ALU.subtract))
            V(dve.tensor_tensor(x2, x2, t1, ALU.add))

        def norm_act(n):
            ss = small[:, 16:16 + n]
            dve_to_act.wait(act)
            A(act.activation(ss, ss, ACT.Ln))
            A(act.activation(ss, ss, ACT.Exp, scale=-0.5))
            tell(A, act_to_dve)

        def transposed_dve(dst, tiles, heads):
            for h in heads:
                b = dve_banks.take(dve)
                hd = dst(h).shape[0]
                V(dve.tensor_copy(dst(h), b[0:hd, 0:P * len(tiles)]), dve_banks.freed)

        def transposed_pe(src, tiles, heads):
            for h in heads:
                b = dve_banks.claim(pe)
                for k, t in enumerate(tiles):
                    s = src(h, t)
                    ins = pe.transpose(b[0:s.shape[1], P * k:P * k + P], s, ident)
                full(dve_banks, ins)

        def conv_stage():
            work = Space(WORK, WORK1)
            bT = work.take(HC, 512)
            aT = work.take(HC, 512)
            pad = TAPS // 2
            cpad = work.take(HC, 2, SEQ + 2 * pad)
            acc = work.take(HC, 512)
            e = work.take(HC, 512)
            w = d["w_in_ab"][0]
            ps = [add_panel(krows(w, 768 + 512 * k, 1280 + 512 * k), KC, 512) for k in range(2)]
            cw = col("conv_w", HC, TAPS)

            def sp_part():
                for n in ps:
                    load_panel(n)

            def pe_part():
                for n in ps:
                    cols_of_panel(n, HC, 512)
                for _ in range(2):
                    dve_to_pe.wait(pe)
                    b = dve_banks.claim(pe)
                    for j in range(HC):
                        ins = mm(b[:, :], ones, acc[:, j, :] if _ == 0 else aT[:, j, :], j == 0, j == HC - 1)
                    full(dve_banks, ins)

            def dve_part():
                V(dve.memset(cpad, 0.0))
                for j in range(HC):
                    b = dve_banks.take(dve)
                    V(dve.tensor_copy(aT[:, j, :], b[:, :]), dve_banks.freed)
                for j in range(HC):
                    b = dve_banks.take(dve)
                    V(dve.tensor_scalar(e[:, j, :], b[:, :], LOW, None, ALU.max), dve_banks.freed)
                ask_act()
                V(dve.tensor_scalar(e, e, 1.0, None, ALU.add))
                V(dve.reciprocal(e, e))
                for s in range(2):
                    c = slice(SEQ * s, SEQ * s + SEQ)
                    V(dve.tensor_tensor(cpad[:, :, s, pad:pad + SEQ], aT[:, :, c], e[:, :, c], ALU.mult))
                for k in range(TAPS):
                    for j in range(HC):
                        src = cpad[:, j, :, k:k + SEQ]
                        o = acc[:, j, :].rearrange("p (s t) -> p s t", s=2)
                        if k == 0:
                            ins = dve.tensor_scalar(o, src, cw[:, j, 0:1], col("conv_b")[:, j:j + 1], ALU.mult, ALU.add)
                        else:
                            ins = stt(o, src, cw[:, j, k:k + 1], o)
                        V(ins)
                tell(V, dve_to_pe)
                b = dve_banks.take(dve)
                V(stt(acc, mid(b[:, :], HC), -1.0 / HALF, acc), dve_banks.freed)
                V(dve.tensor_tensor(aT, acc, acc, ALU.mult))
                tell(V, dve_to_pe)
                b = dve_banks.take(dve)
                V(dve.tensor_scalar(e[:, 0, :], b[:, :], 1.0 / HALF, EPS, ALU.mult, ALU.add), dve_banks.freed)
                ask_act()
                V(dve.tensor_tensor(acc, acc, mid(e[:, 0, :], HC), ALU.mult))
                for j in range(HC):
                    V(dve.tensor_scalar(acc[:, j, :], acc[:, j, :], col("conv_g")[:, j:j + 1],
                                        col("conv_lb")[:, j:j + 1], ALU.mult, ALU.add))
                V(dve.tensor_scalar(acc, acc, LOW, None, ALU.max))
                ask_act()
                silu_parts(bT, acc, e)

            def act_part():
                exp_of(e, e, -1.0)
                dve_to_act.wait(act)
                A(act.activation(e[:, 0, :], e[:, 0, :], ACT.Ln))
                A(act.activation(e[:, 0, :], e[:, 0, :], ACT.Exp, scale=-0.5))
                tell(A, act_to_dve)
                exp_of(e, acc, -1.0)
            return dict(sp=sp_part, pe=pe_part, dve=dve_part, act=act_part), bT

        def attention_stage(i, w, w_out, other_T, tiles_q, names, windowed):
            work = Space(WORK + 2048, WORK1 - 2048)
            qkv = work.take(4, 12, HD)
            qT, kT = work.take(4, 512), work.take(2, 512)
            o = work.take(4, 512) if not windowed else work.take(2, 512)
            s_sb = work.take(2, 512) if windowed else None
            p_sb, pT = work.take(2, 512), work.take(2, 512)
            band = view(HT, 4096)
            oT = qkv.rearrange("p a b c -> p (a b c)")[:, 0:2048].rearrange("p (c t) -> p c t", c=HC)
            tmp = view(WORK + WORK1 - 2048, 2048)
            ps = [add_panel(krows(w, 0, 512), KC, 512), add_panel(krows(w, 512, 768), KC, 256)]
            tables = None
            x0 = tiles_q[0]
            outs = [add_panel(krows(w_out, 512 * k, 512 * k + 512), KC, 512) for k in range(2)]
            gq, gk = row(names[0]), row(names[1])
            cos, sin = const("cos", 4, 32), const("sin", 4, 32)
            units = [[(4 * g + h, t, 4 if t >= 2 else 2) for h in range(4) for t in tiles_q] for g in range(2)]
            mask = view(HT, NX, 512)
            atts = [attention(units[g], HD,
                              lambda h, t: qT[0:HD, h % 4, P * t:P * t + P],
                              lambda h, nk: kT[0:HD, h // 4, 0:P * nk],
                              lambda h, j: qkv[:, j, 10 + h // 4, :],
                              lambda h, t: o[:, t - x0, HD * h:HD * h + HD],
                              HD ** -0.5,
                              (lambda t, nk: mask[:, t - 2, :]) if windowed else None,
                              (lambda h: row("sink")[:, h:h + 1]) if windowed else None,
                              dict(s=s_sb, p=p_sb, pT=pT)) for g in range(2)]

            def sp_part():
                for n in ps:
                    load_panel(n)
                if windowed:
                    dve_to_sp.wait(sp)
                    o_, w_ = TABLES["band"]
                    load_table("band", (mask.rearrange("p a b -> p (a b)"), d["tables"][:, o_:o_ + w_]))
                for n in outs:
                    load_panel(n)

            def pe_part():
                rows_of_panel(ps[0], tiles_q, 512, ht)
                rows_of_panel(ps[1], range(4), 256, ht)
                dve_to_pe.wait(pe)
                transposed_pe(lambda h, t: qkv[:, t, 8 + h, :], range(4), range(2))
                for g in range(2):
                    transposed_pe(lambda h, t: qkv[:, t, 4 * g + h, :], tiles_q, range(4))
                    dve_banks.settled(pe)
                    atts[g]["pe"]()
                for t in tiles_q:
                    b = dve_banks.claim(pe)
                    for c in range(HC):
                        ins = pe.transpose(b[:, P * c:P * c + P], o[:, t - x0, P * c:P * c + P], ident)
                    full(dve_banks, ins)
                dve_banks.settled(pe)
                if not windowed:
                    act_to_pe
                for n in outs:
                    rows_of_panel(n, tiles_q, 512,
                                  lambda c, t: oT[:, c, P * t:P * t + P] if c < HC else other_T(c - HC, t))

            def dve_part():
                for t in tiles_q:
                    b = dve_banks.take(dve)
                    V(dve.tensor_copy(qkv[:, t, 0:8, :].rearrange("p h e -> p (h e)"), b[:, :]), dve_banks.freed)
                for t in range(4):
                    b = dve_banks.take(dve)
                    V(dve.tensor_copy(qkv[:, t, 8:12, :].rearrange("p h e -> p (h e)"), b[:, 0:256]), dve_banks.freed)
                if windowed:
                    tell(V, dve_to_sp)
                for t in range(4):
                    heads = range(0 if t in tiles_q else 8, 10)
                    gains = ([(0, 8, gq)] if t in tiles_q else []) + [(8, 10, gk)]
                    head_norm_rope(qkv[:, t], heads, gains, cos[:, t], sin[:, t], HD, tmp, rope=t >= 2)
                tell(V, dve_to_pe)
                if windowed:
                    table_in(dve, "band")
                transposed_dve(lambda h: kT[0:HD, h, :], range(4), range(2))
                for g in range(2):
                    q0 = P * tiles_q[0]
                    transposed_dve(lambda h: qT[0:HD, h, q0:512], tiles_q, range(4))
                    atts[g]["dve"]()
                for t in tiles_q:
                    b = dve_banks.take(dve)
                    V(dve.tensor_copy(oT[:, :, P * t:P * t + P], b[:, :].rearrange("p (c t) -> p c t", c=HC)),
                      dve_banks.freed)
                residual_dve(tiles_q, lambda t: gates[:, t // 2, :])

            def act_part():
                for t in range(4):
                    norm_act(10 if t in tiles_q else 2)
                for g in range(2):
                    atts[g]["act"]()
            return dict(sp=sp_part, pe=pe_part, dve=dve_part, act=act_part)

        def pool_stage():
            work = Space(WORK, WORK1)
            yT = work.take(HC, 256)
            pw = work.take(HC, P)
            u = view(WORK + 2048, NX, 512)
            table = view(WORK + 3072, NX, 4, SEQ)
            pT = view(WORK + 5120, HC, 256)
            pn = add_panel(krows(d["w_in_cd"][0], 768, 1280), KC, 512)

            def sp_part():
                dve_to_sp.wait(sp)
                o_, w_ = TABLES["pool"]
                load_table("pool", (table.rearrange("p a b c -> p (a b c)"), d["tables"][:, o_:o_ + w_]),
                           (pw, d["pool_w"][0].rearrange("g c e -> c g e")))
                load_panel(pn)

            def pe_part():
                rows_of_panel(pn, (2, 3), 512, ht)
                table_in(pe, "pool")
                dve_banks.settled(pe)
                for g in range(4):
                    b = dve_banks.claim(pe)
                    for k in range(NX):
                        ins = mm(b[:, 0:SEQ], u[:, k, P * g:P * g + P], table[:, k, g, :], k == 0, k == NX - 1)
                    full(dve_banks, ins)
                dve_banks.settled(pe)
                for g in range(4):
                    b = dve_banks.claim(pe)
                    full(dve_banks, mm(b[:, 0:SEQ], pw[:, g, :], pT[:, g, :], True, True))
                dve_banks.settled(pe)

            def dve_part():
                tell(V, dve_to_sp)
                for t in range(NX):
                    b = dve_banks.take(dve)
                    V(dve.tensor_copy(u[:, t, :], b[:, :]), dve_banks.freed)
                for g in range(4):
                    b = dve_banks.take(dve)
                    V(dve.tensor_copy(pT[:, g, :], b[:, 0:SEQ]), dve_banks.freed)
                for g in range(4):
                    b = dve_banks.take(dve)
                    V(dve.tensor_scalar(yT[:, g, :], b[:, 0:SEQ], col("pool_scale")[:, g:g + 1], None, ALU.mult),
                      dve_banks.freed)
            return dict(sp=sp_part, pe=pe_part, dve=dve_part), yT

        def moe_stage(i, tiles):
            nt, t0 = len(tiles), tiles[0]
            extra_max = 2 * nt
            blocks_max = NEXP + extra_max
            NR = NGRP + NEXP
            work = Space(WORK, WORK1)
            rt_w = work.take(KC, NR)
            logit = work.take(nt, NR)
            gpad, gtop = work.take(nt, 8), work.take(nt, 8)
            etop = work.take(nt, 8)
            picks = work.take(nt, 2)
            gidx = work.take(nt)
            one_hot = work.take(2, nt, NEXP)
            both = work.take(nt, NEXP)
            place = work.take(nt, NEXP + 0)
            prod = work.take(2, nt, NEXP)
            pos, slot, over = work.take(2, nt), work.take(2, nt), work.take(2, nt)
            gsum, ratio, wt = work.take(nt), work.take(nt), work.take(2, nt)
            counts, extra, ends, starts = (work.take(NEXP) for _ in range(4))
            past = work.take(extra_max, NEXP)
            experts_f, nb_f, tmp1 = work.take(NEXP + 8), work.take(1), work.take(1)
            over_base = work.take(2, nt)
            xg, xgT = work.take(2, D), work.take(2, KC, P)
            hid, hidT = work.take(2, DE), work.take(2, DE // P, P)
            ex, y = work.take(2, DE), work.take(2, D)
            h_row = view(work.off - 9216, nt, D)
            yg = view(work.off - 9216, 4, D)
            comb = view(work.off - 9216 + 4096, D)
            NB = 16
            experts_i = expert_ids[:, 0:blocks_max]
            slot_i, token_i = bigi[:, 0:2 * nt], bigi[:, 8:12]
            list_i = [bigi[:, 12 + s:13 + s] for s in range(2)]
            index_u = ibuf
            lists = nc.dram_tensor(f"lists{i}", [blocks_max * P, 1], I32, kind="Internal").ap()
            h_dram = nc.dram_tensor(f"h_rows{i}", [nt * P, D], F32, kind="Internal").ap()
            results = nc.dram_tensor(f"results{i}", [blocks_max * P, D], F32, kind="Internal").ap()
            owners = dict(slot_owner)
            ring["next"], ring["moe"] = 0, i + 1
            slot_owner.clear()

            def sem(name):
                return ctx.enter_context(nc.semaphore(f"moe{i}_{name}"))
            w_full = [sem(f"weights_full{k}") for k in range(6)]
            list_full, xg_full = [sem("list0"), sem("list1")], [sem("rows0"), sem("rows1")]
            y_out = [sem("y_out0"), sem("y_out1")]
            lists_ready, h_written, y_back = sem("lists_ready"), sem("h_written"), sem("y_back")
            xT_ps, xT_sb = sem("xT_in_psum"), sem("xT_in_sbuf")
            g_ps, g_free, u_ps = sem("gate_in_psum"), sem("gate_used"), sem("up_in_psum")
            e_sb, hid_sb = sem("exp_ready"), sem("hid_ready")
            h_ps, hT_sb, d_ps, y_sb = sem("hidT_in_psum"), sem("hidT_in_sbuf"), sem("down_in_psum"), sem("y_in_sbuf")
            chain, zeroed = sem("silu_steps"), sem("results_zeroed")
            wg = d["ex_gate"][i].rearrange("e (c p) n -> e p c n", p=P)
            wu = d["ex_up"][i].rearrange("e (c p) n -> e p c n", p=P)
            wd = d["ex_down"][i].rearrange("e (c p) n -> e p c n", p=P)
            wbuf = [[view(RING + (3 * s + k) * PANEL, *((KC, DE) if k < 2 else (DE // P, D))) for k in range(3)]
                    for s in range(2)]

            def n_blocks(eng):
                more = eng.value_load(bigi[0:1, NB:NB + 1], min_val=0, max_val=extra_max)
                return eng.snap(more + NEXP, min_val=NEXP, max_val=blocks_max)

            def sp_part():
                dve_to_sp.wait(sp)
                load_table(f"router{i}", (rt_w, krows(d["rt_w"][i])))
                for b in range(2):
                    for k, w in enumerate((wg, wu, wd)):
                        if 3 * b + k in owners:
                            sp.wait_ge(panel_used.sem, owners[3 * b + k] + 1)
                        if i:
                            sp.wait_ge(pe_done.sem, i)
                        sp.dma_start(wbuf[b][k], w[b]).then_inc(w_full[3 * b + k], 16)
                dve_to_sp.wait(sp)
                sp.dma_start(h_dram.rearrange("(t p) n -> p t n", p=P), h_row).then_inc(h_written, 16)
                dve_to_sp.wait(sp)
                nb = n_blocks(sp)
                with sp.Fori(2, nb, 2) as b:
                    for s in range(2):
                        e = sp.value_load(expert_ids[0:1, bass.ds((b + s).with_bounds(min_val=0, max_val=blocks_max - 1), 1)],
                                          min_val=0, max_val=NEXP - 1)
                        for k, (w, free) in enumerate(((wg, g_ps), (wu, u_ps), (wd, d_ps))):
                            sp.wait_ge(free, b + s - 1)
                            sp.dma_start(wbuf[s][k], w[bass.ds(e, 1)].rearrange("e p c n -> (e p) c n"))\
                                .then_inc(w_full[3 * s + k], 16)

            def pool_part():
                if i == 0:
                    G(pool.memset(zeros_i, 0))
                pool.dma_start(lists.rearrange("(p a) o -> p (a o)", p=P), zeros_i[:, 0:blocks_max]).then_inc(lists_ready, 16)
                pool.wait_ge(lists_ready, 16)
                dve_to_pool.wait(pool)
                for k in range(nt):
                    for j in range(2):
                        c = j * nt + k
                        pool.indirect_dma_start(out=lists, out_offset=bass.IndirectOffsetOnAxis(ap=slot_i[:, c:c + 1], axis=0),
                                                in_=token_i[:, k:k + 1], in_offset=None).then_inc(lists_ready, 16)
                        pool.wait_ge(lists_ready, 16 * (2 + 2 * k + j))
                pool.wait_ge(h_written, 16)
                nb = n_blocks(pool)
                lists_b = lists.rearrange("(b p) o -> b p o", p=P)

                def fetch(b, s, free):
                    if free is not None:
                        pool.wait_ge(xT_ps, free)
                        pool.sem_inc(pool_passed, 1)
                    pool.dma_start(list_i[s], lists_b[bass.ds(b, 1)].rearrange("b p o -> (b p) o"))\
                        .then_inc(list_full[s], 16)
                    pool.wait_ge(list_full[s], (b - s) * 8 + 16)
                    if free is not None:
                        pool.sem_inc(pool_passed, 1)
                    pool.indirect_dma_start(out=xg[:, s, :], out_offset=None, in_=h_dram,
                                            in_offset=bass.IndirectOffsetOnAxis(ap=list_i[s], axis=0))\
                        .then_inc(xg_full[s], 16)
                for s in range(2):
                    fetch(s, s, None)
                with pool.Fori(2, nb, 2) as b:
                    for s in range(2):
                        fetch((b + s).with_bounds(min_val=2, max_val=blocks_max - 1), s, b + s - 1)
                act_to_pool.wait(pool)
                for k in range(nt):
                    if k >= 2:
                        dve_to_pool.wait(pool)
                    for j in range(2):
                        c = j * nt + k
                        pool.indirect_dma_start(out=yg[:, 2 * (k % 2) + j, :], out_offset=None, in_=results,
                                                in_offset=bass.IndirectOffsetOnAxis(ap=slot_i[:, c:c + 1], axis=0))\
                            .then_inc(y_back, 16)
                        pool.wait_ge(y_back, 16 * (2 * k + j + 1))
                    tell(G, pool_to_dve)

            def pe_part():
                dve_banks.settled(pe)
                table_in(pe, f"router{i}")
                for k in range(nt):
                    b = dve_banks.claim(pe)
                    for c in range(KC):
                        ins = mm(b[:, 0:NR], hT[:, c, P * k:P * k + P], rt_w[:, c, :], c == 0, c == KC - 1)
                    full(dve_banks, ins)
                for k in range(nt):
                    for h in range(2):
                        b = dve_banks.claim(pe)
                        for j in range(4):
                            ins = pe.transpose(b[:, P * j:P * j + P], hT[:, 4 * h + j, P * k:P * k + P], ident)
                        full(dve_banks, ins)
                dve_to_pe.wait(pe)
                b = dve_banks.claim(pe)
                for k in range(nt):
                    for m in range(k + 1):
                        mm(b[:, NEXP * k:NEXP * k + NEXP], const("before") if m == k else ones, both[:, m, :],
                           m == 0, m == k)
                for k in range(nt):
                    ins = mm(b[:, NEXP * nt:NEXP * nt + NEXP], ones, both[:, k, :], k == 0, k == nt - 1)
                full(dve_banks, ins)
                dve_to_pe.wait(pe)
                nb = n_blocks(pe)

                def xT(b, s):
                    pe.wait_ge(xg_full[s], (b - s) * 8 + 16)
                    if not (isinstance(b, int) and b == 0):
                        pe.wait_ge(xT_sb, b * 2)
                    for c in range(KC):
                        ins = pe.transpose(psum[2 + c // 4][:, P * (c % 4):P * (c % 4) + P],
                                           xg[:, s, P * c:P * c + P], ident)
                    ins.then_inc(xT_ps, 1)

                def gate_up(b, s, k):
                    if k == 0:
                        pe.wait_ge(xT_sb, b * 2 + 2)
                    pe.wait_ge(w_full[3 * s + k], (b - s) * 8 + 16)
                    if not (isinstance(b, int) and b == 0):
                        pe.wait_ge((g_free, hid_sb)[k], b)
                    for c in range(KC):
                        ins = mm(psum[k][:, :], xgT[:, s, c, :], wbuf[s][k][:, c, :], c == 0, c == KC - 1)
                    ins.then_inc((g_ps, u_ps)[k], 1)

                def hidT_of(b, s):
                    pe.wait_ge(hid_sb, b + 1)
                    if not (isinstance(b, int) and b == 0):
                        pe.wait_ge(hT_sb, b)
                    for c in range(DE // P):
                        ins = pe.transpose(psum[4][:, P * c:P * c + P], hid[:, s, P * c:P * c + P], ident)
                    ins.then_inc(h_ps, 1)

                def down(b, s):
                    pe.wait_ge(hT_sb, b + 1)
                    pe.wait_ge(w_full[3 * s + 2], (b - s) * 8 + 16)
                    if not (isinstance(b, int) and b == 0):
                        pe.wait_ge(y_sb, b * 2)
                    for h in range(2):
                        for c in range(DE // P):
                            ins = mm(psum[5 + h][:, :], hidT[:, s, c, :], wbuf[s][2][:, c, 512 * h:512 * h + 512],
                                     c == 0, c == DE // P - 1)
                    ins.then_inc(d_ps, 1)

                def whole(b, s, ahead):
                    gate_up(b, s, 0)
                    hidT_of(b - 1, 1 - s)
                    gate_up(b, s, 1)
                    if ahead:
                        xT(b + 1, 1 - s)
                    down(b - 1, 1 - s)

                xT(0, 0)
                gate_up(0, 0, 0)
                gate_up(0, 0, 1)
                xT(1, 1)
                with pe.Fori(1, nb - 1, 2) as b:
                    whole(b, 1, True)
                    whole(b + 1, 0, True)
                whole(nb - 1, 1, False)
                hidT_of(nb - 1, 1)
                down(nb - 1, 1)
                mm(psum[7][0:2, 0:2], ident[0:2, 0:2], ident[0:2, 0:2], True, True).then_inc(pe_done.sem, 1)
                dve_to_pe.wait(pe)

            def dve_part():
                V(dve.memset(y[:, 0, :], 0.0))
                tell(V, dve_to_act)
                tell(V, dve_to_sp)
                for k in range(nt):
                    b = dve_banks.take(dve)
                    V(dve.tensor_tensor(logit[:, k, :], b[:, 0:NR], row(f"rtb_{i}"), ALU.add), dve_banks.freed)
                V(dve.memset(gpad, -BIG))
                V(dve.tensor_copy(gpad[:, :, 0:NGRP], logit[:, :, 0:NGRP]))
                for k in range(nt):
                    V(dve.max(gtop[:, k, :], gpad[:, k, :]))
                    V(dve.max_index(index_u[:, 0:8], gtop[:, k, :], gpad[:, k, :]))
                    V(dve.tensor_copy(gidx[:, k:k + 1], index_u[:, 0:1]))
                V(dve.tensor_tensor(gpad, gpad, last(gtop[:, :, 0], 8), ALU.subtract))
                ask_act()
                V(dve.tensor_reduce(gsum, gpad, AX.X, ALU.add))
                V(dve.reciprocal(gsum, gsum))
                V(dve.tensor_tensor(both, mid(const("group"), nt), last(gidx, NEXP), ALU.is_equal))
                V(dve.tensor_scalar(both, both, 1.0, BIG, ALU.subtract, ALU.mult))
                V(dve.tensor_tensor(both, both, logit[:, :, NGRP:NR], ALU.add))
                for k in range(nt):
                    V(dve.max(etop[:, k, :], both[:, k, :]))
                    V(dve.max_index(index_u[:, 0:8], etop[:, k, :], both[:, k, :]))
                    V(dve.tensor_copy(picks[:, k, :], index_u[:, 0:2]))
                for j in range(2):
                    V(dve.tensor_tensor(one_hot[:, j], mid(const("expert"), nt), last(picks[:, :, j], NEXP), ALU.is_equal))
                V(dve.tensor_tensor(both, one_hot[:, 0], one_hot[:, 1], ALU.add))
                V(dve.tensor_tensor(ratio, etop[:, :, 1], etop[:, :, 0], ALU.subtract))
                ask_act()
                V(dve.tensor_scalar(wt[:, 0], ratio, 1.0, None, ALU.add))
                V(dve.reciprocal(wt[:, 0], wt[:, 0]))
                V(dve.tensor_tensor(wt[:, 0], wt[:, 0], gsum, ALU.mult))
                V(dve.tensor_tensor(wt[:, 1], wt[:, 0], ratio, ALU.mult))
                for k in range(nt):
                    for h in range(2):
                        b = dve_banks.take(dve)
                        V(dve.tensor_copy(h_row[:, k, 512 * h:512 * h + 512], b[:, :]), dve_banks.freed)
                tell(V, dve_to_sp)
                tell(V, dve_to_pe)
                b = dve_banks.take(dve)
                for j in range(2):
                    V(dve.tensor_tensor(prod[:, j], one_hot[:, j],
                                        b[:, 0:NEXP * nt].rearrange("p (k e) -> p k e", e=NEXP), ALU.mult))
                V(dve.tensor_copy(counts, b[:, NEXP * nt:NEXP * nt + NEXP]), dve_banks.freed)
                V(dve.tensor_scalar(extra, counts, float(P), None, ALU.is_gt))
                for m in range(2, nt):
                    V(stt(extra, counts, float(P * m), extra, ALU.is_gt, ALU.add))
                V(dve.tensor_tensor_scan(ends, ones[:, 0:NEXP], extra, 0.0, ALU.mult, ALU.add))
                V(dve.tensor_tensor(starts, ends, extra, ALU.subtract))
                for j in range(2):
                    V(dve.tensor_reduce(pos[:, j], prod[:, j], AX.X, ALU.add))
                for j in range(2):
                    V(dve.tensor_tensor(prod[:, j], one_hot[:, j], mid(starts, nt), ALU.mult))
                    V(dve.tensor_reduce(over_base[:, j], prod[:, j], AX.X, ALU.add))
                    V(dve.tensor_tensor(over_base[:, j], over_base[:, j], picks[:, :, j], ALU.subtract))
                    V(stt(slot[:, j], picks[:, :, j], float(P), pos[:, j]))
                V(dve.tensor_scalar(over_base, over_base, float(P), float((NEXP - 1) * P), ALU.mult, ALU.add))
                V(dve.tensor_scalar(over, pos, float(P), None, ALU.is_ge))
                V(dve.tensor_tensor(over, over, over_base, ALU.mult))
                V(dve.tensor_tensor(slot, slot, over, ALU.add))
                V(dve.tensor_copy(slot_i, slot.rearrange("p a b -> p (a b)")))
                V(dve.tensor_copy(token_i, const("token")))
                V(dve.tensor_tensor(past, mid(ends, extra_max), last(const("expert")[:, 0:extra_max], NEXP), ALU.is_le))
                V(dve.tensor_copy(experts_f[:, 0:NEXP], const("expert")))
                V(dve.tensor_reduce(experts_f[:, NEXP:NEXP + extra_max], past, AX.X, ALU.add))
                V(dve.tensor_scalar(experts_f[:, NEXP:blocks_max], experts_f[:, NEXP:blocks_max], float(NEXP - 1), None, ALU.min))
                V(dve.tensor_copy(experts_i, experts_f[:, 0:blocks_max]))
                V(dve.memset(nb_f, 0.0))
                for m in range(nt):
                    V(dve.tensor_scalar(tmp1, ends[:, NEXP - 1:NEXP], float(2 * m), 2.0, ALU.is_gt, ALU.mult))
                    V(dve.tensor_tensor(nb_f, nb_f, tmp1, ALU.add))
                V(dve.tensor_copy(bigi[:, NB:NB + 1], nb_f))
                tell(V, dve_to_pool)
                tell(V, dve_to_sp)
                tell(V, dve_to_pe)
                tell(V, dve_to_act)
                nb = n_blocks(dve)

                def rows_in(b, s, reuse=True):
                    dve.wait_ge(xT_ps, b + 1)
                    if reuse:
                        dve.wait_ge(u_ps, b - 1)
                    for h in range(2):
                        dve.tensor_copy(xgT[:, s, 4 * h:4 * h + 4, :].rearrange("p c t -> p (c t)"), psum[2 + h][:, :])\
                            .then_inc(xT_sb, 1)

                def hidden(b, s, reuse=True):
                    dve.wait_ge(e_sb, b + 1)
                    dve.tensor_scalar(ex[:, s, :], ex[:, s, :], 1.0, None, ALU.add).then_inc(chain, 1)
                    dve.wait_ge(chain, b * 3 + 1)
                    dve.reciprocal(ex[:, s, :], ex[:, s, :]).then_inc(chain, 1)
                    dve.wait_ge(chain, b * 3 + 2)
                    dve.tensor_tensor(ex[:, s, :], ex[:, s, :], psum[0][:, :], ALU.mult).then_inc(g_free, 1)
                    dve.wait_ge(g_free, b + 1)
                    dve.wait_ge(u_ps, b + 1)
                    if reuse:
                        dve.wait_ge(h_ps, b - 1)
                    dve.tensor_tensor(hid[:, s, :], ex[:, s, :], psum[1][:, :], ALU.mult).then_inc(hid_sb, 1)
                    dve.wait_ge(hid_sb, b + 1)
                    dve.sem_inc(chain, 1)

                def hidT_in(b, s, reuse=True):
                    dve.wait_ge(h_ps, b + 1)
                    if reuse:
                        dve.wait_ge(d_ps, b - 1)
                    dve.tensor_copy(hidT[:, s].rearrange("p c t -> p (c t)"), psum[4][:, :]).then_inc(hT_sb, 1)

                dve.wait_ge(h_written, 16)
                rows_in(0, 0, False)
                hidden(0, 0, False)
                rows_in(1, 1, False)
                hidT_in(0, 0, False)
                hidden(1, 1, False)
                rows_in(2, 0)
                hidT_in(1, 1, False)
                hidden(2, 0)
                rows_in(3, 1)
                with dve.Fori(3, nb - 1, 2) as b:
                    hidT_in(b - 1, 0)
                    hidden(b, 1)
                    rows_in(b + 1, 0)
                    hidT_in(b, 1)
                    hidden(b + 1, 0)
                    rows_in(b + 2, 1)
                hidT_in(nb - 2, 0)
                hidden(nb - 1, 1)
                hidT_in(nb - 1, 1)
                for k in range(nt):
                    pool_to_dve.wait(dve)
                    t = tiles[k]
                    V(dve.tensor_scalar(comb, yg[:, 2 * (k % 2), :], wt[:, 0, k:k + 1], None, ALU.mult))
                    V(stt(comb, yg[:, 2 * (k % 2) + 1, :], wt[:, 1, k:k + 1], comb))
                    if k + 2 < nt:
                        tell(V, dve_to_pool)
                    V(dve.tensor_tensor(comb, comb, gates[:, 2 + t // 2, :], ALU.mult))
                    V(dve.tensor_tensor(x[:, t, :], x[:, t, :], comb, ALU.add))
                tell(V, dve_to_pe)

            def act_part():
                dve_to_act.wait(act)
                for m in range(extra_max):
                    act.dma_start(results[(NEXP + m) * P:(NEXP + m + 1) * P, :], y[:, 0, :]).then_inc(zeroed, 16)
                exp_of(gpad, gpad)
                exp_of(ratio, ratio)
                dve_to_act.wait(act)
                act.wait_ge(zeroed, 16 * extra_max)
                nb = n_blocks(act)

                def exps(b, s, reuse=True):
                    act.wait_ge(g_ps, b + 1)
                    if reuse:
                        act.wait_ge(hid_sb, b - 1)
                    act.activation(ex[:, s, :], psum[0][:, :], ACT.Exp, scale=-1.0).then_inc(e_sb, 1)

                def results_out(b, s, reuse=True):
                    act.wait_ge(d_ps, b + 1)
                    if reuse:
                        act.wait_ge(y_out[s], (b - s) * 8)
                    for h in range(2):
                        act.activation(y[:, s, 512 * h:512 * h + 512], psum[5 + h][:, :], ACT.Copy).then_inc(y_sb, 1)
                    act.wait_ge(y_sb, b * 2 + 2)
                    act.dma_start(results.rearrange("(b p) n -> b p n", p=P)[bass.ds(b, 1)].rearrange("b p n -> (b p) n"),
                                  y[:, s, :]).then_inc(y_out[s], 16)

                def bound(b):
                    return b.with_bounds(min_val=0, max_val=blocks_max - 1)
                exps(0, 0, False)
                exps(1, 1, False)
                results_out(0, 0, False)
                exps(2, 0)
                results_out(1, 1, False)
                with act.Fori(3, nb - 1, 2) as b:
                    exps(b, 1)
                    results_out(bound(b - 1), 0)
                    exps(b + 1, 0)
                    results_out(bound(b + 0), 1)
                exps(nb - 1, 1)
                results_out(bound(nb - 2), 0)
                results_out(bound(nb - 1), 1)
                for s in range(2):
                    act.wait_ge(y_out[s], nb * 8)
                A(act.activation(small[:, 120:121], ident[:, 0:1], ACT.Copy))
                tell(A, act_to_pool)

            return dict(sp=sp_part, pe=pe_part, dve=dve_part, act=act_part, pool=pool_part)

        T2 = (2, 3)
        WORK2 = (3 * PANEL, WORK + WORK1 - 3 * PANEL)

        def rms_rows(v, scale, eps=EPS):
            V(dve.tensor_scalar(v, v, scale, eps, ALU.mult, ALU.add))
            ask_act()

        def rsqrt_act(v):
            dve_to_act.wait(act)
            A(act.activation(v, v, ACT.Ln))
            A(act.activation(v, v, ACT.Exp, scale=-0.5))
            tell(A, act_to_dve)

        def column_sums_pe(weights, src):
            dve_to_pe.wait(pe)
            for k in range(2):
                b = dve_banks.claim(pe)
                full(dve_banks, mm(b[:, :], weights, src[:, 2 * k:2 * k + 2, :].rearrange("p a t -> p (a t)"), True, True))

        def column_sums_dve(use):
            tell(V, dve_to_pe)
            for k in range(2):
                b = dve_banks.take(dve)
                V(use(slice(2 * k, 2 * k + 2), b[:, :].rearrange("p (a t) -> p a t", t=SEQ)), dve_banks.freed)

        def chunks(ap):
            return ap.rearrange("p j (c t) -> p (j c) t", t=CH)

        def hgrn_stage(oT):
            work = Space(WORK2[0] + 2048, WORK2[1] - 2048)
            w = d["w_in_ar_2"][0]
            raw = work.take(3, HC, SEQ)
            e3 = work.take(3, HC, SEQ)
            e4 = work.take(4, HC, SEQ)
            b = work.take(HC, SEQ)
            v_tok = work.take(NX, 512)
            last_b = work.take(HC * SEQ // CH)
            lb3, lb1, keep = work.take(3, HC), work.take(HC), work.take(HC)
            sc, k_tok = work.take(2, P), work.take(2, P)
            v_exp = work.take(2, NCH, P)
            S = work.take(NCH + 1, P)
            ps = [add_panel(krows(w, 512 * n, 512 * n + 512), KC, 512) for n in (0, 1, 3, 2)]
            q, f, gate = raw[:, 0], raw[:, 1], raw[:, 2]
            lf = e3[:, 1]
            q_t, k_t, q_e, k_bar = (e4[:, n] for n in range(4))
            units = [(h, B) for h in range(HC) for B in range(NX)]

            def sp_part():
                for n in ps:
                    load_panel(n)

            def pe_part():
                for n in ps[:3]:
                    cols_of_panel(n, HC, SEQ)
                rows_of_panel(ps[3], range(NX), 512, ht)
                dve_to_pe.wait(pe)
                for n, (h, B) in enumerate(units):
                    tok = slice(P * B, P * B + P)
                    vt = v_tok[:, B, P * h:P * h + P]
                    bank = dve_banks.claim(pe)
                    mm(bank[:, 0:P], k_t[:, h, tok], q_t[:, h, tok], True, True)
                    full(dve_banks, pe.transpose(bank[:, P:2 * P], k_bar[:, h, tok], ident))
                    dve_to_pe.wait(pe)
                    for k in range(2):
                        bank = dve_banks.claim(pe)
                        full(dve_banks, mm(bank[:, :], k_tok[:, n % 2, :],
                                           v_exp[:, n % 2, 4 * k:4 * k + 4, :].rearrange("p c e -> p (c e)"), True, True))
                    dve_banks.settled(pe)
                    bank = dve_banks.claim(pe)
                    ins = mm(bank[:, 0:P], vt, sc[:, n % 2, :], True, False)
                    for c in range(NCH):
                        if B or c:
                            ins = mm(bank[:, CH * c:CH * c + CH], S[:, c, :],
                                     q_e[:, h, P * B + CH * c:P * B + CH * c + CH], False, c == NCH - 1)
                    full(dve_banks, ins)
                column_sums_pe(ones, e4[:, 0])

            def dve_part():
                for n in range(3):
                    for j in range(HC):
                        bk = dve_banks.take(dve)
                        V(dve.tensor_scalar(raw[:, n, j, :], bk[:, 0:SEQ], LOW, None, ALU.max), dve_banks.freed)
                ask_act()
                for t in range(NX):
                    bk = dve_banks.take(dve)
                    V(dve.tensor_copy(v_tok[:, t, :], bk[:, :]), dve_banks.freed)
                lb = col("lb", 3, HC)
                V(dve.tensor_tensor(lb1, lb[:, 0], lb[:, 1], ALU.max))
                V(dve.tensor_tensor(lb1, lb1, lb[:, 2], ALU.max))
                V(dve.tensor_tensor(lb3, lb, mid(lb1, 3), ALU.subtract))
                ask_act()
                V(dve.tensor_tensor(lb1, lb3[:, 0], lb3[:, 1], ALU.add))
                V(dve.tensor_tensor(lb1, lb1, lb3[:, 2], ALU.add))
                V(dve.reciprocal(lb1, lb1))
                V(dve.tensor_tensor(lb1, lb1, lb3[:, 0], ALU.mult))
                V(dve.tensor_scalar(keep, lb1, -1.0, 1.0, ALU.mult, ALU.add))
                V(dve.tensor_scalar(e3, e3, 1.0, None, ALU.add))
                V(dve.reciprocal(e3, e3))
                V(dve.tensor_tensor(q, q, e3[:, 0], ALU.mult))
                V(dve.tensor_tensor(gate, gate, e3[:, 2], ALU.mult))
                for j in range(HC):
                    V(dve.tensor_scalar(f[:, j, :], e3[:, 1, j, :], keep[:, j:j + 1], lb1[:, j:j + 1], ALU.mult, ALU.add))
                ask_act()
                V(dve.tensor_scalar(f, f, -1.0, 1.0, ALU.mult, ALU.add))
                for j in range(HC):
                    V(dve.tensor_tensor_scan(b[:, j, :], const("restart"), lf[:, j, :], 0.0, ALU.mult, ALU.add))
                bc = chunks(b)
                middle = bc[:, :, CH // 2 - 1:CH // 2].broadcast_to([P, HC * SEQ // CH, CH])
                end = bc[:, :, CH - 1:CH].broadcast_to([P, HC * SEQ // CH, CH])
                V(dve.tensor_tensor(chunks(q_t), bc, middle, ALU.subtract))
                V(dve.tensor_scalar(q_t, q_t, 40.0, -40.0, ALU.min, ALU.max))
                V(dve.tensor_scalar(k_t, q_t, -1.0, None, ALU.mult))
                V(dve.tensor_copy(q_e, b))
                V(dve.tensor_tensor(chunks(k_bar), end, bc, ALU.subtract))
                ask_act()
                V(dve.tensor_copy(last_b, chunks(q_e)[:, :, CH - 1]))
                for dst, src in ((q_t, q), (k_t, f), (q_e, q), (k_bar, f)):
                    V(dve.tensor_tensor(dst, dst, src, ALU.mult))
                tell(V, dve_to_pe)
                for n, (h, B) in enumerate(units):
                    vt = v_tok[:, B, P * h:P * h + P]
                    V(dve.tensor_tensor(v_exp[:, n % 2], mid(vt, NCH), last(const("chunk_of"), P), ALU.mult))
                    bk = dve_banks.take(dve)
                    V(dve.tensor_tensor(sc[:, n % 2, :], bk[:, 0:P], const("chunk_upto_st"), ALU.mult))
                    V(dve.tensor_copy(k_tok[:, n % 2, :], bk[:, P:2 * P]), dve_banks.freed)
                    tell(V, dve_to_pe)
                    if B:
                        V(dve.tensor_copy(S[:, 0, :], S[:, NCH, :]))
                    for k in range(2):
                        bk = dve_banks.take(dve)
                        for c4 in range(4):
                            c = 4 * k + c4
                            u = bk[:, P * c4:P * c4 + P]
                            s = dve_banks.freed if c4 == 3 else None
                            if B or c:
                                at = h * (SEQ // CH) + B * NCH + c
                                V(stt(S[:, c + 1, :], S[:, c, :], last_b[:, at:at + 1], u), s)
                            else:
                                V(dve.tensor_copy(S[:, 1, :], u), s)
                    bk = dve_banks.take(dve)
                    V(dve.tensor_copy(oT[:, h, P * B:P * B + P], bk[:, 0:P]), dve_banks.freed)
                V(dve.tensor_tensor(e4[:, 0], oT, oT, ALU.mult))
                column_sums_dve(lambda k, bk: dve.tensor_copy(e4[:, 1, k, :], bk))
                rms_rows(e4[:, 1], 1.0 / P)
                V(dve.tensor_tensor(oT, oT, e4[:, 1], ALU.mult))
                for h in range(HC):
                    V(stt(oT[:, h, :], oT[:, h, :], col("onorm")[:, h:h + 1], gate[:, h, :], ALU.mult, ALU.mult))

            def act_part():
                exp_of(e3, raw, -1.0)
                exp_of(lb3, lb3)
                exp_of(lf, f, func=ACT.Ln)
                exp_of(e4, e4)
                rsqrt_act(e4[:, 1])
            return dict(sp=sp_part, pe=pe_part, dve=dve_part, act=act_part)

        def rwkv_stage(obT):
            work = Space(WORK2[0] + 2048, WORK2[1] - 2048)
            w = d["w_in_ar_2"][0]
            kept = [work.take(HC, SEQ) for _ in range(9)]
            r_e, kappa, beta, key, beta_end, key_end, v, bonus, g = kept
            mark = work.off
            ur = work.take(14, SEQ)
            za = work.take(2, HC, SEQ)
            kk, k2, b = work.take(HC, SEQ), work.take(HC, SEQ), work.take(HC, SEQ)
            e4 = work.take(4, HC, SEQ)
            lora, lora_g = view(X, 512), view(X + 512, 512)
            el = view(X + 1024, HC, SEQ // CH)
            work.off = mark
            Y1, Y2 = work.take(8, P), work.take(8, P)
            v_tok = work.take(8, 64)
            Z = work.take(8, P)
            GT = work.take(8, NCH, 64)
            S = work.take(NCH + 1, 8, 64)
            spread = work.take(3, NCH, 64)
            ke_tok = work.take(512)
            beta_tok = work.take(512)
            Nt = work.take(4, P)
            DI = work.take(HC, NCH, 64)
            H = view(HT, 8, NCH, 64)
            P0, Pt0 = [work.take(4, P), view(X, 4, P)], [view(X + 512, 4, P), view(X + 1536, 4, P)]
            ad_raw = view(X + 1088, SEQ)
            e_post = [view(mark, HC, SEQ), view(mark + HC * SEQ, HC, SEQ)]
            ps = [add_panel(krows(w, 2048 + 512 * n, 2560 + 512 * n), KC, 512) for n in range(3)] + \
                 [add_panel(krows(w, 3584, 3840), KC, 256)]
            R = Nt
            ra, k_raw, v_raw = ur[:, 0:4], ur[:, 4:8], ur[:, 8:12]
            zz, aa = za[:, 0], za[:, 1]

            def head(ap, h, B):
                return ap[64 * (h % 2):64 * (h % 2) + 64, h // 2, P * B:P * B + P]

            def eye(h):
                o = 64 * (h % 2)
                return ident[o:o + 64, o:o + 64]

            def sp_part():
                dve_to_sp.wait(sp)
                load_table("lora", (lora[0:64, :], d["rwkv_w2_2"][0]), (lora[64:P, :], d["rwkv_a2_2"][0]),
                           (lora_g, d["rwkv_g2_2"][0]))
                for n in ps:
                    load_panel(n)

            def pe_part():
                for k, n in enumerate(ps):
                    cols_of_panel(n, 4 if k < 3 else 2, SEQ)
                table_in(pe, "lora")
                act_to_pe.wait(pe)
                for kind in range(3):
                    for j in range(2):
                        bank = dve_banks.claim(pe)
                        for m in range(2):
                            jj = 2 * j + m
                            c = slice(P * jj, P * jj + P)
                            lhs, rhs = ((lora[0:64, c], ur[0:64, 12, :]), (lora[64:P, c], ur[64:P, 12, :]),
                                        (lora_g[:, c], ur[:, 13, :]))[kind]
                            if kind == 1:
                                rhs = ad_raw[64:P, :]
                            ins = mm(bank[:, SEQ * m:SEQ * m + SEQ], lhs, rhs, True, True)
                        full(dve_banks, ins)
                column_sums_pe(const("pair_ones"), e4[:, 0])
                column_sums_pe(const("pair_ones"), e4[:, 0])
                dve_to_pe.wait(pe)
                for B in range(NX):
                    for src in (kappa, key_end, beta_end, v):
                        bank = dve_banks.claim(pe)
                        for m in range(HC):
                            ins = pe.transpose(bank[:, P * m:P * m + P], src[:, m, P * B:P * B + P], ident)
                        full(dve_banks, ins)
                    for o in range(2):
                        heads = range(o, 8, 2)
                        for left, right in ((beta, kappa), (kappa, beta), (key, kappa), (beta, r_e), (key, r_e)):
                            bank = dve_banks.claim(pe)
                            for q, h in enumerate(heads):
                                ins = mm(bank[:, P * q:P * q + P], head(left, h, B), head(right, h, B), True, True)
                            full(dve_banks, ins)
                        dve_banks.settled(pe)
                        bank = dve_banks.claim(pe)
                        for q, h in enumerate(heads):
                            ins = mm(bank[:, 64 * q:64 * q + 64], Nt[:, q, :], v_tok[:, h, :], True, True)
                        full(dve_banks, ins)
                        for j in range(4):
                            dve_banks.settled(pe)
                            Pj, Ptj = P0[j % 2], Pt0[j % 2]
                            todo = [lambda q, h: (Ptj[:, q, :], Z[:, h, :])]
                            if j < 3:
                                todo.append(lambda q, h: (Pj[:, q, :], Ptj[:, q, :]))
                            if j < 2:
                                todo.append(lambda q, h: (Ptj[:, q, :], Pj[:, q, :]))
                            for f in todo:
                                bank = dve_banks.claim(pe)
                                for q, h in enumerate(heads):
                                    ins = mm(bank[:, P * q:P * q + P], *f(q, h), True, True)
                                full(dve_banks, ins)
                        dve_banks.settled(pe)
                        for q, h in enumerate(heads):
                            dve_to_pe.wait(pe)
                            base = 64 * o
                            flat = lambda a: a.rearrange("p c e -> p (c e)")
                            bank = dve_banks.claim(pe)
                            mm(bank[0:64, :], eye(h), flat(DI[:, h // 2])[base:base + 64, :], True, False)
                            full(dve_banks, mm(bank[0:64, :], Z[:, h, 0:64], flat(spread[:, 0]), False, True))
                            bank = dve_banks.claim(pe)
                            mm(bank[0:64, :], ke_tok[:, 64 * h:64 * h + 64], flat(spread[:, 1]), True, False)
                            full(dve_banks, mm(bank[0:64, :], beta_tok[:, 64 * h:64 * h + 64], flat(spread[:, 2]), False, True))
                    dve_banks.settled(pe)
                    dve_to_pe.wait(pe)
                    for c in range(NCH):
                        dve_banks.settled(pe)
                        bank = dve_banks.claim(pe)
                        for h in range(8):
                            ins = mm(bank[0:64, 64 * h:64 * h + 64], GT[0:64, h, c, :], S[0:64, c, h, :], True, True)
                        full(dve_banks, ins)
                    for o in range(2):
                        heads = range(o, 8, 2)
                        bank = dve_banks.claim(pe)
                        for q, h in enumerate(heads):
                            mm(bank[0:64, P * q:P * q + P], eye(h), head(r_e, h, B), True, False)
                            ins = mm(bank[0:64, P * q:P * q + P], Z[:, h, 0:64], Y1[:, h, :], False, True)
                        full(dve_banks, ins)
                        dve_banks.settled(pe)
                        bank = dve_banks.claim(pe)
                        for q, h in enumerate(heads):
                            mm(bank[0:64, P * q:P * q + P], v_tok[:, h, :], Y2[:, h, :], True, False)
                            mm(bank[0:64, P * q:P * q + P], Z[:, h, 64:P], Y1[:, h, :], False, False)
                            for c in range(NCH):
                                ins = mm(bank[0:64, P * q + CH * c:P * q + CH * c + CH], S[0:64, c, h, :],
                                         R[0:64, q, CH * c:CH * c + CH], False, c == NCH - 1)
                        full(dve_banks, ins)
                        dve_banks.settled(pe)
                column_sums_pe(const("pair_ones"), obT)
                column_sums_pe(const("pair_ones"), e_post[0])

            def dve_part():
                tell(V, dve_to_sp)
                for j in range(14):
                    bk = dve_banks.take(dve)
                    V(dve.tensor_copy(ur[:, j, :], bk[:, 0:SEQ]), dve_banks.freed)
                dd = e4.rearrange("p a b c -> p (a b c)")[:, 0:14 * SEQ].rearrange("p (j t) -> p j t", t=SEQ)
                V(dve.tensor_tensor(dd[:, :, 1:SEQ], ur[:, :, 0:SEQ - 1], ur[:, :, 1:SEQ], ALU.subtract))
                V(dve.tensor_scalar(dd[:, :, 0:1], ur[:, :, 0:1], -1.0, None, ALU.mult))
                V(dve.tensor_tensor(dd, dd, last(col("mu"), SEQ), ALU.mult))
                V(dve.tensor_tensor(ur, ur, dd, ALU.add))
                V(dve.tensor_copy(ad_raw, ur[:, 12, :]))
                tell(V, dve_to_act)
                act_to_dve.wait(dve)
                V(dve.tensor_scalar(ur[:, 13, :], ur[:, 13, :], 1.0, None, ALU.add))
                V(dve.reciprocal(ur[:, 13, :], ur[:, 13, :]))
                tell(V, dve_to_act)
                for kind in range(3):
                    for j in range(2):
                        bk = dve_banks.take(dve)
                        for m in range(2):
                            jj = 2 * j + m
                            src = bk[:, SEQ * m:SEQ * m + SEQ]
                            s = dve_banks.freed if m else None
                            if kind < 2:
                                c0 = col(("w0", "a0")[kind])[:, jj:jj + 1]
                                V(dve.tensor_scalar(za[:, kind, jj, :], src, c0, LOW, ALU.add, ALU.max), s)
                            else:
                                V(dve.tensor_copy(g[:, jj, :], src), s)
                ask_act()
                V(dve.tensor_scalar(za, za, 1.0, None, ALU.add))
                V(dve.reciprocal(za, za))
                V(dve.tensor_scalar(zz, zz, -float(np.exp(-0.5)), None, ALU.mult))
                V(dve.tensor_tensor(kk, k_raw, last(col("kk"), SEQ), ALU.mult))
                V(dve.tensor_tensor(e4[:, 0], kk, kk, ALU.mult))
                column_sums_dve(lambda k, bk: dve.tensor_scalar(e4[:, 1, k, :], bk, 1e-24, None, ALU.max))
                ask_act()
                V(dve.reciprocal(e4[:, 1], e4[:, 1]))
                V(dve.tensor_tensor(kk, kk, e4[:, 1], ALU.mult))
                V(dve.tensor_scalar(k2, aa, 1.0, None, ALU.subtract))
                V(dve.tensor_tensor(k2, k2, last(col("ka"), SEQ), ALU.mult))
                V(stt(k2, k2, 1.0, k_raw, ALU.add, ALU.mult))
                V(dve.tensor_copy(v, v_raw))
                V(dve.tensor_tensor(e4[:, 0], ra, k2, ALU.mult))
                V(dve.tensor_tensor(e4[:, 0], e4[:, 0], last(col("rk"), SEQ), ALU.mult))
                column_sums_dve(lambda k, bk: dve.tensor_tensor(bonus[:, k, :], bk, v[:, k, :], ALU.mult))
                for j in range(HC):
                    V(dve.tensor_tensor_scan(b[:, j, :], const("restart"), zz[:, j, :], 0.0, ALU.mult, ALU.add))
                bc = chunks(b)
                end = bc[:, :, CH - 1:CH].broadcast_to([P, HC * SEQ // CH, CH])
                V(dve.tensor_tensor(e4[:, 0], b, zz, ALU.subtract))
                V(dve.tensor_scalar(e4[:, 1], b, -1.0, None, ALU.mult))
                V(dve.tensor_copy(e4[:, 2], b))
                V(dve.tensor_tensor(chunks(e4[:, 3]), end, bc, ALU.subtract))
                ask_act()
                V(dve.tensor_tensor(kappa, kk, e4[:, 0], ALU.mult))
                V(stt(kk, kk, -1.0, aa, ALU.mult, ALU.mult))
                for dst, src, n in ((beta, kk, 1), (key, k2, 1), (r_e, ra, 2), (beta_end, kk, 3), (key_end, k2, 3)):
                    V(dve.tensor_tensor(dst, src, e4[:, n], ALU.mult))
                V(dve.tensor_copy(el.rearrange("p j c -> p (j c)"), chunks(e4[:, 2])[:, :, CH - 1]))
                V(dve.memset(S[:, 0], 0.0))
                tell(V, dve_to_pe)
                for B in range(NX):
                    for dst in (Z[:, :, 0:64], ke_tok, beta_tok, v_tok):
                        bk = dve_banks.take(dve)
                        src = bk[:, :] if len(dst.shape) == 2 else bk[:, :].rearrange("p (h e) -> p h e", e=64)
                        V(dve.tensor_copy(dst, src), dve_banks.freed)
                    for m in range(HC):
                        V(dve.tensor_tensor(DI[:, m], mid(const("eye_pair"), NCH),
                                            last(el[:, m, NCH * B:NCH * B + NCH], 64), ALU.mult))
                    for o in range(2):
                        heads = range(o, 8, 2)
                        hs = slice(o, 8, 2)
                        quad = lambda bk: bk[:, :].rearrange("p (q t) -> p q t", q=4)
                        for dst, m in ((Pt0[0], "chunk_before_st"), (P0[0], "chunk_before_ts"), (Nt, "chunk_before_st"),
                                       (Y1[:, hs], "chunk_upto_st"), (Y2[:, hs], "chunk_upto_st")):
                            bk = dve_banks.take(dve)
                            V(dve.tensor_tensor(dst, quad(bk), mid(const(m), 4), ALU.mult), dve_banks.freed)
                        bk = dve_banks.take(dve)
                        V(dve.tensor_copy(Z[:, hs, 64:P], bk[:, 0:256].rearrange("p (q e) -> p q e", q=4)), dve_banks.freed)
                        for j in range(4):
                            bk = dve_banks.take(dve)
                            V(dve.tensor_tensor(Z[:, hs], Z[:, hs], quad(bk), ALU.add), dve_banks.freed)
                            if j < 3:
                                bk = dve_banks.take(dve)
                                V(dve.tensor_copy(Pt0[(j + 1) % 2], quad(bk)), dve_banks.freed)
                            if j < 2:
                                bk = dve_banks.take(dve)
                                V(dve.tensor_copy(P0[(j + 1) % 2], quad(bk)), dve_banks.freed)
                        for q, h in enumerate(heads):
                            for k, src in enumerate((beta_tok[:, 64 * h:64 * h + 64], v_tok[:, h, :], Z[:, h, 64:P])):
                                V(dve.tensor_tensor(spread[:, k], mid(src, NCH), last(const("chunk_of"), 64), ALU.mult))
                            tell(V, dve_to_pe)
                            bk = dve_banks.take(dve)
                            V(dve.tensor_copy(GT[0:64, h].rearrange("p c e -> p (c e)"), bk[0:64, :]), dve_banks.freed)
                            bk = dve_banks.take(dve)
                            V(dve.tensor_copy(H[0:64, h].rearrange("p c e -> p (c e)"), bk[0:64, :]), dve_banks.freed)
                    if B:
                        V(dve.tensor_copy(S[0:64, 0], S[0:64, NCH]))
                    tell(V, dve_to_pe)
                    for c in range(NCH):
                        bk = dve_banks.take(dve)
                        V(dve.tensor_tensor(S[0:64, c + 1], bk[0:64, :].rearrange("p (h e) -> p h e", e=64),
                                            H[0:64, :, c, :], ALU.add), dve_banks.freed)
                    for o in range(2):
                        bk = dve_banks.take(dve)
                        V(dve.tensor_copy(R[0:64].rearrange("p q t -> p (q t)"), bk[0:64, :]), dve_banks.freed)
                        bk = dve_banks.take(dve)
                        V(dve.tensor_copy(obT[64 * o:64 * o + 64, :, P * B:P * B + P],
                                          bk[0:64, :].rearrange("p (m t) -> p m t", m=HC)), dve_banks.freed)
                column_sums_dve(lambda k, bk: stt(obT[:, k, :], bk, -1.0 / 64, obT[:, k, :]))
                V(dve.tensor_tensor(e_post[0], obT, obT, ALU.mult))
                column_sums_dve(lambda k, bk: dve.tensor_copy(e_post[1][:, k, :], bk))
                rms_rows(e_post[1], 1.0 / 64, LN_EPS)
                V(dve.tensor_tensor(obT, obT, e_post[1], ALU.mult))
                for j in range(HC):
                    V(dve.tensor_scalar(obT[:, j, :], obT[:, j, :], col("lnw")[:, j:j + 1], col("lnb")[:, j:j + 1],
                                        ALU.mult, ALU.add))
                V(dve.tensor_tensor(obT, obT, bonus, ALU.add))
                V(dve.tensor_tensor(obT, obT, g, ALU.mult))

            def act_part():
                dve_to_act.wait(act)
                A(act.activation(ur[0:64, 12, :], ur[0:64, 12, :], ACT.Tanh))
                A(act.activation(ur[:, 13, :], ur[:, 13, :], ACT.Exp, scale=-1.0))
                tell(A, act_to_dve)
                dve_to_act.wait(act)
                tell(A, act_to_pe)
                exp_of(za, za, -1.0)
                exp_of(e4[:, 1], e4[:, 1], func=ACT.Sqrt)
                exp_of(e4, e4)
                rsqrt_act(e_post[1])
            return dict(sp=sp_part, pe=pe_part, dve=dve_part, act=act_part)

        def out_stage(w, lhs):
            ps = [add_panel(krows(w, 512 * k, 512 * k + 512), KC, 512) for k in range(2)]

            def sp_part():
                for n in ps:
                    load_panel(n)

            def pe_part():
                dve_to_pe.wait(pe)
                for n in ps:
                    rows_of_panel(n, T2, 512, lhs)

            def dve_part():
                tell(V, dve_to_pe)
                residual_dve(T2, None)
            return dict(sp=sp_part, pe=pe_part, dve=dve_part)

        def mlp_stage(l):
            work = Space(*WORK2)
            uT = work.take(FFN // P, SEQ)
            ups = [add_panel(krows(d["w_up_2"][l], 512 * n, 512 * n + 512), KC, 512) for n in range(8)]
            downs = [add_panel(d["w_down_2"][l][512 * n:512 * n + 512, :].rearrange("(c p) n -> p c n", p=P), 4, D)
                     for n in range(8)]

            def sp_part():
                for n in ups + downs:
                    load_panel(n)

            def pe_part():
                for n in ups:
                    cols_of_panel(n, 4, SEQ)
                dve_banks.settled(pe)
                places = [(h, t) for h in range(2) for t in range(NX)]
                banks = [dve_banks.claim(pe) for _ in places]
                for m, n in enumerate(downs):
                    w = open_panel(pe, n)
                    for (h, t), bank in zip(places, banks):
                        for c in range(4):
                            ins = mm(bank[:, :], uT[:, 4 * m + c, P * t:P * t + P], w[:, c, 512 * h:512 * h + 512],
                                     m == 0 and c == 0, m == 7 and c == 3)
                        if m == 7:
                            full(dve_banks, ins)
                    pe_used(n)

            def dve_part():
                for j in range(FFN // P):
                    bk = dve_banks.take(dve)
                    V(dve.tensor_scalar(uT[:, j, :], bk[:, 0:SEQ], 0.0, None, ALU.max))
                    V(dve.tensor_tensor(uT[:, j, :], uT[:, j, :], uT[:, j, :], ALU.mult), dve_banks.freed)
                residual_dve(T2, None)
            return dict(sp=sp_part, pe=pe_part, dve=dve_part)

        def ple_stage(l):
            work = Space(*WORK2)
            pT = work.take(PLE // P, SEQ)
            gain = work.take(D)
            pp, gg = work.take(NX, D), work.take(NX, D)
            sq = work.take(D)
            xT = view(HT, KC, 512)
            ss = small[:, 0:NX]
            proj = add_panel(d["ple_proj_2"][l].rearrange("(c p) n -> p c n", p=P), PLE // P, D)
            gs = [add_panel(krows(d["ple_gate_2"][l], 512 * k, 512 * k + 512), KC, 512) for k in range(2)]

            def sp_part():
                dve_to_sp.wait(sp)
                load_table(f"ple{l}", (pT, d["pT"][l].rearrange("(c p) t -> p c t", p=P)),
                           (gain, d["ple_rows"][:, D * l:D * l + D]))
                for n in [proj] + gs:
                    load_panel(n)

            def pe_part():
                dve_to_pe.wait(pe)
                for t in range(NX):
                    for h in range(2):
                        b = dve_banks.claim(pe)
                        for j in range(4):
                            c = 4 * h + j
                            ins = pe.transpose(b[:, P * j:P * j + P], x[:, 2 + t, P * c:P * c + P], ident)
                        full(dve_banks, ins)
                table_in(pe, f"ple{l}")
                w = open_panel(pe, proj)
                for t in range(NX):
                    for h in range(2):
                        b = dve_banks.claim(pe)
                        for c in range(PLE // P):
                            ins = mm(b[:, :], pT[:, c, P * t:P * t + P], w[:, c, 512 * h:512 * h + 512],
                                     c == 0, c == PLE // P - 1)
                        full(dve_banks, ins)
                pe_used(proj)
                dve_banks.settled(pe)
                for n in gs:
                    rows_of_panel(n, range(NX), 512, ht)

            def dve_part():
                tell(V, dve_to_sp)
                tell(V, dve_to_pe)
                for t in range(NX):
                    for h in range(2):
                        b = dve_banks.take(dve)
                        V(dve.tensor_copy(xT[:, 4 * h:4 * h + 4, P * t:P * t + P],
                                          b[:, :].rearrange("p (c t) -> p c t", c=4)), dve_banks.freed)
                for t in range(NX):
                    for h in range(2):
                        b = dve_banks.take(dve)
                        V(dve.tensor_copy(pp[:, t, 512 * h:512 * h + 512], b[:, :]), dve_banks.freed)
                for t in range(NX):
                    V(dve.tensor_tensor(sq, pp[:, t, :], pp[:, t, :], ALU.mult))
                    V(dve.tensor_reduce(ss[:, t:t + 1], sq, AX.X, ALU.add))
                rms_rows(ss, 1.0 / D)
                table_in(dve, f"ple{l}")
                for t in range(NX):
                    V(stt(pp[:, t, :], pp[:, t, :], ss[:, t:t + 1], gain, ALU.mult, ALU.mult))
                for h in range(2):
                    for t in range(NX):
                        b = dve_banks.take(dve)
                        V(dve.tensor_scalar(gg[:, t, 512 * h:512 * h + 512], b[:, :], LOW, None, ALU.max), dve_banks.freed)
                ask_act()
                V(dve.tensor_scalar(gg, gg, 1.0, None, ALU.add))
                V(dve.reciprocal(gg, gg))
                V(dve.tensor_tensor(gg, gg, pp, ALU.mult))
                V(dve.tensor_tensor(x[:, 2:4, :], x[:, 2:4, :], gg, ALU.add))

            def act_part():
                rsqrt_act(ss)
                exp_of(gg, gg, -1.0)
            return dict(sp=sp_part, pe=pe_part, dve=dve_part, act=act_part)

        def causal_stage():
            work = Space(*WORK2)
            qkv = work.take(NX, 24, HEAD2)
            qT, kT = work.take(8, SEQ), work.take(8, SEQ)
            o = work.take(NX, D)
            s_sb, p_sb, pT = work.take(2, SEQ), work.take(2, SEQ), work.take(2, SEQ)
            mask = work.take(NX, SEQ)
            tmp = work.take(3072)
            ps = [add_panel(krows(d["w_qkv_2"][0], 512 * n, 512 * n + 512), KC, 512) for n in range(6)]
            units = [(h, t, t + 1) for h in range(8) for t in range(NX)]
            att = attention(units, HEAD2, lambda h, t: qT[:, h, P * t:P * t + P], lambda h, nk: kT[:, h, 0:P * nk],
                            lambda h, j: qkv[:, j, 16 + h, :], lambda h, t: o[:, t, P * h:P * h + P], HEAD2 ** -0.5,
                            lambda t, nk: mask[:, t, 0:P * nk], None, dict(s=s_sb, p=p_sb, pT=pT))

            def sp_part():
                dve_to_sp.wait(sp)
                o_, w_ = TABLES["causal"]
                load_table("causal", (mask.rearrange("p a b -> p (a b)"), d["tables"][:, o_:o_ + w_]))
                for n in ps:
                    load_panel(n)

            def pe_part():
                for n in ps:
                    rows_of_panel(n, range(NX), 512, ht)
                dve_to_pe.wait(pe)
                transposed_pe(lambda h, t: qkv[:, t, h, :], range(NX), range(16))
                dve_banks.settled(pe)
                att["pe"]()
                for t in range(NX):
                    for hf in range(2):
                        b = dve_banks.claim(pe)
                        for j in range(4):
                            c = 4 * hf + j
                            ins = pe.transpose(b[:, P * j:P * j + P], o[:, t, P * c:P * c + P], ident)
                        full(dve_banks, ins)
                dve_banks.settled(pe)

            def dve_part():
                tell(V, dve_to_sp)
                for n in range(6):
                    for t in range(NX):
                        b = dve_banks.take(dve)
                        V(dve.tensor_copy(qkv[:, t, 4 * n:4 * n + 4, :].rearrange("p h e -> p (h e)"), b[:, :]),
                          dve_banks.freed)
                for t in range(NX):
                    head_norm_rope(qkv[:, t], range(16), [(0, 8, row("q2")), (8, 16, row("k2"))],
                                   const("cos2", NX, 64)[:, t], const("sin2", NX, 64)[:, t], HEAD2, tmp)
                tell(V, dve_to_pe)
                table_in(dve, "causal")
                transposed_dve(lambda h: qT[:, h, :] if h < 8 else kT[:, h - 8, :], range(NX), range(16))
                att["dve"]()
                for t in range(NX):
                    for hf in range(2):
                        b = dve_banks.take(dve)
                        V(dve.tensor_copy(hT[:, 4 * hf:4 * hf + 4, P * t:P * t + P],
                                          b[:, :].rearrange("p (c t) -> p c t", c=4)), dve_banks.freed)

            def act_part():
                for t in range(NX):
                    norm_act(16)
                att["act"]()
            return dict(sp=sp_part, pe=pe_part, dve=dve_part, act=act_part)

        def store_stage():
            def sp_part():
                dve_to_sp.wait(sp)
                sp.dma_start(d["out"].rearrange("a (t p) n -> p (a t) n", p=P), x[:, 2:4, :]).then_inc(out_written.sem, 16)
                sp.wait_ge(out_written.sem, 16)
            return dict(sp=sp_part, dve=lambda: tell(V, dve_to_sp))

        plan = [load_stage()]
        r = lambda t: t // 2
        for i in range(2):
            plan.append(mod_stage(i))
            plan.append(norm_stage(range(4), lambda c, t: norm_a[:, 0, c, r(t):r(t) + 1],
                                     lambda c, t: mod_col[:, c, r(t):r(t) + 1]))
            if i == 0:
                conv, bT = conv_stage()
                plan.append(conv)
                plan.append(attention_stage(0, d["w_in_ab"][0], d["w_out_ab"][0],
                                              lambda c, t: bT[:, c, P * t:P * t + P], (0, 1, 2, 3), ("qa", "ka"), False))
            else:
                pl, yT = pool_stage()
                plan.append(pl)
                plan.append(attention_stage(1, d["w_in_cd"][0], d["w_out_cd"][0],
                                              lambda c, t: yT[:, c, P * (t - 2):P * (t - 2) + P], (2, 3), ("qc", "kc"), True))
            plan.append(norm_stage(range(4) if i == 0 else (2, 3), lambda c, t: norm_a[:, 1, c, r(t):r(t) + 1],
                                     lambda c, t: mod_col[:, 24 + c, r(t):r(t) + 1],
                                     first_tile=0 if i == 0 else 2))
            plan.append(moe_stage(i, (0, 1, 2, 3) if i == 0 else (2, 3)))
        ring["n"] = 3
        oT = view(WORK2[0], HC, SEQ)
        obT = view(WORK2[0] + HC * SEQ, HC, SEQ)

        def norm2(name):
            return norm_stage((2, 3), lambda c, t: col(name)[:, c:c + 1], first_tile=2)
        for l in range(2):
            plan.append(norm2(f"an_{l}"))
            if l == 0:
                plan += [hgrn_stage(oT), rwkv_stage(obT)]
                plan.append(out_stage(d["w_out_ar_2"][0],
                                        lambda c, t: (oT if c < HC else obT)[:, c % HC, P * (t - 2):P * (t - 2) + P]))
            else:
                plan.append(causal_stage())
                plan.append(out_stage(d["w_o_attn_2"][0], lambda c, t: hT[:, c, P * (t - 2):P * (t - 2) + P]))
            plan += [norm2(f"mn_{l}"), mlp_stage(l), ple_stage(l)]
        plan.append(store_stage())

        @block.sync
        def _(_sp):
            for stage in plan:
                stage.get("sp", lambda: None)()

        @block.tensor
        def _(_pe):
            for stage in plan:
                stage.get("pe", lambda: None)()

        @block.vector
        def _(_dve):
            for stage in plan:
                stage.get("dve", lambda: None)()

        @block.scalar
        def _(_act):
            for stage in plan:
                stage.get("act", lambda: None)()

        @block.gpsimd
        def _(_pool):
            for stage in plan:
                stage.get("pool", lambda: None)()


def shape_tables():
    c = np.zeros((P, NCONST), np.float32)
    t = np.zeros((P, NTABLE), np.float32)

    def put(a, name, v):
        where, arr = (CONSTS, c) if a == "c" else (TABLES, t)
        o, w = where[name]
        arr[:, o:o + w] = np.broadcast_to(np.asarray(v, np.float32).reshape(np.shape(v)[0], -1), (P, w))
    i = np.arange(P)
    p_, q_ = i[:, None], i[None, :]
    same = p_ // CH == q_ // CH
    put("c", "ident", np.eye(P))
    put("c", "ones", np.ones((P, P)))
    put("c", "before", p_ < q_)
    put("c", "pair_ones", p_ // 64 == q_ // 64)
    put("c", "chunk_before_st", same & (p_ < q_))
    put("c", "chunk_before_ts", same & (q_ < p_))
    put("c", "chunk_upto_st", same & (p_ <= q_))
    put("c", "chunk_of", p_ // CH == np.arange(NCH)[None])
    put("c", "restart", np.broadcast_to((np.arange(SEQ) % CH != 0)[None], (P, SEQ)))
    tok = np.arange(SEQ)
    inv = (np.float32(10000.0) ** (-np.arange(16, dtype=np.float32) / np.float32(16))).astype(np.float32)
    ang = np.concatenate([(tok // 64).astype(np.float32)[:, None] * inv, (tok % 64).astype(np.float32)[:, None] * inv], -1)
    cos = np.concatenate([np.ones((2, P, 32)), np.cos(ang).reshape(2, P, 32)]).transpose(1, 0, 2)
    sin = np.concatenate([np.zeros((2, P, 32)), np.sin(ang).reshape(2, P, 32)]).transpose(1, 0, 2)
    put("c", "cos", cos)
    put("c", "sin", sin)
    inv = (np.float32(10000.0) ** (-np.arange(64, dtype=np.float32) / np.float32(64))).astype(np.float32)
    ang = tok.astype(np.float32)[:, None] * inv[None]
    put("c", "cos2", np.cos(ang).reshape(2, P, 64).transpose(1, 0, 2))
    put("c", "sin2", np.sin(ang).reshape(2, P, 64).transpose(1, 0, 2))
    put("c", "expert", np.broadcast_to(np.arange(NEXP)[None], (P, NEXP)))
    put("c", "eye_pair", p_ % 64 == np.arange(64)[None])
    put("c", "group", np.broadcast_to((np.arange(NEXP) // EPG)[None], (P, NEXP)))
    put("c", "token", np.arange(4)[None] * P + p_)
    sel = np.zeros((P, 2, P))
    sel[0, 0] = sel[1, 1] = 1
    put("c", "rowsel", sel)
    qpos = np.arange(SEQ)
    far = np.where(np.abs(qpos[:, None] - qpos[None]) <= 128, 0.0, -BIG)
    band = np.concatenate([np.zeros((SEQ, SEQ)), far], 1)
    put("t", "band", band.reshape(NX, P, 512).transpose(1, 0, 2))
    causal = np.where(qpos[None] <= qpos[:, None], 0.0, -BIG)
    put("t", "causal", causal.reshape(NX, P, SEQ).transpose(1, 0, 2))
    pm = np.zeros((SEQ, 4, SEQ))
    for g, w in enumerate((2, 4, 8, 16)):
        for s in range(SEQ):
            lo, hi = max(s - w // 2, 0), min(s - w // 2 + w, SEQ)
            pm[lo:hi, g, s] = 1.0 / (hi - lo)
            pm[s, g, s] -= 1.0
    put("t", "pool", pm.reshape(NX, P, 4, SEQ).transpose(1, 0, 2, 3))
    return c, t


def layout(v):
    def dcol(a):
        return a.reshape(-1, P).T
    cols = {
        "ln1_0": dcol(v["ln1_g"][0]), "ln1_1": dcol(v["ln1_g"][1]),
        "ln2_0": dcol(v["ln2_g"][0]), "ln2_1": dcol(v["ln2_g"][1]),
        "cond": np.stack([dcol(v["c_ctx"]), dcol(v["c"][0])], -1).reshape(P, -1),
        "conv_w": v["conv_w"][0].reshape(TAPS, HC, P).transpose(2, 1, 0).reshape(P, -1),
        "conv_b": dcol(v["conv_b"][0]), "conv_g": dcol(v["conv_ln_g"][0]), "conv_lb": dcol(v["conv_ln_b"][0]),
        "pool_scale": dcol(v["pool_scale"][0]),
        "an_0": dcol(v["attn_norm_2"][0]), "an_1": dcol(v["attn_norm_2"][1]),
        "mn_0": dcol(v["mlp_norm_2"][0]), "mn_1": dcol(v["mlp_norm_2"][1]),
        "lb": v["hgrn_lb_2"].reshape(3 * HC, P).T, "onorm": dcol(v["hgrn_onorm_2"][0]), "mu": dcol(v["rwkv_mu_2"][0]),
        "w0": dcol(v["rwkv_w0_2"][0]), "a0": dcol(v["rwkv_a0_2"][0]), "kk": dcol(v["rwkv_kk_2"][0]),
        "ka": dcol(v["rwkv_ka_2"][0]), "rk": dcol(v["rwkv_rk_2"][0]),
        "lnw": dcol(v["rwkv_ln_w_2"][0]), "lnb": dcol(v["rwkv_ln_b_2"][0]),
    }
    rows = {
        "qa": v["q_norm_a"][0], "ka": v["k_norm_a"][0], "qc": v["q_norm_c"][0], "kc": v["k_norm_c"][0],
        "q2": v["q_norm_2"][0], "k2": v["k_norm_2"][0], "sink": v["sink_c"][0],
        "rtb_0": np.concatenate([v["rt_grp_b"][0], v["rt_exp_b"][0]]),
        "rtb_1": np.concatenate([v["rt_grp_b"][1], v["rt_exp_b"][1]]),
    }
    out = {
        "cols": np.concatenate([cols[k] for k in COLS], 1),
        "rows": np.repeat(np.concatenate([rows[k] for k in ROWS])[None], P, 0),
        "mod_b": np.repeat(v["mod_b"][:, None], 2, 1),
        "rt_w": np.concatenate([v["rt_grp_w"], v["rt_exp_w"]], -1),
        "ple_rows": np.repeat(v["ple_norm_2"].reshape(1, -1), P, 0),
        "pT": v["p_2"][:, 0].transpose(0, 2, 1),
    }
    return {k: np.ascontiguousarray(a) for k, a in out.items()}


DIRECT = ["x", "ctx", "mod_w", "w_in_ab", "w_out_ab", "w_in_cd", "w_out_cd", "pool_w", "ex_gate", "ex_up",
          "ex_down", "w_in_ar_2", "w_out_ar_2", "rwkv_w2_2", "rwkv_a2_2", "rwkv_g2_2", "w_qkv_2", "w_o_attn_2",
          "w_up_2", "w_down_2", "ple_proj_2", "ple_gate_2"]


def kernel(**inputs):
    import concourse.bacc as bacc
    from concourse.bass_utils import run_bass_kernel_spmd as run

    nc = bacc.Bacc("TRN2", target_bir_lowering=False, num_devices=1)
    v = {k: np.asarray(a) for k, a in inputs.items()}
    consts, tables = shape_tables()
    arrays = {**{k: np.ascontiguousarray(v[k]) for k in DIRECT}, **layout(v), "consts": consts, "tables": tables}
    d = {k: nc.dram_tensor(f"in_{k}", a.shape, F32, kind="ExternalInput").ap() for k, a in arrays.items()}
    d["out"] = nc.dram_tensor("out_x", (1, SEQ, D), F32, kind="ExternalOutput").ap()
    build_program(nc, d)
    return run(nc, [{f"in_{k}": a for k, a in arrays.items()}], core_ids=[0]).results[0]["out_x"]
```

```python
from contextlib import ExitStack

import numpy as np
import concourse.bass as bass
from concourse import mybir

P = 128
F32 = mybir.dt.float32
I32 = mybir.dt.int32
ALU = mybir.AluOpType
ACT = mybir.ActivationFunctionType
AX = mybir.AxisListType

D = 1024
KC = D // P
SEQ = 256
NX = SEQ // P
FFN = 4 * D
NEXP, NGRP = 32, 4
EPG = NEXP // NGRP
DE = D // 2
HALF = D // 2
HC = HALF // P
TAPS = 31
POOL_TAPS = 16
HD = 64
CH = 16
NCH = P // CH
EPS = 1e-6
LN_EPS = 64e-5
BIG = 1e30
PANEL = 4096
HEAD2 = 128
PLE = 256


def pack(entries):
    at, off = {}, 0
    for name, width in entries:
        at[name] = (off, width)
        off += width
    return at, off


CONSTS, NCONST = pack([
    ("ident", P), ("ones", P), ("before", P), ("pair_ones", P), ("chunk_before_st", P),
    ("chunk_before_ts", P), ("chunk_upto_st", P), ("chunk_of", NCH), ("restart", SEQ),
    ("cos", 4 * 32), ("sin", 4 * 32), ("cos2", NX * 64), ("sin2", NX * 64),
    ("eye_pair", 64), ("eps", 1), ("expert", NEXP), ("group", NEXP), ("token", 4), ("rowsel", 2 * P),
])
TABLES, NTABLE = pack([("band", NX * 512), ("pool", NX * 4 * SEQ), ("causal", NX * SEQ)])
COLS, NCOL = pack([
    ("ln1_0", KC), ("ln1_1", KC), ("ln2_0", KC), ("ln2_1", KC), ("cond", 2 * KC),
    ("conv_w", HC * TAPS), ("conv_b", HC), ("conv_g", HC), ("conv_lb", HC), ("pool_scale", HC),
    ("an_0", KC), ("an_1", KC), ("mn_0", KC), ("mn_1", KC), ("lb", 3 * HC), ("onorm", HC),
    ("mu", 14), ("w0", HC), ("a0", HC), ("kk", HC), ("ka", HC), ("rk", HC), ("lnw", HC), ("lnb", HC),
])
ROWS, NROW = pack([
    ("qa", HD), ("ka", HD), ("qc", HD), ("kc", HD), ("q2", HEAD2), ("k2", HEAD2), ("sink", 8),
    ("rtb_0", NGRP + NEXP), ("rtb_1", NGRP + NEXP),
])


class Signal:

    def __init__(self, sem):
        self.sem, self.sent, self.seen = sem, 0, {}

    def wait(self, eng, n=1):
        self.seen[eng.engine] = self.seen.get(eng.engine, 0) + n
        eng.wait_ge(self.sem, self.seen[eng.engine])


class Steps:

    def __init__(self, eng, order):
        self.eng, self.order = eng, order

    def __call__(self, ins, signal=None):
        s = signal or self.order
        ins.then_inc(s.sem, 1)
        s.sent += 1
        self.eng.wait_ge(s.sem, s.sent)


class Banks:

    def __init__(self, banks, full, freed):
        self.banks, self.full, self.freed = banks, full, freed
        self.filling = self.taking = 0

    def claim(self, pe):
        n = self.filling
        self.filling += 1
        if n >= len(self.banks):
            pe.wait_ge(self.freed.sem, n - len(self.banks) + 1)
        return self.banks[n % len(self.banks)]

    def settled(self, pe):
        if self.filling:
            pe.wait_ge(self.freed.sem, self.filling)

    def take(self, eng):
        n = self.taking
        self.taking += 1
        eng.wait_ge(self.full.sem, n + 1)
        return self.banks[n % len(self.banks)]


def build_program(nc, d):
    with ExitStack() as ctx:
        def signal(name):
            return Signal(ctx.enter_context(nc.semaphore(name)))

        WORK1 = 12800
        FIX = NCONST + NCOL + NROW + 2 * (3 * KC * 2) + 48 * 2 + 64
        RING, GATES, WORK = 0, 6 * PANEL, 6 * PANEL + 4096
        X = WORK + WORK1
        HT = X + 4096
        CONST = HT + 4096
        TOTAL = CONST + FIX
        big = ctx.enter_context(nc.sbuf_tensor("big", [P, TOTAL], F32))
        bigi = ctx.enter_context(nc.sbuf_tensor("bigi", [P, 24], I32))
        zeros_i = ctx.enter_context(nc.sbuf_tensor("zeros_i", [P, P], I32))[:, :]
        ibuf = ctx.enter_context(nc.sbuf_tensor("ibuf", [P, 8], mybir.dt.uint32))[:, :]
        expert_ids = ctx.enter_context(nc.sbuf_tensor("expert_ids", [P, NEXP + 8], I32))[:, :]
        pool_passed = ctx.enter_context(nc.semaphore("pool_passed"))
        psum = [ctx.enter_context(nc.psum_tensor(f"bank{i}", [P, 512], F32)) for i in range(8)]

        def view(off, *dims, p0=0, p1=P):
            n = int(np.prod(dims))
            ap = big[p0:p1, off:off + n]
            names = "abcd"[:len(dims)]
            if len(dims) > 1:
                ap = ap.rearrange(f"p ({' '.join(names)}) -> p {' '.join(names)}",
                                  **dict(zip(names[1:], dims[1:])))
            return ap

        class Space:

            def __init__(self, off, size):
                self.off, self.end = off, off + size

            def take(self, *dims):
                o = self.off
                self.off += int(np.prod(dims))
                assert self.off <= self.end, (self.off, self.end)
                return view(o, *dims)

        fixed = Space(CONST, FIX)
        const_sb, col_sb, row_sb = fixed.take(NCONST), fixed.take(NCOL), fixed.take(NROW)
        mod_col = fixed.take(48, 2)
        norm_a = fixed.take(2, KC, 2)
        small = fixed.take(96 + 32)

        def const(name, *dims):
            o, w = CONSTS[name]
            return view(CONST + o, *(dims or (w,)))

        def col(name, *dims):
            o, w = COLS[name]
            return view(CONST + NCONST + o, *(dims or (w,)))

        def row(name):
            o, w = ROWS[name]
            return row_sb[:, o:o + w]

        x = view(X, 4, D)
        hT = view(HT, KC, 512)
        gates = view(GATES, 4, D)
        ident = const("ident")
        ones = const("ones")

        loaded = signal("params_loaded")
        panel_full = [signal(f"panel_full{i}") for i in range(6)]
        panel_used = signal("panel_used")
        dve_banks = Banks(psum[0:4], signal("dve_bank_full"), signal("dve_bank_freed"))
        act_banks = Banks(psum[4:7], signal("act_bank_full"), signal("act_bank_freed"))
        dve_to_pe = signal("dve_result_for_pe")
        dve_to_act = signal("dve_result_for_act")
        dve_to_pool = signal("dve_result_for_pool")
        dve_to_sp = signal("dve_result_for_sp")
        act_to_dve = signal("act_result_for_dve")
        act_to_pe = signal("act_result_for_pe")
        act_to_pool = signal("act_result_for_pool")
        act_to_sp = signal("act_result_for_sp")
        results_zeroed = signal("results_zeroed")
        pool_to_dve = signal("pool_result_for_dve")
        pool_to_pe = signal("pool_result_for_pe")
        pool_to_act = signal("pool_result_for_act")
        stage_loaded = signal("stage_table_loaded")
        pe_done = signal("pe_loop_done")
        out_written = signal("out_written")

        block = ctx.enter_context(nc.Block())

        panels = []
        slot_owner = {}
        ring = {"n": 6, "next": 0, "moe": 0}
        panel_at = [0]
        slot_uses = {}

        def add_panel(src, *dims):
            s = ring["next"] % ring["n"]
            ring["next"] += 1
            slot_uses[s] = slot_uses.get(s, 0) + 1
            panels.append((s, view(RING + s * PANEL, *dims), src, slot_owner.get(s), slot_uses[s], ring["moe"]))
            slot_owner[s] = len(panels) - 1
            return len(panels) - 1

        def load_panel(n):
            s, dst, src, before, _, moe = panels[n]
            sp = nc.sync
            if before is not None:
                sp.wait_ge(panel_used.sem, before + 1)
            if moe:
                sp.wait_ge(pe_done.sem, moe)
            sp.dma_start(dst, src).then_inc(panel_full[s].sem, 16)

        stage_at = {}

        def load_table(name, *pairs):
            for dst, src in pairs:
                sp.dma_start(dst, src).then_inc(stage_loaded.sem, 16)
                stage_loaded.sent += 16
            stage_at[name] = stage_loaded.sent

        def table_in(eng, name):
            eng.wait_ge(stage_loaded.sem, stage_at[name])

        def open_panel(pe, n):
            s, dst, _, _, use, _ = panels[n]
            pe.wait_ge(panel_full[s].sem, 16 * use)
            return dst

        def krows(w, n0=None, n1=None):
            v = w.rearrange("(c p) n -> p c n", p=P)
            return v if n0 is None else v[:, :, n0:n1]

        pe, dve, act, pool, sp = nc.tensor, nc.vector, nc.scalar, nc.gpsimd, nc.sync
        V = Steps(dve, signal("dve_order"))
        A = Steps(act, signal("act_order"))
        G = Steps(pool, signal("pool_order"))

        def tell(steps, sig):
            steps.eng.sem_inc(sig.sem, 1)
            sig.sent += 1

        def bcast(ap, *dims):
            return ap.broadcast_to([ap.shape[0], *dims])

        def mid(ap, n):
            return ap.unsqueeze(1).broadcast_to([ap.shape[0], n, ap.shape[1]])

        def last(ap, n):
            return ap.unsqueeze(len(ap.shape)).broadcast_to([*ap.shape, n])

        def mm(out, lhsT, rhs, start, stop):
            return pe.matmul(out, lhsT, rhs, start=start, stop=stop, skip_group_check=True)

        def stt(out, in0, scalar, in1, op0=ALU.mult, op1=ALU.add):
            return dve.scalar_tensor_tensor(out=out, in0=in0, scalar=scalar, in1=in1, op0=op0, op1=op1)

        def full(banks, ins):
            ins.then_inc(banks.full.sem, 1)

        def load_stage():
            def sp_part():
                items = [(const_sb, d["consts"]), (col_sb, d["cols"]), (row_sb, d["rows"]),
                         (x[:, 0:2, :], d["ctx"].rearrange("a (t p) n -> p (a t) n", p=P)),
                         (x[:, 2:4, :], d["x"].rearrange("a (t p) n -> p (a t) n", p=P))]
                for dst, src in items:
                    sp.dma_start(dst, src).then_inc(loaded.sem, 16)
                loaded.sent = 16 * len(items)

            def wait_all(eng):
                eng.wait_ge(loaded.sem, 16 * 5)
            return dict(sp=sp_part, pe=lambda: wait_all(pe), dve=lambda: wait_all(dve),
                        act=lambda: wait_all(act), pool=lambda: wait_all(pool))

        def mod_stage(i):
            work = Space(WORK, WORK1)
            mod_row, mod_b = work.take(6 * D), work.take(6 * D)
            cond = small[:, 96:96 + 2 * KC].rearrange("p (c r) -> p c r", r=2)
            raw = col("cond", KC, 2)
            first = [add_panel(krows(d["mod_w"][i], 512 * n, 512 * n + 512), KC, 512) for n in range(12)]

            def sp_part():
                for n in first[:6]:
                    if i and n == first[2]:
                        sp.wait_ge(*rows_back[0])
                    load_panel(n)
                if i:
                    stage_in_dve(sp)
                load_table(f"mod_b{i}", (mod_b[0:2, :], d["mod_b"][i]))
                for n in first[6:]:
                    load_panel(n)

            def act_part():
                if i == 0:
                    A(act.activation(cond, raw, ACT.Silu))
                    tell(A, act_to_pe)

            def dve_part():
                if i:
                    tell(V, dve_to_sp)
                table_in(dve, f"mod_b{i}")
                for n in range(12):
                    b = dve_banks.take(dve)
                    c = slice(512 * n, 512 * n + 512)
                    V(dve.tensor_tensor(mod_row[0:2, c], b[0:2, :], mod_b[0:2, c], ALU.add), dve_banks.freed)
                b = dve_banks.take(dve)
                V(dve.tensor_copy(mod_col, b[:, 0:96].rearrange("p (n r) -> p n r", r=2)), dve_banks.freed)
                for k, at in enumerate((8, 32)):
                    V(stt(norm_a[:, k], mod_col[:, at:at + KC, :], 1.0,
                          last(col(f"ln{k + 1}_{i}"), 2), ALU.add, ALU.mult))
                for g in range(4):
                    for h in range(2):
                        b = dve_banks.take(dve)
                        V(dve.tensor_copy(gates[:, g, 512 * h:512 * h + 512], b[:, :]), dve_banks.freed)

            def pe_part():
                if i == 0:
                    act_to_pe.wait(pe)
                for n in first:
                    w = open_panel(pe, n)
                    b = dve_banks.claim(pe)
                    for c in range(KC):
                        ins = mm(b[0:2, :], cond[:, c, :], w[:, c, :], c == 0, c == KC - 1)
                    full(dve_banks, ins)
                    pe_used(n)
                dve_banks.settled(pe)
                b = dve_banks.claim(pe)
                for n in range(48):
                    ins = mm(b[:, 2 * n:2 * n + 2], mod_row[0:2, P * n:P * n + P], ident[0:2, 0:2], True, True)
                full(dve_banks, ins)
                for g in range(4):
                    at = (2 if g < 2 else 5) * D
                    for h in range(2):
                        b = dve_banks.claim(pe)
                        r = g % 2
                        full(dve_banks, mm(b[:, :], const("rowsel", 2, P)[0:2, r, :],
                                           mod_row[0:2, at + 512 * h:at + 512 * h + 512], True, True))
            return dict(sp=sp_part, act=act_part, dve=dve_part, pe=pe_part)

        def stage_in_dve(eng):
            dve_to_sp.wait(eng)

        def pe_used(n):
            b = psum[7]
            mm(b[0:2, 0:2], ident[0:2, 0:2], ident[0:2, 0:2], True, True).then_inc(panel_used.sem, 1)
            panel_used.sent += 1
            assert panel_used.sent == n + 1

        def norm_stage(tiles, gain, shift=None, first_tile=0):
            ssq, rstd = small[:, 0:4], small[:, 4:8]
            junk = view(WORK + WORK1 - 3072, D)
            xn = view(WORK + WORK1 - 2048, 2, D)

            def place(c, t):
                o = (t - first_tile) * P
                return hT[:, c, o:o + P]

            def dve_part():
                tell(V, dve_to_act)
                for k, t in enumerate(tiles):
                    act_to_dve.wait(dve)
                    if k >= 2:
                        dve.wait_ge(act_banks.full.sem, act_at[0] + k - 1)
                    V(dve.tensor_scalar(xn[:, k % 2, :], x[:, t, :], rstd[:, k:k + 1], None, ALU.mult))
                    tell(V, dve_to_pe)
                    if k:
                        take_half(k - 1)
                take_half(len(tiles) - 1)

            def take_half(k):
                t = tiles[k]
                b = dve_banks.take(dve)
                for c in range(4):
                    s = None if shift is None else shift(c, t)
                    ins = dve.tensor_scalar(place(c, t), b[:, P * c:P * c + P], gain(c, t), s,
                                            ALU.mult, *([ALU.add] if s is not None else []))
                    if c == 3:
                        V(ins, dve_banks.freed)

            def act_part():
                dve_to_act.wait(act)
                for k, t in enumerate(tiles):
                    m = slice(k, k + 1)
                    A(act.activation(junk, x[:, t, :], ACT.Square, accum_out=ssq[:, m]))
                    A(act.activation(rstd[:, m], ssq[:, m], ACT.Ln, bias=const("eps"), scale=1.0 / D))
                    A(act.activation(rstd[:, m], rstd[:, m], ACT.Exp, scale=-0.5))
                    tell(A, act_to_dve)
                for k, t in enumerate(tiles):
                    b = act_banks.take(act)
                    for j in range(4):
                        c = 4 + j
                        s = 0.0 if shift is None else shift(c, t)
                        ins = act.activation(place(c, t), b[:, P * j:P * j + P], ACT.Identity, bias=s, scale=gain(c, t))
                        if j == 3:
                            A(ins, act_banks.freed)

            act_at = [0]

            def pe_part():
                act_at[0] = act_banks.filling
                for k, t in enumerate(tiles):
                    dve_to_pe.wait(pe)
                    for h, banks in enumerate((dve_banks, act_banks)):
                        b = banks.claim(pe)
                        for j in range(4):
                            c = 4 * h + j
                            ins = pe.transpose(b[:, P * j:P * j + P], xn[:, k % 2, P * c:P * c + P], ident)
                        full(banks, ins)
                dve_banks.settled(pe)
                act_banks.settled(pe)
            return dict(dve=dve_part, act=act_part, pe=pe_part)

        def rows_of_panel(n, tiles, width, lhs, banks=None):
            banks = banks or dve_banks
            w = open_panel(pe, n)
            kc = w.shape[1]
            for t in tiles:
                b = banks.claim(pe)
                for c in range(kc):
                    ins = mm(b[:, 0:width], lhs(c, t), w[:, c, :], c == 0, c == kc - 1)
                full(banks, ins)
            pe_used(n)

        def cols_of_panel(n, nblocks, ntok, off=0, banks=None):
            banks = banks or dve_banks
            w = open_panel(pe, n)
            for j in range(nblocks):
                b = banks.claim(pe)
                for c in range(KC):
                    ins = mm(b[:, 0:ntok], w[:, c, P * j:P * j + P], hT[:, c, off:off + ntok], c == 0, c == KC - 1)
                full(banks, ins)
            pe_used(n)

        def ht(c, t):
            return hT[:, c, P * t:P * t + P]

        def exp_of(act_out, act_in, scale=1.0, func=ACT.Exp):
            dve_to_act.wait(act)
            A(act.activation(act_out, act_in, func, scale=scale))
            tell(A, act_to_dve)

        def ask_act():
            tell(V, dve_to_act)
            act_to_dve.wait(dve)

        def residual_dve(tiles, gate_of):
            tmp = view(WORK + WORK1 - 512, 512)
            for h in range(2):
                for t in tiles:
                    b = dve_banks.take(dve)
                    c = slice(512 * h, 512 * h + 512)
                    if gate_of is None:
                        V(dve.tensor_tensor(x[:, t, c], x[:, t, c], b[:, :], ALU.add), dve_banks.freed)
                    else:
                        V(dve.tensor_tensor(tmp, b[:, :], gate_of(t)[:, c], ALU.mult), dve_banks.freed)
                        V(dve.tensor_tensor(x[:, t, c], x[:, t, c], tmp, ALU.add))

        def attention(units, hd, q_of, k_of, v_of, o_of, scale, mask_of, sink_of, buf):
            s_sb, p_sb, pT = buf["s"], buf["p"], buf["pT"]
            nmax, den, rec, sunk = small[:, 32:36], small[:, 36:40], small[:, 40:44], small[:, 44:48]
            N = len(units)

            def scores(n):
                h, t, nk = units[n]
                b = act_banks.claim(pe)
                full(act_banks, mm(b[:, 0:P * nk], q_of(h, t), k_of(h, nk), True, True))

            def values(n):
                h, t, nk = units[n]
                pe.wait_ge(dve_banks.freed.sem, t_jobs[n] + 1)
                b = dve_banks.claim(pe)
                for j in range(nk):
                    ins = mm(b[:, 0:hd], pT[:, n % 2, P * j:P * j + P], v_of(h, j), j == 0, j == nk - 1)
                v_jobs[n] = dve_banks.filling - 1
                full(dve_banks, ins)
            t_jobs, v_jobs = {}, {}

            def pe_part():
                for n in range(min(2, N)):
                    scores(n)
                for n, (h, t, nk) in enumerate(units):
                    if n + 2 < N:
                        scores(n + 2)
                    act_to_pe.wait(pe)
                    b = dve_banks.claim(pe)
                    t_jobs[n] = dve_banks.filling - 1
                    for j in range(nk):
                        ins = pe.transpose(b[:, P * j:P * j + P], p_sb[:, n % 2, P * j:P * j + P], ident)
                    full(dve_banks, ins)
                    if n:
                        values(n - 1)
                values(N - 1)
                dve_banks.settled(pe)

            def highest(n):
                h, t, nk = units[n]
                at = attention_marks[id(units)][1] + n
                dve.wait_ge(act_banks.full.sem, at + 1)
                b = act_banks.banks[at % len(act_banks.banks)]
                m = nmax[:, n % 4:n % 4 + 1]
                if mask_of is None:
                    V(dve.tensor_reduce(m, b[:, 0:P * nk], AX.X, ALU.max))
                    V(dve.tensor_scalar(m, m, -scale, None, ALU.mult))
                else:
                    s = s_sb[:, n % 3, 0:P * nk]
                    V(stt(s, b[:, 0:P * nk], scale, mask_of(t, nk)))
                    V(dve.tensor_reduce(m, s, AX.X, ALU.max))
                    if sink_of is None:
                        V(dve.tensor_scalar(m, m, -1.0, None, ALU.mult))
                    else:
                        V(dve.tensor_scalar(m, m, sink_of(h), -1.0, ALU.max, ALU.mult))
                tell(V, dve_to_act)

            def results_of(n):
                h, t, nk = units[n]
                k = slice(n % 4, n % 4 + 1)
                if sink_of is not None:
                    V(dve.tensor_tensor(den[:, k], den[:, k], sunk[:, k], ALU.add))
                V(dve.reciprocal(rec[:, k], den[:, k]))
                b = dve_banks.take(dve)
                V(dve.tensor_scalar(o_of(h, t), b[:, 0:hd], rec[:, k], None, ALU.mult), dve_banks.freed)

            def dve_part():
                for n in range(min(2, N)):
                    highest(n)
                for n, (h, t, nk) in enumerate(units):
                    act_to_dve.wait(dve)
                    if n + 2 < N:
                        highest(n + 2)
                    b = dve_banks.take(dve)
                    if n >= 2:
                        dve.wait_ge(dve_banks.full.sem, v_jobs[n - 2] + 1)
                    V(dve.tensor_copy(pT[:, n % 2, 0:P * nk], b[:, 0:P * nk]), dve_banks.freed)
                    if n:
                        results_of(n - 1)
                results_of(N - 1)

            def act_part():
                for n, (h, t, nk) in enumerate(units):
                    k = slice(n % 4, n % 4 + 1)
                    dve_to_act.wait(act)
                    b = act_banks.take(act)
                    if n >= 2:
                        act.wait_ge(dve_banks.full.sem, t_jobs[n - 2] + 1)
                    if mask_of is None:
                        A(act.activation(p_sb[:, n % 2, 0:P * nk], b[:, 0:P * nk], ACT.Exp, bias=nmax[:, k],
                                         scale=scale, accum_out=den[:, k]), act_banks.freed)
                    else:
                        if sink_of is not None:
                            A(act.activation(sunk[:, k], sink_of(h), ACT.Exp, bias=nmax[:, k]))
                        A(act.activation(p_sb[:, n % 2, 0:P * nk], s_sb[:, n % 3, 0:P * nk], ACT.Exp,
                                         bias=nmax[:, k], accum_out=den[:, k]), act_banks.freed)
                    tell(A, act_to_pe)
                    tell(A, act_to_dve)

            def pe_whole():
                attention_marks[id(units)] = (dve_banks.filling, act_banks.filling)
                pe_part()
            return dict(pe=pe_whole, act=act_part, dve=dve_part)

        attention_marks = {}

        def head_norm_rope(src, heads, gain_of, cos, sin, hd, tmp, rope=True):
            n = len(heads)
            h0, h1 = heads[0], heads[-1] + 1
            v = src[:, h0:h1, :]
            sq = tmp[:, 0:n * hd].rearrange("p (h e) -> p h e", e=hd)
            ss = small[:, 16:16 + n]
            V(dve.tensor_tensor(sq, v, v, ALU.mult))
            V(dve.tensor_reduce(ss, sq, AX.X, ALU.add))
            V(dve.tensor_scalar(ss, ss, 1.0 / hd, EPS, ALU.mult, ALU.add))
            ask_act()
            gain_rope(V, src, v, ss, gain_of, cos, sin, hd, tmp, rope)

        def gain_rope(steps, src, v, ss, gain_of, cos, sin, hd, tmp, rope):
            n = v.shape[1]

            def times(out, a, b, op=ALU.mult):
                steps(steps.eng.tensor_tensor(out, a, b, op))
            times(v, v, last(ss, hd))
            for a, b_, g in gain_of:
                times(src[:, a:b_, :], src[:, a:b_, :], mid(g, b_ - a))
            if not rope:
                return
            hf = hd // 2
            x1, x2 = v[:, :, 0:hf], v[:, :, hf:hd]
            t1 = tmp[:, 0:n * hf].rearrange("p (h e) -> p h e", e=hf)
            t2 = tmp[:, n * hf:2 * n * hf].rearrange("p (h e) -> p h e", e=hf)
            c, s = mid(cos, n), mid(sin, n)
            times(t1, x1, s)
            times(t2, x2, s)
            times(x1, x1, c)
            times(x2, x2, c)
            times(x1, x1, t2, ALU.subtract)
            times(x2, x2, t1, ALU.add)

        def norm_act(n):
            ss = small[:, 16:16 + n]
            dve_to_act.wait(act)
            A(act.activation(ss, ss, ACT.Ln))
            A(act.activation(ss, ss, ACT.Exp, scale=-0.5))
            tell(A, act_to_dve)

        def transposed_dve(dst, tiles, heads):
            for h in heads:
                b = dve_banks.take(dve)
                hd = dst(h).shape[0]
                V(dve.tensor_copy(dst(h), b[0:hd, 0:P * len(tiles)]), dve_banks.freed)

        def transposed_pe(src, tiles, heads):
            for h in heads:
                b = dve_banks.claim(pe)
                for k, t in enumerate(tiles):
                    s = src(h, t)
                    ins = pe.transpose(b[0:s.shape[1], P * k:P * k + P], s, ident)
                full(dve_banks, ins)

        extra_of_layer = (8, 4)
        results_of_layer = [nc.dram_tensor(f"results{i}", [(NEXP + m) * P, D], F32, kind="Internal").ap()
                            for i, m in enumerate(extra_of_layer)]

        def conv_stage():
            work = Space(WORK, WORK1)
            bT = work.take(HC, 512)
            qkv = work.take(4, 12, HD)
            pad = TAPS // 2
            cpad = work.take(HC, 2, SEQ + 2 * pad)
            acc = work.take(HC, 512)
            sq = work.take(HC, 512)
            e = work.take(2, 512)
            w = d["w_in_ab"][0]
            ps = [add_panel(krows(w, 768 + 512 * k, 1280 + 512 * k), KC, 512) for k in range(2)]
            pq = [add_panel(krows(w, 0, 512), KC, 512), add_panel(krows(w, 512, 768), KC, 256)]
            cw = col("conv_w", HC, TAPS)
            head_ss = small[:, 48:88]
            zero = work.take(256)

            def sp_part():
                for n in ps + pq:
                    load_panel(n)

            def pe_part():
                value, gate = open_panel(pe, ps[0]), open_panel(pe, ps[1])
                for j in range(HC):
                    for w_, banks in ((value, dve_banks), (gate, act_banks)):
                        b = banks.claim(pe)
                        for c in range(KC):
                            ins = mm(b[:, :], w_[:, c, P * j:P * j + P], hT[:, c, :], c == 0, c == KC - 1)
                        full(banks, ins)
                for n in ps:
                    pe_used(n)
                rows_of_panel(pq[0], range(4), 512, ht, act_banks)
                rows_of_panel(pq[1], range(4), 256, ht, act_banks)
                for src in (acc, sq):
                    dve_to_pe.wait(pe)
                    b = dve_banks.claim(pe)
                    for j in range(HC):
                        ins = mm(b[:, :], ones, src[:, j, :], j == 0, j == HC - 1)
                    full(dve_banks, ins)

            def dve_part():
                V(dve.memset(cpad, 0.0))
                for j in range(HC):
                    act_to_dve.wait(dve)
                    if j == 0:
                        V(dve.memset(zero, 0.0))
                        tell(V, dve_to_act)
                    b = dve_banks.take(dve)
                    V(dve.tensor_tensor(cpad[:, j, :, pad:pad + SEQ], b[:, :].rearrange("p (s t) -> p s t", s=2),
                                        e[:, j % 2].rearrange("p (s t) -> p s t", s=2), ALU.mult), dve_banks.freed)
                    tell(V, dve_to_act)
                tell(V, dve_to_pool)
                done = {}
                for k in range(TAPS):
                    for j in range(HC - 1 if k < POOL_TAPS else HC):
                        src = cpad[:, j, :, k:k + SEQ]
                        o = (acc[:, j, :] if j < HC - 1 else sq[:, 2, :]).rearrange("p (s t) -> p s t", s=2)
                        if j in done:
                            dve.wait_ge(V.order.sem, done[j])
                            ins = stt(o, src, cw[:, j, k:k + 1], o)
                        elif j < HC - 1:
                            ins = dve.tensor_scalar(o, src, cw[:, j, 0:1], col("conv_b")[:, j:j + 1], ALU.mult, ALU.add)
                        else:
                            ins = dve.tensor_scalar(o, src, cw[:, j, k:k + 1], None, ALU.mult)
                        ins.then_inc(V.order.sem, 1)
                        V.order.sent += 1
                        done[j] = V.order.sent
                dve.wait_ge(V.order.sem, V.order.sent)
                pool_to_dve.wait(dve)
                V(dve.tensor_tensor(acc[:, HC - 1, :], acc[:, HC - 1, :], sq[:, 2, :], ALU.add))
                tell(V, dve_to_pe)
                b = dve_banks.take(dve)
                V(stt(acc, mid(b[:, :], HC), -1.0 / HALF, acc), dve_banks.freed)
                V(dve.tensor_tensor(sq, acc, acc, ALU.mult))
                tell(V, dve_to_pe)
                b = dve_banks.take(dve)
                V(dve.tensor_scalar(e[:, 0, :], b[:, :], 1.0 / HALF, EPS, ALU.mult, ALU.add), dve_banks.freed)
                ask_act()
                for j in range(HC):
                    V(dve.tensor_tensor(acc[:, j, :], acc[:, j, :], e[:, 0, :], ALU.mult))
                    tell(V, dve_to_act)
                for j in range(HC + 1):
                    act_to_dve.wait(dve)

            def act_part():
                for j in range(HC):
                    b = act_banks.take(act)
                    if j >= 2:
                        dve_to_act.wait(act)
                    A(act.activation(e[:, j % 2], b[:, :], ACT.Sigmoid), act_banks.freed)
                    tell(A, act_to_dve)
                    if j == 0:
                        dve_to_act.wait(act)
                        for res, more in zip(results_of_layer, extra_of_layer):
                            for h in range(D // 256):
                                act.dma_start(res[NEXP * P:(NEXP + more) * P, 256 * h:256 * h + 256]
                                              .rearrange("(m p) n -> p m n", p=P), mid(zero, more))\
                                    .then_inc(results_zeroed.sem, 16)
                                results_zeroed.sent += 16
                for t in range(4):
                    b = act_banks.take(act)
                    A(act.activation(qkv[:, t, 0:8, :].rearrange("p h e -> p (h e)"), b[:, :], ACT.Copy), act_banks.freed)
                for t in range(4):
                    b = act_banks.take(act)
                    A(act.activation(qkv[:, t, 8:12, :].rearrange("p h e -> p (h e)"), b[:, 0:256], ACT.Copy), act_banks.freed)
                for t in range(4):
                    ss = head_ss[:, 10 * t:10 * t + 10]
                    for h in range(10):
                        ins = act.activation(view(HT + HD * h, HD), qkv[:, t, h, :], ACT.Square, accum_out=ss[:, h:h + 1])
                        if h == 9:
                            A(ins)
                    A(act.activation(ss, ss, ACT.Ln, bias=const("eps"), scale=1.0 / HD))
                    A(act.activation(ss, ss, ACT.Exp, scale=-0.5))
                    tell(A, act_to_pool)
                for _ in range(2):
                    dve_to_act.wait(act)
                rsqrt_act(e[:, 0, :])
                for j in range(HC):
                    dve_to_act.wait(act)
                    A(act.activation(bT[:, j, :], acc[:, j, :], ACT.Silu, bias=col("conv_lb")[:, j:j + 1],
                                     scale=col("conv_g")[:, j:j + 1]))
                    tell(A, act_to_dve)
                act.wait_ge(results_zeroed.sem, results_zeroed.sent)
                tell(A, act_to_dve)
            def pool_part():
                dve_to_pool.wait(pool)
                j = HC - 1
                o = acc[:, j, :].rearrange("p (s t) -> p s t", s=2)
                G(pool.tensor_scalar(o, cpad[:, j, :, 0:SEQ], cw[:, j, 0:1], col("conv_b")[:, j:j + 1], ALU.mult, ALU.add))
                for k in range(1, POOL_TAPS):
                    term = sq[:, k % 2, :].rearrange("p (s t) -> p s t", s=2)
                    G(pool.tensor_scalar(term, cpad[:, j, :, k:k + SEQ], cw[:, j, k:k + 1], None, ALU.mult))
                    G(pool.tensor_tensor(o, o, term, ALU.add))
                tell(G, pool_to_dve)
                for t in range(4):
                    act_to_pool.wait(pool)
                    gain_rope(G, qkv[:, t], qkv[:, t, 0:10, :], head_ss[:, 10 * t:10 * t + 10],
                              [(0, 8, row("qa")), (8, 10, row("ka"))], const("cos", 4, 32)[:, t],
                              const("sin", 4, 32)[:, t], HD, view(HT + 1024, 1024), t >= 2)
                tell(G, pool_to_pe)
            return dict(sp=sp_part, pe=pe_part, dve=dve_part, act=act_part, pool=pool_part), bT

        def attention_stage(i, w, w_out, other_T, tiles_q, names, windowed):
            work = Space(WORK + 2048, WORK1 - 2048)
            qkv = work.take(4, 12, HD)
            qT, kT = work.take(4, 512), work.take(2, 512)
            o = work.take(4, 512) if not windowed else work.take(2, 512)
            s_sb = work.take(3, 512) if windowed else None
            p_sb, pT = work.take(2, 512), work.take(2, 512)
            band = view(HT, 4096)
            oT = qkv.rearrange("p a b c -> p (a b c)")[:, 0:2048].rearrange("p (c t) -> p c t", c=HC)
            tmp = view(WORK + WORK1 - 2048, 2048)
            ps = [add_panel(krows(w, 512, 768), KC, 256), add_panel(krows(w, 0, 512), KC, 512)] if windowed else []
            x0 = tiles_q[0]
            outs = [add_panel(krows(w_out, 512 * k, 512 * k + 512), KC, 512) for k in range(2)]
            gq, gk = row(names[0]), row(names[1])
            cos, sin = const("cos", 4, 32), const("sin", 4, 32)
            units = [[(4 * g + h, t, 4 if t >= 2 else 2) for h in range(4) for t in tiles_q] for g in range(2)]
            mask = view(HT, NX, 512)
            atts = [attention(units[g], HD,
                              lambda h, t: qT[0:HD, h % 4, P * t:P * t + P],
                              lambda h, nk: kT[0:HD, h // 4, 0:P * nk],
                              lambda h, j: qkv[:, j, 10 + h // 4, :],
                              lambda h, t: o[:, t - x0, HD * h:HD * h + HD],
                              HD ** -0.5,
                              (lambda t, nk: mask[:, t - 2, :]) if windowed else None,
                              (lambda h: row("sink")[:, h:h + 1]) if windowed else None,
                              dict(s=s_sb, p=p_sb, pT=pT)) for g in range(2)]

            def sp_part():
                for n in ps:
                    load_panel(n)
                if windowed:
                    dve_to_sp.wait(sp)
                    o_, w_ = TABLES["band"]
                    load_table("band", (mask.rearrange("p a b -> p (a b)"), d["tables"][:, o_:o_ + w_]))
                for n in outs:
                    load_panel(n)

            def pe_part():
                if windowed:
                    rows_of_panel(ps[0], range(4), 256, ht)
                    rows_of_panel(ps[1], tiles_q, 512, ht)
                else:
                    pool_to_pe.wait(pe)
                dve_to_pe.wait(pe)
                transposed_pe(lambda h, t: qkv[:, t, 8 + h, :], range(4), range(2))
                for g in range(2):
                    transposed_pe(lambda h, t: qkv[:, t, 4 * g + h, :], tiles_q, range(4))
                    dve_banks.settled(pe)
                    atts[g]["pe"]()
                for t in tiles_q:
                    b = dve_banks.claim(pe)
                    for c in range(HC):
                        ins = pe.transpose(b[:, P * c:P * c + P], o[:, t - x0, P * c:P * c + P], ident)
                    full(dve_banks, ins)
                dve_banks.settled(pe)
                for n in outs:
                    rows_of_panel(n, tiles_q, 512,
                                  lambda c, t: oT[:, c, P * t:P * t + P] if c < HC else other_T(c - HC, t))

            def dve_part():
                if windowed:
                    for t in range(4):
                        b = dve_banks.take(dve)
                        V(dve.tensor_copy(qkv[:, t, 8:12, :].rearrange("p h e -> p (h e)"), b[:, 0:256]), dve_banks.freed)
                    for t in range(4):
                        head_norm_rope(qkv[:, t], range(8, 10), [(8, 10, gk)], cos[:, t], sin[:, t], HD, tmp, rope=t >= 2)
                    for t in tiles_q:
                        b = dve_banks.take(dve)
                        V(dve.tensor_copy(qkv[:, t, 0:8, :].rearrange("p h e -> p (h e)"), b[:, :]), dve_banks.freed)
                        head_norm_rope(qkv[:, t], range(8), [(0, 8, gq)], cos[:, t], sin[:, t], HD, tmp, rope=t >= 2)
                    tell(V, dve_to_sp)
                tell(V, dve_to_pe)
                if windowed:
                    table_in(dve, "band")
                transposed_dve(lambda h: kT[0:HD, h, :], range(4), range(2))
                for g in range(2):
                    q0 = P * tiles_q[0]
                    transposed_dve(lambda h: qT[0:HD, h, q0:512], tiles_q, range(4))
                    atts[g]["dve"]()
                for t in tiles_q:
                    b = dve_banks.take(dve)
                    V(dve.tensor_copy(oT[:, :, P * t:P * t + P], b[:, :].rearrange("p (c t) -> p c t", c=HC)),
                      dve_banks.freed)
                residual_dve(tiles_q, lambda t: gates[:, t // 2, :])

            def act_part():
                for n in (2, 2, 2, 2, 8, 8) if windowed else ():
                    norm_act(n)
                for g in range(2):
                    atts[g]["act"]()
            return dict(sp=sp_part, pe=pe_part, dve=dve_part, act=act_part)

        def pool_stage():
            work = Space(WORK, WORK1)
            yT = work.take(HC, 256)
            pw = work.take(HC, P)
            u = view(WORK + 2048, NX, 512)
            table = view(WORK + 3072, NX, 4, SEQ)
            pT = view(WORK + 5120, HC, 256)
            pn = add_panel(krows(d["w_in_cd"][0], 768, 1280), KC, 512)

            def sp_part():
                dve_to_sp.wait(sp)
                o_, w_ = TABLES["pool"]
                load_table("pool", (table.rearrange("p a b c -> p (a b c)"), d["tables"][:, o_:o_ + w_]),
                           (pw, d["pool_w"][0].rearrange("g c e -> c g e")))
                load_panel(pn)

            def pe_part():
                rows_of_panel(pn, (2, 3), 512, ht)
                table_in(pe, "pool")
                dve_banks.settled(pe)
                for g in range(4):
                    b = dve_banks.claim(pe)
                    for k in range(NX):
                        ins = mm(b[:, 0:SEQ], u[:, k, P * g:P * g + P], table[:, k, g, :], k == 0, k == NX - 1)
                    full(dve_banks, ins)
                dve_banks.settled(pe)
                for g in range(4):
                    b = dve_banks.claim(pe)
                    full(dve_banks, mm(b[:, 0:SEQ], pw[:, g, :], pT[:, g, :], True, True))
                dve_banks.settled(pe)

            def dve_part():
                tell(V, dve_to_sp)
                for t in range(NX):
                    b = dve_banks.take(dve)
                    V(dve.tensor_copy(u[:, t, :], b[:, :]), dve_banks.freed)
                for g in range(4):
                    b = dve_banks.take(dve)
                    V(dve.tensor_copy(pT[:, g, :], b[:, 0:SEQ]), dve_banks.freed)
                for g in range(4):
                    b = dve_banks.take(dve)
                    V(dve.tensor_scalar(yT[:, g, :], b[:, 0:SEQ], col("pool_scale")[:, g:g + 1], None, ALU.mult),
                      dve_banks.freed)
            return dict(sp=sp_part, pe=pe_part, dve=dve_part), yT

        rows_back = {}

        def moe_stage(i, tiles):
            nt, t0 = len(tiles), tiles[0]
            extra_max = 2 * nt
            assert extra_max == extra_of_layer[i]
            blocks_max = NEXP + extra_max
            NR = NGRP + NEXP
            work = Space(WORK, WORK1)
            rt_w = work.take(KC, NR)
            logit = work.take(nt, NR)
            gpad, gtop = work.take(nt, 8), work.take(nt, 8)
            etop = work.take(nt, 8)
            picks = work.take(nt, 2)
            gidx = work.take(nt)
            one_hot = work.take(2, nt, NEXP)
            both = work.take(nt, NEXP)
            place = work.take(nt, NEXP + 0)
            prod = work.take(2, nt, NEXP)
            pos, slot, over = work.take(2, nt), work.take(2, nt), work.take(2, nt)
            gsum, ratio, wt = work.take(nt), work.take(nt), work.take(2, nt)
            counts, extra, ends, starts = (work.take(NEXP) for _ in range(4))
            past = work.take(extra_max, NEXP)
            experts_f, nb_f, tmp1 = work.take(NEXP + 8), work.take(1), work.take(1)
            over_base = work.take(2, nt)
            xg, xgT = work.take(2, D), work.take(2, KC, P)
            hid, hidT = work.take(2, DE), work.take(2, DE // P, P)
            ex, y = work.take(2, DE), work.take(2, D)
            h_row = view(work.off - 9216, nt, D)
            yg = view(work.off - 9216, 4, D)
            comb = view(work.off - 9216 + 4096, D)
            NB = 16
            experts_i = expert_ids[:, 0:blocks_max]
            slot_i, token_i = bigi[:, 0:2 * nt], bigi[:, 8:12]
            list_i = [bigi[:, 12 + s:13 + s] for s in range(2)]
            index_u = ibuf
            lists = nc.dram_tensor(f"lists{i}", [blocks_max * P, 1], I32, kind="Internal").ap()
            h_dram = nc.dram_tensor(f"h_rows{i}", [nt * P, D], F32, kind="Internal").ap()
            results = results_of_layer[i]
            owners = dict(slot_owner)
            ring["next"], ring["moe"] = 0, i + 1
            slot_owner.clear()

            def sem(name):
                return ctx.enter_context(nc.semaphore(f"moe{i}_{name}"))
            w_full = [sem(f"weights_full{k}") for k in range(6)]
            list_full, xg_full = [sem("list0"), sem("list1")], [sem("rows0"), sem("rows1")]
            y_out = [sem("y_out0"), sem("y_out1")]
            lists_ready, h_written, y_back = sem("lists_ready"), sem("h_written"), sem("y_back")
            xT_ps, xT_sb = sem("xT_in_psum"), sem("xT_in_sbuf")
            g_ps, u_ps = sem("gate_in_psum"), sem("up_in_psum")
            e_sb, hid_sb = sem("silu_ready"), sem("hid_ready")
            h_ps, hT_sb, d_ps, y_sb = sem("hidT_in_psum"), sem("hidT_in_sbuf"), sem("down_in_psum"), sem("y_in_sbuf")
            wg = d["ex_gate"][i].rearrange("e (c p) n -> e p c n", p=P)
            wu = d["ex_up"][i].rearrange("e (c p) n -> e p c n", p=P)
            wd = d["ex_down"][i].rearrange("e (c p) n -> e p c n", p=P)
            wbuf = [[view(RING + (3 * s + k) * PANEL, *((KC, DE) if k < 2 else (DE // P, D))) for k in range(3)]
                    for s in range(2)]

            def n_blocks(eng):
                more = eng.value_load(bigi[0:1, NB:NB + 1], min_val=0, max_val=extra_max)
                return eng.snap(more + NEXP, min_val=NEXP, max_val=blocks_max)

            def sp_part():
                dve_to_sp.wait(sp)
                load_table(f"router{i}", (rt_w, krows(d["rt_w"][i])))
                for b in range(2):
                    for k, w in enumerate((wg, wu, wd)):
                        if 3 * b + k in owners:
                            sp.wait_ge(panel_used.sem, owners[3 * b + k] + 1)
                        if i:
                            sp.wait_ge(pe_done.sem, i)
                        sp.dma_start(wbuf[b][k], w[b]).then_inc(w_full[3 * b + k], 16)
                dve_to_sp.wait(sp)
                sp.dma_start(h_dram.rearrange("(t p) n -> p t n", p=P), h_row).then_inc(h_written, 16)
                dve_to_sp.wait(sp)
                nb = n_blocks(sp)
                with sp.Fori(2, nb, 2) as b:
                    for s in range(2):
                        e = sp.value_load(expert_ids[0:1, bass.ds((b + s).with_bounds(min_val=0, max_val=blocks_max - 1), 1)],
                                          min_val=0, max_val=NEXP - 1)
                        for k, (w, free) in enumerate(((wg, g_ps), (wu, u_ps), (wd, d_ps))):
                            sp.wait_ge(free, b + s - 1)
                            sp.dma_start(wbuf[s][k], w[bass.ds(e, 1)].rearrange("e p c n -> (e p) c n"))\
                                .then_inc(w_full[3 * s + k], 16)
                act_to_sp.wait(sp)
                if i:
                    sp.wait_ge(y_back, 32 * nt)

            def pool_part():
                if i == 0:
                    G(pool.memset(zeros_i, 0))
                pool.dma_start(lists.rearrange("(p a) o -> p (a o)", p=P), zeros_i[:, 0:blocks_max]).then_inc(lists_ready, 16)
                pool.wait_ge(lists_ready, 16)
                dve_to_pool.wait(pool)
                for k in range(nt):
                    for j in range(2):
                        c = j * nt + k
                        pool.indirect_dma_start(out=lists, out_offset=bass.IndirectOffsetOnAxis(ap=slot_i[:, c:c + 1], axis=0),
                                                in_=token_i[:, k:k + 1], in_offset=None).then_inc(lists_ready, 16)
                pool.wait_ge(lists_ready, 16 * (1 + 2 * nt))
                pool.wait_ge(h_written, 16)
                dve_to_pool.wait(pool)
                nb = n_blocks(pool)
                lists_b = lists.rearrange("(b p) o -> b p o", p=P)

                def fetch(b, s, free):
                    if free is not None:
                        pool.wait_ge(xT_ps, free)
                        pool.sem_inc(pool_passed, 1)
                    pool.dma_start(list_i[s], lists_b[bass.ds(b, 1)].rearrange("b p o -> (b p) o"))\
                        .then_inc(list_full[s], 16)
                    pool.wait_ge(list_full[s], (b - s) * 8 + 16)
                    if free is not None:
                        pool.sem_inc(pool_passed, 1)
                    pool.indirect_dma_start(out=xg[:, s, :], out_offset=None, in_=h_dram,
                                            in_offset=bass.IndirectOffsetOnAxis(ap=list_i[s], axis=0))\
                        .then_inc(xg_full[s], 16)
                for s in range(2):
                    fetch(s, s, None)
                with pool.Fori(2, nb, 2) as b:
                    for s in range(2):
                        fetch((b + s).with_bounds(min_val=2, max_val=blocks_max - 1), s, b + s - 1)
                act_to_pool.wait(pool)
                for k in range(nt):
                    if k >= 2:
                        dve_to_pool.wait(pool)
                    for j in range(2):
                        c = j * nt + k
                        pool.indirect_dma_start(out=yg[:, 2 * (k % 2) + j, :], out_offset=None, in_=results,
                                                in_offset=bass.IndirectOffsetOnAxis(ap=slot_i[:, c:c + 1], axis=0))\
                            .then_inc(y_back, 16)
                    pool.wait_ge(y_back, 32 * (k + 1))
                    tell(G, pool_to_dve)

            def pe_part():
                dve_banks.settled(pe)
                table_in(pe, f"router{i}")
                for k in range(nt):
                    b = dve_banks.claim(pe)
                    for c in range(KC):
                        ins = mm(b[:, 0:NR], hT[:, c, P * k:P * k + P], rt_w[:, c, :], c == 0, c == KC - 1)
                    full(dve_banks, ins)
                for k in range(nt):
                    for h in range(2):
                        b = dve_banks.claim(pe)
                        for j in range(4):
                            ins = pe.transpose(b[:, P * j:P * j + P], hT[:, 4 * h + j, P * k:P * k + P], ident)
                        full(dve_banks, ins)
                dve_to_pe.wait(pe)
                b = dve_banks.claim(pe)
                for k in range(nt):
                    for m in range(k + 1):
                        mm(b[:, NEXP * k:NEXP * k + NEXP], const("before") if m == k else ones, both[:, m, :],
                           m == 0, m == k)
                for k in range(nt):
                    ins = mm(b[:, NEXP * nt:NEXP * nt + NEXP], ones, both[:, k, :], k == 0, k == nt - 1)
                full(dve_banks, ins)
                dve_to_pe.wait(pe)
                nb = n_blocks(pe)

                def xT(b, s):
                    pe.wait_ge(xg_full[s], (b - s) * 8 + 16)
                    if not (isinstance(b, int) and b == 0):
                        pe.wait_ge(xT_sb, b * 2)
                    for c in range(KC):
                        ins = pe.transpose(psum[2 + c // 4][:, P * (c % 4):P * (c % 4) + P],
                                           xg[:, s, P * c:P * c + P], ident)
                    ins.then_inc(xT_ps, 1)

                def gate_up(b, s, k):
                    if k == 0:
                        pe.wait_ge(xT_sb, b * 2 + 2)
                    pe.wait_ge(w_full[3 * s + k], (b - s) * 8 + 16)
                    if not (isinstance(b, int) and b == 0):
                        pe.wait_ge((e_sb, hid_sb)[k], b)
                    for c in range(KC):
                        ins = mm(psum[k][:, :], xgT[:, s, c, :], wbuf[s][k][:, c, :], c == 0, c == KC - 1)
                    ins.then_inc((g_ps, u_ps)[k], 1)

                def hidT_of(b, s):
                    pe.wait_ge(hid_sb, b + 1)
                    if not (isinstance(b, int) and b == 0):
                        pe.wait_ge(hT_sb, b)
                    for c in range(DE // P):
                        ins = pe.transpose(psum[4][:, P * c:P * c + P], hid[:, s, P * c:P * c + P], ident)
                    ins.then_inc(h_ps, 1)

                def down(b, s):
                    pe.wait_ge(hT_sb, b + 1)
                    pe.wait_ge(w_full[3 * s + 2], (b - s) * 8 + 16)
                    if not (isinstance(b, int) and b == 0):
                        pe.wait_ge(y_sb, b * 2)
                    for h in range(2):
                        for c in range(DE // P):
                            ins = mm(psum[5 + h][:, :], hidT[:, s, c, :], wbuf[s][2][:, c, 512 * h:512 * h + 512],
                                     c == 0, c == DE // P - 1)
                    ins.then_inc(d_ps, 1)

                def whole(b, s, ahead):
                    gate_up(b, s, 0)
                    hidT_of(b - 1, 1 - s)
                    gate_up(b, s, 1)
                    if ahead:
                        xT(b + 1, 1 - s)
                    down(b - 1, 1 - s)

                xT(0, 0)
                gate_up(0, 0, 0)
                gate_up(0, 0, 1)
                xT(1, 1)
                with pe.Fori(1, nb - 1, 2) as b:
                    whole(b, 1, True)
                    whole(b + 1, 0, True)
                whole(nb - 1, 1, False)
                hidT_of(nb - 1, 1)
                down(nb - 1, 1)
                mm(psum[7][0:2, 0:2], ident[0:2, 0:2], ident[0:2, 0:2], True, True).then_inc(pe_done.sem, 1)

            def dve_part():
                tell(V, dve_to_sp)
                for k in range(nt):
                    b = dve_banks.take(dve)
                    V(dve.tensor_tensor(logit[:, k, :], b[:, 0:NR], row(f"rtb_{i}"), ALU.add), dve_banks.freed)
                V(dve.memset(gpad, -BIG))
                V(dve.tensor_copy(gpad[:, :, 0:NGRP], logit[:, :, 0:NGRP]))
                for k in range(nt):
                    V(dve.max(gtop[:, k, :], gpad[:, k, :]))
                    V(dve.max_index(index_u[:, 0:8], gtop[:, k, :], gpad[:, k, :]))
                    V(dve.tensor_copy(gidx[:, k:k + 1], index_u[:, 0:1]))
                V(dve.tensor_tensor(gpad, gpad, last(gtop[:, :, 0], 8), ALU.subtract))
                ask_act()
                V(dve.tensor_reduce(gsum, gpad, AX.X, ALU.add))
                V(dve.reciprocal(gsum, gsum))
                V(dve.tensor_tensor(both, mid(const("group"), nt), last(gidx, NEXP), ALU.is_equal))
                V(dve.tensor_scalar(both, both, 1.0, BIG, ALU.subtract, ALU.mult))
                V(dve.tensor_tensor(both, both, logit[:, :, NGRP:NR], ALU.add))
                for k in range(nt):
                    V(dve.max(etop[:, k, :], both[:, k, :]))
                    V(dve.max_index(index_u[:, 0:8], etop[:, k, :], both[:, k, :]))
                    V(dve.tensor_copy(picks[:, k, :], index_u[:, 0:2]))
                for j in range(2):
                    V(dve.tensor_tensor(one_hot[:, j], mid(const("expert"), nt), last(picks[:, :, j], NEXP), ALU.is_equal))
                V(dve.tensor_tensor(both, one_hot[:, 0], one_hot[:, 1], ALU.add))
                V(dve.tensor_tensor(ratio, etop[:, :, 1], etop[:, :, 0], ALU.subtract))
                ask_act()
                V(dve.tensor_scalar(wt[:, 0], ratio, 1.0, None, ALU.add))
                V(dve.reciprocal(wt[:, 0], wt[:, 0]))
                V(dve.tensor_tensor(wt[:, 0], wt[:, 0], gsum, ALU.mult))
                V(dve.tensor_tensor(wt[:, 1], wt[:, 0], ratio, ALU.mult))
                for k in range(nt):
                    for h in range(2):
                        b = dve_banks.take(dve)
                        V(dve.tensor_copy(h_row[:, k, 512 * h:512 * h + 512], b[:, :]), dve_banks.freed)
                tell(V, dve_to_sp)
                tell(V, dve_to_pe)
                b = dve_banks.take(dve)
                for j in range(2):
                    V(dve.tensor_tensor(prod[:, j], one_hot[:, j],
                                        b[:, 0:NEXP * nt].rearrange("p (k e) -> p k e", e=NEXP), ALU.mult))
                V(dve.tensor_copy(counts, b[:, NEXP * nt:NEXP * nt + NEXP]), dve_banks.freed)
                V(dve.tensor_scalar(extra, counts, float(P), None, ALU.is_gt))
                for m in range(2, nt):
                    V(stt(extra, counts, float(P * m), extra, ALU.is_gt, ALU.add))
                V(dve.tensor_tensor_scan(ends, ones[:, 0:NEXP], extra, 0.0, ALU.mult, ALU.add))
                V(dve.tensor_tensor(starts, ends, extra, ALU.subtract))
                for j in range(2):
                    V(dve.tensor_reduce(pos[:, j], prod[:, j], AX.X, ALU.add))
                for j in range(2):
                    V(dve.tensor_tensor(prod[:, j], one_hot[:, j], mid(starts, nt), ALU.mult))
                    V(dve.tensor_reduce(over_base[:, j], prod[:, j], AX.X, ALU.add))
                    V(dve.tensor_tensor(over_base[:, j], over_base[:, j], picks[:, :, j], ALU.subtract))
                    V(stt(slot[:, j], picks[:, :, j], float(P), pos[:, j]))
                V(dve.tensor_scalar(over_base, over_base, float(P), float((NEXP - 1) * P), ALU.mult, ALU.add))
                V(dve.tensor_scalar(over, pos, float(P), None, ALU.is_ge))
                V(dve.tensor_tensor(over, over, over_base, ALU.mult))
                V(dve.tensor_tensor(slot, slot, over, ALU.add))
                V(dve.tensor_copy(token_i, const("token")))
                V(dve.tensor_copy(slot_i, slot.rearrange("p a b -> p (a b)")))
                tell(V, dve_to_pool)
                V(dve.tensor_tensor(past, mid(ends, extra_max), last(const("expert")[:, 0:extra_max], NEXP), ALU.is_le))
                V(dve.tensor_copy(experts_f[:, 0:NEXP], const("expert")))
                V(dve.tensor_reduce(experts_f[:, NEXP:NEXP + extra_max], past, AX.X, ALU.add))
                V(dve.tensor_scalar(experts_f[:, NEXP:blocks_max], experts_f[:, NEXP:blocks_max], float(NEXP - 1), None, ALU.min))
                V(dve.tensor_copy(experts_i, experts_f[:, 0:blocks_max]))
                V(dve.memset(nb_f, 0.0))
                for m in range(nt):
                    V(dve.tensor_scalar(tmp1, ends[:, NEXP - 1:NEXP], float(2 * m), 2.0, ALU.is_gt, ALU.mult))
                    V(dve.tensor_tensor(nb_f, nb_f, tmp1, ALU.add))
                V(dve.tensor_copy(bigi[:, NB:NB + 1], nb_f))
                tell(V, dve_to_pool)
                tell(V, dve_to_sp)
                tell(V, dve_to_pe)
                tell(V, dve_to_act)
                nb = n_blocks(dve)

                def rows_in(b, s, reuse=True):
                    dve.wait_ge(xT_ps, b + 1)
                    if reuse:
                        dve.wait_ge(u_ps, b - 1)
                    for h in range(2):
                        dve.tensor_copy(xgT[:, s, 4 * h:4 * h + 4, :].rearrange("p c t -> p (c t)"), psum[2 + h][:, :])\
                            .then_inc(xT_sb, 1)

                def hidden(b, s, reuse=True):
                    dve.wait_ge(e_sb, b + 1)
                    dve.wait_ge(u_ps, b + 1)
                    if reuse:
                        dve.wait_ge(h_ps, b - 1)
                    dve.tensor_tensor(hid[:, s, :], ex[:, s, :], psum[1][:, :], ALU.mult).then_inc(hid_sb, 1)

                def hidT_in(b, s, reuse=True):
                    dve.wait_ge(h_ps, b + 1)
                    if reuse:
                        dve.wait_ge(d_ps, b - 1)
                    dve.tensor_copy(hidT[:, s].rearrange("p c t -> p (c t)"), psum[4][:, :]).then_inc(hT_sb, 1)

                dve.wait_ge(h_written, 16)
                rows_in(0, 0, False)
                hidden(0, 0, False)
                rows_in(1, 1, False)
                hidT_in(0, 0, False)
                hidden(1, 1, False)
                rows_in(2, 0)
                hidT_in(1, 1, False)
                hidden(2, 0)
                rows_in(3, 1)
                with dve.Fori(3, nb - 1, 2) as b:
                    hidT_in(b - 1, 0)
                    hidden(b, 1)
                    rows_in(b + 1, 0)
                    hidT_in(b, 1)
                    hidden(b + 1, 0)
                    rows_in(b + 2, 1)
                hidT_in(nb - 2, 0)
                hidden(nb - 1, 1)
                hidT_in(nb - 1, 1)
                for k in range(nt):
                    pool_to_dve.wait(dve)
                    t = tiles[k]
                    V(dve.tensor_scalar(comb, yg[:, 2 * (k % 2), :], wt[:, 0, k:k + 1], None, ALU.mult))
                    V(stt(comb, yg[:, 2 * (k % 2) + 1, :], wt[:, 1, k:k + 1], comb))
                    if k + 2 < nt:
                        tell(V, dve_to_pool)
                    V(dve.tensor_tensor(comb, comb, gates[:, 2 + t // 2, :], ALU.mult))
                    V(dve.tensor_tensor(x[:, t, :], x[:, t, :], comb, ALU.add))

            def act_part():
                exp_of(gpad, gpad)
                exp_of(ratio, ratio)
                dve_to_act.wait(act)
                nb = n_blocks(act)

                def silus(b, s, reuse=True):
                    act.wait_ge(g_ps, b + 1)
                    if reuse:
                        act.wait_ge(hid_sb, b - 1)
                    act.activation(ex[:, s, :], psum[0][:, :], ACT.Silu).then_inc(e_sb, 1)

                def results_out(b, s, reuse=True):
                    act.wait_ge(d_ps, b + 1)
                    if reuse:
                        act.wait_ge(y_out[s], (b - s) * 8)
                    for h in range(2):
                        act.activation(y[:, s, 512 * h:512 * h + 512], psum[5 + h][:, :], ACT.Copy).then_inc(y_sb, 1)
                    act.wait_ge(y_sb, b * 2 + 2)
                    act.dma_start(results.rearrange("(b p) n -> b p n", p=P)[bass.ds(b, 1)].rearrange("b p n -> (b p) n"),
                                  y[:, s, :]).then_inc(y_out[s], 16)

                def bound(b):
                    return b.with_bounds(min_val=0, max_val=blocks_max - 1)
                silus(0, 0, False)
                silus(1, 1, False)
                results_out(0, 0, False)
                silus(2, 0)
                results_out(1, 1, False)
                with act.Fori(3, nb - 1, 2) as b:
                    silus(b, 1)
                    results_out(bound(b - 1), 0)
                    silus(b + 1, 0)
                    results_out(bound(b + 0), 1)
                silus(nb - 1, 1)
                results_out(bound(nb - 2), 0)
                results_out(bound(nb - 1), 1)
                for s in range(2):
                    act.wait_ge(y_out[s], nb * 8)
                A(act.activation(small[:, 120:121], ident[:, 0:1], ACT.Copy))
                tell(A, act_to_pool)
                tell(A, act_to_sp)

            rows_back[i] = (y_back, 32 * nt)
            return dict(sp=sp_part, pe=pe_part, dve=dve_part, act=act_part, pool=pool_part)

        T2 = (2, 3)
        RWKV_U = 2 * PANEL + 2048 + 18432
        AD_RAW = X + 1088
        WORK2 = (2 * PANEL, WORK + WORK1 - 2 * PANEL)

        def rms_rows(v, scale, eps=EPS):
            V(dve.tensor_scalar(v, v, scale, eps, ALU.mult, ALU.add))
            ask_act()

        def rsqrt_act(v):
            dve_to_act.wait(act)
            A(act.activation(v, v, ACT.Ln))
            A(act.activation(v, v, ACT.Exp, scale=-0.5))
            tell(A, act_to_dve)

        def column_sums_pe(weights, src):
            dve_to_pe.wait(pe)
            for k in range(2):
                b = dve_banks.claim(pe)
                full(dve_banks, mm(b[:, :], weights, src[:, 2 * k:2 * k + 2, :].rearrange("p a t -> p (a t)"), True, True))

        def column_sums_dve(use):
            tell(V, dve_to_pe)
            for k in range(2):
                b = dve_banks.take(dve)
                V(use(slice(2 * k, 2 * k + 2), b[:, :].rearrange("p (a t) -> p a t", t=SEQ)), dve_banks.freed)

        def chunks(ap):
            return ap.rearrange("p j (c t) -> p (j c) t", t=CH)

        def hgrn_stage(oT):
            work = Space(WORK2[0] + 2048, WORK2[1] - 2048)
            w = d["w_in_ar_2"][0]
            raw = work.take(3, HC, SEQ)
            e3 = work.take(3, HC, SEQ)
            e4 = work.take(4, HC, SEQ)
            b = work.take(HC, SEQ)
            v_tok = work.take(NX, 512)
            last_b = work.take(HC * SEQ // CH)
            lb3, lb1, keep = work.take(3, HC), work.take(HC), work.take(HC)
            sc, k_tok = work.take(2, P), work.take(2, P)
            v_exp = work.take(2, NCH, P)
            S = work.take(NCH + 1, P)
            ps = [add_panel(krows(w, 512 * n, 512 * n + 512), KC, 512) for n in (0, 1, 3, 2)]
            rwkv_ps = [add_panel(krows(w, 2048 + 512 * n, 2560 + 512 * n), KC, 512) for n in range(3)] + \
                      [add_panel(krows(w, 3584, 3840), KC, 256)]
            assert work.off <= RWKV_U
            ur, step = view(RWKV_U, 14, SEQ), view(RWKV_U + 14 * SEQ, 14, SEQ)
            q, f, gate = raw[:, 0], raw[:, 1], raw[:, 2]
            lf = e3[:, 1]
            q_t, k_t, q_e, k_bar = (e4[:, n] for n in range(4))
            units = [(h, B) for h in range(HC) for B in range(NX)]

            def sp_part():
                for n in ps + rwkv_ps:
                    load_panel(n)

            def pe_part():
                for n in ps[:3]:
                    cols_of_panel(n, HC, SEQ)
                rows_of_panel(ps[3], range(NX), 512, ht)
                for k, n in enumerate(rwkv_ps):
                    cols_of_panel(n, 4 if k < 3 else 2, SEQ, banks=act_banks)
                dve_to_pe.wait(pe)

                def scores(n):
                    h, B = units[n]
                    tok = slice(P * B, P * B + P)
                    bank = dve_banks.claim(pe)
                    mm(bank[:, 0:P], k_t[:, h, tok], q_t[:, h, tok], True, True)
                    full(dve_banks, pe.transpose(bank[:, P:2 * P], k_bar[:, h, tok], ident))
                scores(0)
                for n, (h, B) in enumerate(units):
                    vt = v_tok[:, B, P * h:P * h + P]
                    dve_to_pe.wait(pe)
                    for k in range(2):
                        bank = dve_banks.claim(pe)
                        full(dve_banks, mm(bank[:, :], k_tok[:, n % 2, :],
                                           v_exp[:, n % 2, 4 * k:4 * k + 4, :].rearrange("p c e -> p (c e)"), True, True))
                    states_in = dve_banks.filling
                    if n + 1 < len(units):
                        scores(n + 1)
                    pe.wait_ge(dve_banks.freed.sem, states_in)
                    bank = dve_banks.claim(pe)
                    ins = mm(bank[:, 0:P], vt, sc[:, n % 2, :], True, False)
                    for c in range(NCH):
                        if B or c:
                            ins = mm(bank[:, CH * c:CH * c + CH], S[:, c, :],
                                     q_e[:, h, P * B + CH * c:P * B + CH * c + CH], False, c == NCH - 1)
                    full(dve_banks, ins)
                column_sums_pe(ones, e4[:, 0])

            def dve_part():
                for n in range(3):
                    for j in range(HC):
                        bk = dve_banks.take(dve)
                        V(dve.tensor_copy(raw[:, n, j, :], bk[:, 0:SEQ]), dve_banks.freed)
                ask_act()
                for t in range(NX):
                    bk = dve_banks.take(dve)
                    V(dve.tensor_copy(v_tok[:, t, :], bk[:, :]), dve_banks.freed)
                lb = col("lb", 3, HC)
                V(dve.tensor_tensor(lb1, lb[:, 0], lb[:, 1], ALU.max))
                V(dve.tensor_tensor(lb1, lb1, lb[:, 2], ALU.max))
                V(dve.tensor_tensor(lb3, lb, mid(lb1, 3), ALU.subtract))
                ask_act()
                V(dve.tensor_tensor(lb1, lb3[:, 0], lb3[:, 1], ALU.add))
                V(dve.tensor_tensor(lb1, lb1, lb3[:, 2], ALU.add))
                V(dve.reciprocal(lb1, lb1))
                V(dve.tensor_tensor(lb1, lb1, lb3[:, 0], ALU.mult))
                V(dve.tensor_scalar(keep, lb1, -1.0, 1.0, ALU.mult, ALU.add))
                V(dve.tensor_tensor(q, q, e3[:, 0], ALU.mult))
                V(dve.tensor_tensor(gate, gate, e3[:, 2], ALU.mult))
                for j in range(HC):
                    V(dve.tensor_scalar(f[:, j, :], e3[:, 1, j, :], keep[:, j:j + 1], lb1[:, j:j + 1], ALU.mult, ALU.add))
                ask_act()
                V(dve.tensor_scalar(f, f, -1.0, 1.0, ALU.mult, ALU.add))
                for j in range(HC):
                    V(dve.tensor_tensor_scan(b[:, j, :], const("restart"), lf[:, j, :], 0.0, ALU.mult, ALU.add))
                bc = chunks(b)
                middle = bc[:, :, CH // 2 - 1:CH // 2].broadcast_to([P, HC * SEQ // CH, CH])
                end = bc[:, :, CH - 1:CH].broadcast_to([P, HC * SEQ // CH, CH])
                V(dve.tensor_tensor(chunks(q_t), bc, middle, ALU.subtract))
                V(dve.tensor_scalar(q_t, q_t, 40.0, -40.0, ALU.min, ALU.max))
                V(dve.tensor_tensor(chunks(k_bar), end, bc, ALU.subtract))
                tell(V, dve_to_act)
                for dst, src in ((k_t, f), (q_t, q), (q_e, q), (k_bar, f)):
                    act_to_dve.wait(dve)
                    if dst is q_e:
                        V(dve.tensor_copy(last_b, chunks(q_e)[:, :, CH - 1]))
                    V(dve.tensor_tensor(dst, dst, src, ALU.mult))
                tell(V, dve_to_pe)

                def scores_in(n):
                    h, B = units[n]
                    vt = v_tok[:, B, P * h:P * h + P]
                    V(dve.tensor_tensor(v_exp[:, n % 2], mid(vt, NCH), last(const("chunk_of"), P), ALU.mult))
                    bk = dve_banks.take(dve)
                    V(dve.tensor_tensor(sc[:, n % 2, :], bk[:, 0:P], const("chunk_upto_st"), ALU.mult))
                    V(dve.tensor_copy(k_tok[:, n % 2, :], bk[:, P:2 * P]), dve_banks.freed)
                    tell(V, dve_to_pe)
                scores_in(0)
                for n, (h, B) in enumerate(units):
                    if B:
                        V(dve.tensor_copy(S[:, 0, :], S[:, NCH, :]))
                    for k in range(2):
                        bk = dve_banks.take(dve)
                        for c4 in range(4):
                            c = 4 * k + c4
                            u = bk[:, P * c4:P * c4 + P]
                            s = dve_banks.freed if c4 == 3 else None
                            if B or c:
                                at = h * (SEQ // CH) + B * NCH + c
                                V(stt(S[:, c + 1, :], S[:, c, :], last_b[:, at:at + 1], u), s)
                            else:
                                V(dve.tensor_copy(S[:, 1, :], u), s)
                    if n + 1 < len(units):
                        scores_in(n + 1)
                    bk = dve_banks.take(dve)
                    V(dve.tensor_copy(oT[:, h, P * B:P * B + P], bk[:, 0:P]), dve_banks.freed)
                V(dve.tensor_tensor(e4[:, 0], oT, oT, ALU.mult))
                column_sums_dve(lambda k, bk: dve.tensor_copy(e4[:, 1, k, :], bk))
                rms_rows(e4[:, 1], 1.0 / P)
                V(dve.tensor_tensor(oT, oT, e4[:, 1], ALU.mult))
                for h in range(HC):
                    V(stt(oT[:, h, :], oT[:, h, :], col("onorm")[:, h:h + 1], gate[:, h, :], ALU.mult, ALU.mult))

            def act_part():
                def rwkv_rows(first, end):
                    for j in range(first, end):
                        bk = act_banks.take(act)
                        A(act.activation(ur[:, j, :], bk[:, 0:SEQ], ACT.Copy), act_banks.freed)
                exp_of(e3, raw, func=ACT.Sigmoid)
                exp_of(lb3, lb3)
                rwkv_rows(0, 2)
                exp_of(lf, f, func=ACT.Ln)
                rwkv_rows(2, 7)
                dve_to_act.wait(act)
                for dst, src, sign in ((k_t, q_t, -1.0), (q_t, q_t, 1.0), (q_e, b, 1.0), (k_bar, k_bar, 1.0)):
                    A(act.activation(dst, src, ACT.Exp, scale=sign))
                    tell(A, act_to_dve)
                rwkv_rows(7, 14)
                tell(A, act_to_pool)
                rsqrt_act(e4[:, 1])

            def pool_part():
                act_to_pool.wait(pool)
                G(pool.tensor_tensor(step[:, :, 1:SEQ], ur[:, :, 0:SEQ - 1], ur[:, :, 1:SEQ], ALU.subtract))
                G(pool.tensor_scalar(step[:, :, 0:1], ur[:, :, 0:1], -1.0, None, ALU.mult))
                G(pool.tensor_tensor(step, step, last(col("mu"), SEQ), ALU.mult))
                G(pool.tensor_tensor(ur, ur, step, ALU.add))
                G(pool.tensor_copy(view(AD_RAW, SEQ), ur[:, 12, :]))
                tell(G, pool_to_act)
                tell(G, pool_to_dve)
            return dict(sp=sp_part, pe=pe_part, dve=dve_part, act=act_part, pool=pool_part)

        def rwkv_stage(obT):
            work = Space(WORK2[0] + 2048, WORK2[1] - 2048)
            w = d["w_in_ar_2"][0]
            kept = [work.take(HC, SEQ) for _ in range(9)]
            r_e, kappa, beta, key, beta_end, key_end, v, bonus, g = kept
            mark = work.off
            ur = view(RWKV_U, 14, SEQ)
            za = work.take(2, HC, SEQ)
            kk, k2, b = work.take(HC, SEQ), work.take(HC, SEQ), work.take(HC, SEQ)
            e4 = work.take(4, HC, SEQ)
            assert work.off <= RWKV_U
            lora, lora_g = view(X, 512), view(X + 512, 512)
            el = view(X + 1024, HC, SEQ // CH)
            work.off = mark
            Y1, Y2 = work.take(8, P), work.take(8, P)
            v_tok = work.take(8, 64)
            Z = work.take(8, P)
            GT = work.take(8, NCH, 64)
            S = work.take(NCH + 1, 8, 64)
            spread = work.take(2, 3, NCH, 64)
            ke_tok = work.take(512)
            beta_tok = work.take(512)
            Nt = work.take(4, P)
            DI = work.take(HC, NCH, 64)
            H = view(HT, 8, NCH, 64)
            P0, Pt0 = [work.take(4, P), view(X, 4, P)], [view(X + 512, 4, P), view(X + 1536, 4, P)]
            ad_raw = view(AD_RAW, SEQ)
            e_post = [view(mark, HC, SEQ), view(mark + HC * SEQ, HC, SEQ)]
            R = Nt
            ra, k_raw, v_raw = ur[:, 0:4], ur[:, 4:8], ur[:, 8:12]
            zz, aa = za[:, 0], za[:, 1]

            def head(ap, h, B):
                return ap[64 * (h % 2):64 * (h % 2) + 64, h // 2, P * B:P * B + P]

            def eye(h):
                o = 64 * (h % 2)
                return ident[o:o + 64, o:o + 64]

            def sp_part():
                dve_to_sp.wait(sp)
                load_table("lora", (lora[0:64, :], d["rwkv_w2_2"][0]), (lora[64:P, :], d["rwkv_a2_2"][0]),
                           (lora_g, d["rwkv_g2_2"][0]))

            act_at = [0]

            def pe_part():
                act_at[0] = act_banks.filling
                table_in(pe, "lora")
                column_sums_pe(const("pair_ones"), e4[:, 0])
                act_to_pe.wait(pe)
                for kind in range(3):
                    for j in range(2):
                        bank = dve_banks.claim(pe)
                        for m in range(2):
                            jj = 2 * j + m
                            c = slice(P * jj, P * jj + P)
                            lhs, rhs = ((lora[0:64, c], ur[0:64, 12, :]), (lora[64:P, c], ur[64:P, 12, :]),
                                        (lora_g[:, c], ur[:, 13, :]))[kind]
                            if kind == 1:
                                rhs = ad_raw[64:P, :]
                            ins = mm(bank[:, SEQ * m:SEQ * m + SEQ], lhs, rhs, True, True)
                        full(dve_banks, ins)
                column_sums_pe(const("pair_ones"), e4[:, 0])
                dve_to_pe.wait(pe)
                for B in range(NX):
                    for src in (kappa, key_end, beta_end, v):
                        bank = dve_banks.claim(pe)
                        for m in range(HC):
                            ins = pe.transpose(bank[:, P * m:P * m + P], src[:, m, P * B:P * B + P], ident)
                        full(dve_banks, ins)
                    for o in range(2):
                        heads = range(o, 8, 2)
                        for left, right in ((beta, kappa), (kappa, beta), (key, kappa), (beta, r_e), (key, r_e)):
                            bank = dve_banks.claim(pe)
                            for q, h in enumerate(heads):
                                ins = mm(bank[:, P * q:P * q + P], head(left, h, B), head(right, h, B), True, True)
                            full(dve_banks, ins)
                        dve_banks.settled(pe)
                        bank = dve_banks.claim(pe)
                        for q, h in enumerate(heads):
                            ins = mm(bank[:, 64 * q:64 * q + 64], Nt[:, q, :], v_tok[:, h, :], True, True)
                        full(dve_banks, ins)
                        for j in range(4):
                            if j:
                                pe.wait_ge(dve_banks.freed.sem, powers_in)
                            Pj, Ptj = P0[j % 2], Pt0[j % 2]
                            todo = []
                            if j < 3:
                                todo.append(lambda q, h: (Pj[:, q, :], Ptj[:, q, :]))
                            if j < 2:
                                todo.append(lambda q, h: (Ptj[:, q, :], Pj[:, q, :]))
                            z_in = dve_banks.filling
                            for f in todo:
                                bank = dve_banks.claim(pe)
                                for q, h in enumerate(heads):
                                    ins = mm(bank[:, P * q:P * q + P], *f(q, h), True, True)
                                full(dve_banks, ins)
                            powers_in = dve_banks.filling
                            pe.wait_ge(dve_banks.freed.sem, z_in)
                            bank = dve_banks.claim(pe)
                            for q, h in enumerate(heads):
                                ins = mm(bank[:, P * q:P * q + P], Ptj[:, q, :], Z[:, h, :], True, True)
                            full(dve_banks, ins)
                        dve_banks.settled(pe)
                        for q, h in enumerate(heads):
                            dve_to_pe.wait(pe)
                            base = 64 * o
                            flat = lambda a: a.rearrange("p c e -> p (c e)")
                            sp3 = spread[:, q % 2]
                            bank = act_banks.claim(pe)
                            mm(bank[0:64, :], eye(h), flat(DI[:, h // 2])[base:base + 64, :], True, False)
                            full(act_banks, mm(bank[0:64, :], Z[:, h, 0:64], flat(sp3[:, 0]), False, True))
                            bank = act_banks.claim(pe)
                            mm(bank[0:64, :], ke_tok[:, 64 * h:64 * h + 64], flat(sp3[:, 1]), True, False)
                            full(act_banks, mm(bank[0:64, :], beta_tok[:, 64 * h:64 * h + 64], flat(sp3[:, 2]), False, True))
                    act_banks.settled(pe)
                    dve_banks.settled(pe)
                    dve_to_pe.wait(pe)
                    for c in range(NCH):
                        dve_banks.settled(pe)
                        bank = dve_banks.claim(pe)
                        for h in range(8):
                            ins = mm(bank[0:64, 64 * h:64 * h + 64], GT[0:64, h, c, :], S[0:64, c, h, :], True, True)
                        full(dve_banks, ins)
                    for o in range(2):
                        heads = range(o, 8, 2)
                        bank = dve_banks.claim(pe)
                        for q, h in enumerate(heads):
                            mm(bank[0:64, P * q:P * q + P], eye(h), head(r_e, h, B), True, False)
                            ins = mm(bank[0:64, P * q:P * q + P], Z[:, h, 0:64], Y1[:, h, :], False, True)
                        full(dve_banks, ins)
                        dve_banks.settled(pe)
                        bank = dve_banks.claim(pe)
                        for q, h in enumerate(heads):
                            mm(bank[0:64, P * q:P * q + P], v_tok[:, h, :], Y2[:, h, :], True, False)
                            mm(bank[0:64, P * q:P * q + P], Z[:, h, 64:P], Y1[:, h, :], False, False)
                            for c in range(NCH):
                                ins = mm(bank[0:64, P * q + CH * c:P * q + CH * c + CH], S[0:64, c, h, :],
                                         R[0:64, q, CH * c:CH * c + CH], False, c == NCH - 1)
                        full(dve_banks, ins)
                        dve_banks.settled(pe)
                column_sums_pe(const("pair_ones"), obT)
                column_sums_pe(const("pair_ones"), e_post[0])

            def dve_part():
                tell(V, dve_to_sp)
                pool_to_dve.wait(dve)
                V(dve.tensor_tensor(kk, k_raw, last(col("kk"), SEQ), ALU.mult))
                V(dve.tensor_tensor(e4[:, 0], kk, kk, ALU.mult))
                column_sums_dve(lambda k, bk: dve.tensor_scalar(e4[:, 1, k, :], bk, 1e-24, None, ALU.max))
                tell(V, dve_to_act)
                for kind in range(3):
                    for j in range(2):
                        bk = dve_banks.take(dve)
                        for m in range(2):
                            jj = 2 * j + m
                            src = bk[:, SEQ * m:SEQ * m + SEQ]
                            s = dve_banks.freed if m else None
                            if kind < 2:
                                c0 = col(("w0", "a0")[kind])[:, jj:jj + 1]
                                V(dve.tensor_scalar(za[:, kind, jj, :], src, c0, None, ALU.add), s)
                            else:
                                V(dve.tensor_copy(g[:, jj, :], src), s)
                act_to_dve.wait(dve)
                tell(V, dve_to_act)
                V(dve.tensor_tensor(kk, kk, e4[:, 1], ALU.mult))
                act_to_dve.wait(dve)
                V(dve.tensor_scalar(zz, zz, -float(np.exp(-0.5)), None, ALU.mult))
                V(dve.tensor_scalar(k2, aa, 1.0, None, ALU.subtract))
                V(dve.tensor_tensor(k2, k2, last(col("ka"), SEQ), ALU.mult))
                V(stt(k2, k2, 1.0, k_raw, ALU.add, ALU.mult))
                V(dve.tensor_tensor(e4[:, 0], ra, k2, ALU.mult))
                V(dve.tensor_tensor(e4[:, 0], e4[:, 0], last(col("rk"), SEQ), ALU.mult))
                column_sums_dve(lambda k, bk: dve.tensor_tensor(bonus[:, k, :], bk, v[:, k, :], ALU.mult))
                for j in range(HC):
                    V(dve.tensor_tensor_scan(b[:, j, :], const("restart"), zz[:, j, :], 0.0, ALU.mult, ALU.add))
                bc = chunks(b)
                end = bc[:, :, CH - 1:CH].broadcast_to([P, HC * SEQ // CH, CH])
                V(dve.tensor_tensor(e4[:, 0], b, zz, ALU.subtract))
                V(dve.tensor_tensor(chunks(e4[:, 3]), end, bc, ALU.subtract))
                tell(V, dve_to_act)
                act_to_dve.wait(dve)
                V(dve.tensor_tensor(kappa, kk, e4[:, 0], ALU.mult))
                V(stt(kk, kk, -1.0, aa, ALU.mult, ALU.mult))
                at = 0
                for dst, src, n in ((beta, kk, 1), (key, k2, 1), (r_e, ra, 2), (beta_end, kk, 3), (key_end, k2, 3)):
                    if n > at:
                        act_to_dve.wait(dve)
                        at = n
                    V(dve.tensor_tensor(dst, src, e4[:, n], ALU.mult))
                V(dve.tensor_copy(el.rearrange("p j c -> p (j c)"), chunks(e4[:, 2])[:, :, CH - 1]))
                V(dve.memset(S[:, 0], 0.0))
                tell(V, dve_to_pe)
                spreads, products0 = 0, act_at[0]
                for B in range(NX):
                    for dst in (Z[:, :, 0:64], ke_tok, beta_tok, v_tok):
                        bk = dve_banks.take(dve)
                        src = bk[:, :] if len(dst.shape) == 2 else bk[:, :].rearrange("p (h e) -> p h e", e=64)
                        V(dve.tensor_copy(dst, src), dve_banks.freed)
                    for m in range(HC):
                        V(dve.tensor_tensor(DI[:, m], mid(const("eye_pair"), NCH),
                                            last(el[:, m, NCH * B:NCH * B + NCH], 64), ALU.mult))
                    for o in range(2):
                        heads = range(o, 8, 2)
                        hs = slice(o, 8, 2)
                        quad = lambda bk: bk[:, :].rearrange("p (q t) -> p q t", q=4)
                        for dst, m in ((Pt0[0], "chunk_before_st"), (P0[0], "chunk_before_ts"), (Nt, "chunk_before_st"),
                                       (Y1[:, hs], "chunk_upto_st"), (Y2[:, hs], "chunk_upto_st")):
                            bk = dve_banks.take(dve)
                            V(dve.tensor_tensor(dst, quad(bk), mid(const(m), 4), ALU.mult), dve_banks.freed)
                        bk = dve_banks.take(dve)
                        V(dve.tensor_copy(Z[:, hs, 64:P], bk[:, 0:256].rearrange("p (q e) -> p q e", q=4)), dve_banks.freed)
                        for j in range(4):
                            if j < 3:
                                bk = dve_banks.take(dve)
                                V(dve.tensor_copy(Pt0[(j + 1) % 2], quad(bk)), dve_banks.freed)
                            if j < 2:
                                bk = dve_banks.take(dve)
                                V(dve.tensor_copy(P0[(j + 1) % 2], quad(bk)), dve_banks.freed)
                            bk = dve_banks.take(dve)
                            V(dve.tensor_tensor(Z[:, hs], Z[:, hs], quad(bk), ALU.add), dve_banks.freed)
                        for q, h in enumerate(heads):
                            if spreads >= 2:
                                dve.wait_ge(act_banks.full.sem, products0 + 2 * spreads - 2)
                            spreads += 1
                            for k, src in enumerate((beta_tok[:, 64 * h:64 * h + 64], v_tok[:, h, :], Z[:, h, 64:P])):
                                ins = dve.tensor_tensor(spread[:, q % 2, k], mid(src, NCH), last(const("chunk_of"), 64), ALU.mult)
                                if k == 2:
                                    V(ins)
                            tell(V, dve_to_pe)
                    if B:
                        V(dve.tensor_copy(S[0:64, 0], S[0:64, NCH]))
                    tell(V, dve_to_pe)
                    for c in range(NCH):
                        bk = dve_banks.take(dve)
                        V(dve.tensor_tensor(S[0:64, c + 1], bk[0:64, :].rearrange("p (h e) -> p h e", e=64),
                                            H[0:64, :, c, :], ALU.add), dve_banks.freed)
                    for o in range(2):
                        bk = dve_banks.take(dve)
                        V(dve.tensor_copy(R[0:64].rearrange("p q t -> p (q t)"), bk[0:64, :]), dve_banks.freed)
                        bk = dve_banks.take(dve)
                        V(dve.tensor_copy(obT[64 * o:64 * o + 64, :, P * B:P * B + P],
                                          bk[0:64, :].rearrange("p (m t) -> p m t", m=HC)), dve_banks.freed)
                column_sums_dve(lambda k, bk: stt(obT[:, k, :], bk, -1.0 / 64, obT[:, k, :]))
                V(dve.tensor_tensor(e_post[0], obT, obT, ALU.mult))
                column_sums_dve(lambda k, bk: dve.tensor_copy(e_post[1][:, k, :], bk))
                rms_rows(e_post[1], 1.0 / 64, LN_EPS)
                V(dve.tensor_tensor(obT, obT, e_post[1], ALU.mult))
                for j in range(HC):
                    V(dve.tensor_scalar(obT[:, j, :], obT[:, j, :], col("lnw")[:, j:j + 1], col("lnb")[:, j:j + 1],
                                        ALU.mult, ALU.add))
                V(dve.tensor_tensor(obT, obT, bonus, ALU.add))
                V(dve.tensor_tensor(obT, obT, g, ALU.mult))

            def act_part():
                pool_to_act.wait(act)
                A(act.activation(ur[0:64, 12, :], ur[0:64, 12, :], ACT.Tanh))
                A(act.activation(ur[:, 13, :], ur[:, 13, :], ACT.Sigmoid))
                tell(A, act_to_pe)
                dve_to_act.wait(act)
                A(act.activation(e4[:, 1], e4[:, 1], ACT.Ln))
                A(act.activation(e4[:, 1], e4[:, 1], ACT.Exp, scale=-0.5))
                A(act.activation(v, v_raw, ACT.Copy))
                tell(A, act_to_dve)
                exp_of(za, za, func=ACT.Sigmoid)
                dve_to_act.wait(act)
                for k, (src, sign) in enumerate(((e4[:, 0], 1.0), (b, -1.0), (b, 1.0), (e4[:, 3], 1.0))):
                    A(act.activation(e4[:, k], src, ACT.Exp, scale=sign))
                    tell(A, act_to_dve)
                for B in range(NX):
                    for o in range(2):
                        for h in range(o, 8, 2):
                            for dst in (GT, H):
                                bk = act_banks.take(act)
                                A(act.activation(dst[0:64, h].rearrange("p c e -> p (c e)"), bk[0:64, :], ACT.Copy),
                                  act_banks.freed)
                rsqrt_act(e_post[1])
            return dict(sp=sp_part, pe=pe_part, dve=dve_part, act=act_part)

        def out_stage(w, lhs):
            ps = [add_panel(krows(w, 512 * k, 512 * k + 512), KC, 512) for k in range(2)]

            def sp_part():
                for n in ps:
                    load_panel(n)

            def pe_part():
                dve_to_pe.wait(pe)
                for n in ps:
                    rows_of_panel(n, T2, 512, lhs)

            def dve_part():
                tell(V, dve_to_pe)
                residual_dve(T2, None)
            return dict(sp=sp_part, pe=pe_part, dve=dve_part)

        def mlp_stage(l):
            work = Space(*WORK2)
            uT = work.take(FFN // P, SEQ)
            ups = [add_panel(krows(d["w_up_2"][l], 512 * n, 512 * n + 512), KC, 512) for n in range(8)]
            downs = [add_panel(d["w_down_2"][l][512 * n:512 * n + 512, :].rearrange("(c p) n -> p c n", p=P), 4, D)
                     for n in range(8)]

            def sp_part():
                for n in ups + downs:
                    load_panel(n)

            def pe_part():
                for n in ups:
                    cols_of_panel(n, 4, SEQ)
                dve_banks.settled(pe)
                places = [(h, t) for h in range(2) for t in range(NX)]
                banks = [dve_banks.claim(pe) for _ in places]
                for m, n in enumerate(downs):
                    w = open_panel(pe, n)
                    for (h, t), bank in zip(places, banks):
                        for c in range(4):
                            ins = mm(bank[:, :], uT[:, 4 * m + c, P * t:P * t + P], w[:, c, 512 * h:512 * h + 512],
                                     m == 0 and c == 0, m == 7 and c == 3)
                        if m == 7:
                            full(dve_banks, ins)
                    pe_used(n)

            def dve_part():
                for j in range(FFN // P):
                    bk = dve_banks.take(dve)
                    V(dve.tensor_scalar(uT[:, j, :], bk[:, 0:SEQ], 0.0, None, ALU.max))
                    V(dve.tensor_tensor(uT[:, j, :], uT[:, j, :], uT[:, j, :], ALU.mult), dve_banks.freed)
                residual_dve(T2, None)
            return dict(sp=sp_part, pe=pe_part, dve=dve_part)

        def ple_stage(l):
            work = Space(*WORK2)
            pT = work.take(PLE // P, SEQ)
            gain = work.take(D)
            pp, gg = work.take(NX, D), work.take(NX, D)
            sq = work.take(D)
            xT = view(HT, KC, 512)
            ss = small[:, 0:NX]
            proj = add_panel(d["ple_proj_2"][l].rearrange("(c p) n -> p c n", p=P), PLE // P, D)
            gs = [add_panel(krows(d["ple_gate_2"][l], 512 * k, 512 * k + 512), KC, 512) for k in range(2)]

            def sp_part():
                dve_to_sp.wait(sp)
                load_table(f"ple{l}", (pT, d["pT"][l].rearrange("(c p) t -> p c t", p=P)),
                           (gain, d["ple_rows"][:, D * l:D * l + D]))
                for n in [proj] + gs:
                    load_panel(n)

            def pe_part():
                dve_to_pe.wait(pe)
                for t in range(NX):
                    for h in range(2):
                        b = dve_banks.claim(pe)
                        for j in range(4):
                            c = 4 * h + j
                            ins = pe.transpose(b[:, P * j:P * j + P], x[:, 2 + t, P * c:P * c + P], ident)
                        full(dve_banks, ins)
                table_in(pe, f"ple{l}")
                w = open_panel(pe, proj)
                for t in range(NX):
                    for h in range(2):
                        b = dve_banks.claim(pe)
                        for c in range(PLE // P):
                            ins = mm(b[:, :], pT[:, c, P * t:P * t + P], w[:, c, 512 * h:512 * h + 512],
                                     c == 0, c == PLE // P - 1)
                        full(dve_banks, ins)
                pe_used(proj)
                dve_banks.settled(pe)
                for n in gs:
                    rows_of_panel(n, range(NX), 512, ht, act_banks)

            def dve_part():
                tell(V, dve_to_sp)
                tell(V, dve_to_pe)
                for t in range(NX):
                    for h in range(2):
                        b = dve_banks.take(dve)
                        V(dve.tensor_copy(xT[:, 4 * h:4 * h + 4, P * t:P * t + P],
                                          b[:, :].rearrange("p (c t) -> p c t", c=4)), dve_banks.freed)
                for t in range(NX):
                    for h in range(2):
                        b = dve_banks.take(dve)
                        V(dve.tensor_copy(pp[:, t, 512 * h:512 * h + 512], b[:, :]), dve_banks.freed)
                for t in range(NX):
                    V(dve.tensor_tensor(sq, pp[:, t, :], pp[:, t, :], ALU.mult))
                    V(dve.tensor_reduce(ss[:, t:t + 1], sq, AX.X, ALU.add))
                rms_rows(ss, 1.0 / D)
                table_in(dve, f"ple{l}")
                for t in range(NX):
                    V(stt(pp[:, t, :], pp[:, t, :], ss[:, t:t + 1], gain, ALU.mult, ALU.mult))
                for h in range(2):
                    for t in range(NX):
                        c = slice(512 * h, 512 * h + 512)
                        act_to_dve.wait(dve)
                        V(dve.tensor_tensor(gg[:, t, c], gg[:, t, c], pp[:, t, c], ALU.mult))
                        V(dve.tensor_tensor(x[:, 2 + t, c], x[:, 2 + t, c], gg[:, t, c], ALU.add))

            def act_part():
                rsqrt_act(ss)
                for h in range(2):
                    for t in range(NX):
                        b = act_banks.take(act)
                        A(act.activation(gg[:, t, 512 * h:512 * h + 512], b[:, :], ACT.Sigmoid), act_banks.freed)
                        tell(A, act_to_dve)
            return dict(sp=sp_part, pe=pe_part, dve=dve_part, act=act_part)

        def causal_stage():
            work = Space(*WORK2)
            qkv = work.take(NX, 24, HEAD2)
            qT, kT = work.take(8, SEQ), work.take(8, SEQ)
            o = work.take(NX, D)
            s_sb, p_sb, pT = work.take(3, SEQ), work.take(2, SEQ), work.take(2, SEQ)
            mask = work.take(NX, SEQ)
            tmp = work.take(3072)
            ps = [add_panel(krows(d["w_qkv_2"][0], 512 * n, 512 * n + 512), KC, 512) for n in range(6)]
            units = [(h, t, t + 1) for h in range(8) for t in range(NX)]
            att = attention(units, HEAD2, lambda h, t: qT[:, h, P * t:P * t + P], lambda h, nk: kT[:, h, 0:P * nk],
                            lambda h, j: qkv[:, j, 16 + h, :], lambda h, t: o[:, t, P * h:P * h + P], HEAD2 ** -0.5,
                            lambda t, nk: mask[:, t, 0:P * nk], None, dict(s=s_sb, p=p_sb, pT=pT))

            def sp_part():
                dve_to_sp.wait(sp)
                o_, w_ = TABLES["causal"]
                load_table("causal", (mask.rearrange("p a b -> p (a b)"), d["tables"][:, o_:o_ + w_]))
                for n in ps:
                    load_panel(n)

            def pe_part():
                for n in ps:
                    rows_of_panel(n, range(NX), 512, ht)
                dve_to_pe.wait(pe)
                transposed_pe(lambda h, t: qkv[:, t, h, :], range(NX), range(16))
                dve_banks.settled(pe)
                att["pe"]()
                for t in range(NX):
                    for hf in range(2):
                        b = dve_banks.claim(pe)
                        for j in range(4):
                            c = 4 * hf + j
                            ins = pe.transpose(b[:, P * j:P * j + P], o[:, t, P * c:P * c + P], ident)
                        full(dve_banks, ins)
                dve_banks.settled(pe)

            def dve_part():
                tell(V, dve_to_sp)
                for n in range(6):
                    for t in range(NX):
                        b = dve_banks.take(dve)
                        V(dve.tensor_copy(qkv[:, t, 4 * n:4 * n + 4, :].rearrange("p h e -> p (h e)"), b[:, :]),
                          dve_banks.freed)
                    if n in (1, 3):
                        for t in range(NX):
                            head_norm_rope(qkv[:, t], range(4 * n - 4, 4 * n + 4),
                                           [(4 * n - 4, 4 * n + 4, row("q2" if n == 1 else "k2"))],
                                           const("cos2", NX, 64)[:, t], const("sin2", NX, 64)[:, t], HEAD2, tmp)
                tell(V, dve_to_pe)
                table_in(dve, "causal")
                transposed_dve(lambda h: qT[:, h, :] if h < 8 else kT[:, h - 8, :], range(NX), range(16))
                att["dve"]()
                for t in range(NX):
                    for hf in range(2):
                        b = dve_banks.take(dve)
                        V(dve.tensor_copy(hT[:, 4 * hf:4 * hf + 4, P * t:P * t + P],
                                          b[:, :].rearrange("p (c t) -> p c t", c=4)), dve_banks.freed)

            def act_part():
                for _ in range(2 * NX):
                    norm_act(8)
                att["act"]()
            return dict(sp=sp_part, pe=pe_part, dve=dve_part, act=act_part)

        def store_stage():
            def sp_part():
                dve_to_sp.wait(sp)
                sp.dma_start(d["out"].rearrange("a (t p) n -> p (a t) n", p=P), x[:, 2:4, :]).then_inc(out_written.sem, 16)
                sp.wait_ge(out_written.sem, 16)
            return dict(sp=sp_part, dve=lambda: tell(V, dve_to_sp))

        plan = [load_stage()]
        r = lambda t: t // 2
        for i in range(2):
            plan.append(mod_stage(i))
            plan.append(norm_stage(range(4), lambda c, t: norm_a[:, 0, c, r(t):r(t) + 1],
                                     lambda c, t: mod_col[:, c, r(t):r(t) + 1]))
            if i == 0:
                conv, bT = conv_stage()
                plan.append(conv)
                plan.append(attention_stage(0, d["w_in_ab"][0], d["w_out_ab"][0],
                                              lambda c, t: bT[:, c, P * t:P * t + P], (0, 1, 2, 3), ("qa", "ka"), False))
            else:
                pl, yT = pool_stage()
                plan.append(pl)
                plan.append(attention_stage(1, d["w_in_cd"][0], d["w_out_cd"][0],
                                              lambda c, t: yT[:, c, P * (t - 2):P * (t - 2) + P], (2, 3), ("qc", "kc"), True))
            plan.append(norm_stage(range(4) if i == 0 else (2, 3), lambda c, t: norm_a[:, 1, c, r(t):r(t) + 1],
                                     lambda c, t: mod_col[:, 24 + c, r(t):r(t) + 1],
                                     first_tile=0 if i == 0 else 2))
            plan.append(moe_stage(i, (0, 1, 2, 3) if i == 0 else (2, 3)))
        ring["n"] = 2
        oT = view(WORK2[0], HC, SEQ)
        obT = view(WORK2[0] + HC * SEQ, HC, SEQ)

        def norm2(name):
            return norm_stage((2, 3), lambda c, t: col(name)[:, c:c + 1], first_tile=2)
        for l in range(2):
            plan.append(norm2(f"an_{l}"))
            if l == 0:
                plan += [hgrn_stage(oT), rwkv_stage(obT)]
                plan.append(out_stage(d["w_out_ar_2"][0],
                                        lambda c, t: (oT if c < HC else obT)[:, c % HC, P * (t - 2):P * (t - 2) + P]))
            else:
                plan.append(causal_stage())
                plan.append(out_stage(d["w_o_attn_2"][0], lambda c, t: hT[:, c, P * (t - 2):P * (t - 2) + P]))
            plan += [norm2(f"mn_{l}"), mlp_stage(l), ple_stage(l)]
        plan.append(store_stage())

        @block.sync
        def _(_sp):
            for stage in plan:
                stage.get("sp", lambda: None)()

        @block.tensor
        def _(_pe):
            for stage in plan:
                stage.get("pe", lambda: None)()

        @block.vector
        def _(_dve):
            for stage in plan:
                stage.get("dve", lambda: None)()

        @block.scalar
        def _(_act):
            for stage in plan:
                stage.get("act", lambda: None)()

        @block.gpsimd
        def _(_pool):
            for stage in plan:
                stage.get("pool", lambda: None)()


def shape_tables():
    c = np.zeros((P, NCONST), np.float32)
    t = np.zeros((P, NTABLE), np.float32)

    def put(a, name, v):
        where, arr = (CONSTS, c) if a == "c" else (TABLES, t)
        o, w = where[name]
        arr[:, o:o + w] = np.broadcast_to(np.asarray(v, np.float32).reshape(np.shape(v)[0], -1), (P, w))
    i = np.arange(P)
    p_, q_ = i[:, None], i[None, :]
    same = p_ // CH == q_ // CH
    put("c", "ident", np.eye(P))
    put("c", "ones", np.ones((P, P)))
    put("c", "before", p_ < q_)
    put("c", "pair_ones", p_ // 64 == q_ // 64)
    put("c", "chunk_before_st", same & (p_ < q_))
    put("c", "chunk_before_ts", same & (q_ < p_))
    put("c", "chunk_upto_st", same & (p_ <= q_))
    put("c", "chunk_of", p_ // CH == np.arange(NCH)[None])
    put("c", "restart", np.broadcast_to((np.arange(SEQ) % CH != 0)[None], (P, SEQ)))
    tok = np.arange(SEQ)
    inv = (np.float32(10000.0) ** (-np.arange(16, dtype=np.float32) / np.float32(16))).astype(np.float32)
    ang = np.concatenate([(tok // 64).astype(np.float32)[:, None] * inv, (tok % 64).astype(np.float32)[:, None] * inv], -1)
    cos = np.concatenate([np.ones((2, P, 32)), np.cos(ang).reshape(2, P, 32)]).transpose(1, 0, 2)
    sin = np.concatenate([np.zeros((2, P, 32)), np.sin(ang).reshape(2, P, 32)]).transpose(1, 0, 2)
    put("c", "cos", cos)
    put("c", "sin", sin)
    inv = (np.float32(10000.0) ** (-np.arange(64, dtype=np.float32) / np.float32(64))).astype(np.float32)
    ang = tok.astype(np.float32)[:, None] * inv[None]
    put("c", "cos2", np.cos(ang).reshape(2, P, 64).transpose(1, 0, 2))
    put("c", "sin2", np.sin(ang).reshape(2, P, 64).transpose(1, 0, 2))
    put("c", "expert", np.broadcast_to(np.arange(NEXP)[None], (P, NEXP)))
    put("c", "eps", np.full((P, 1), EPS))
    put("c", "eye_pair", p_ % 64 == np.arange(64)[None])
    put("c", "group", np.broadcast_to((np.arange(NEXP) // EPG)[None], (P, NEXP)))
    put("c", "token", np.arange(4)[None] * P + p_)
    sel = np.zeros((P, 2, P))
    sel[0, 0] = sel[1, 1] = 1
    put("c", "rowsel", sel)
    qpos = np.arange(SEQ)
    far = np.where(np.abs(qpos[:, None] - qpos[None]) <= 128, 0.0, -BIG)
    band = np.concatenate([np.zeros((SEQ, SEQ)), far], 1)
    put("t", "band", band.reshape(NX, P, 512).transpose(1, 0, 2))
    causal = np.where(qpos[None] <= qpos[:, None], 0.0, -BIG)
    put("t", "causal", causal.reshape(NX, P, SEQ).transpose(1, 0, 2))
    pm = np.zeros((SEQ, 4, SEQ))
    for g, w in enumerate((2, 4, 8, 16)):
        for s in range(SEQ):
            lo, hi = max(s - w // 2, 0), min(s - w // 2 + w, SEQ)
            pm[lo:hi, g, s] = 1.0 / (hi - lo)
            pm[s, g, s] -= 1.0
    put("t", "pool", pm.reshape(NX, P, 4, SEQ).transpose(1, 0, 2, 3))
    return c, t


def layout(v):
    def dcol(a):
        return a.reshape(-1, P).T
    cols = {
        "ln1_0": dcol(v["ln1_g"][0]), "ln1_1": dcol(v["ln1_g"][1]),
        "ln2_0": dcol(v["ln2_g"][0]), "ln2_1": dcol(v["ln2_g"][1]),
        "cond": np.stack([dcol(v["c_ctx"]), dcol(v["c"][0])], -1).reshape(P, -1),
        "conv_w": v["conv_w"][0].reshape(TAPS, HC, P).transpose(2, 1, 0).reshape(P, -1),
        "conv_b": dcol(v["conv_b"][0]), "conv_g": dcol(v["conv_ln_g"][0]), "conv_lb": dcol(v["conv_ln_b"][0]),
        "pool_scale": dcol(v["pool_scale"][0]),
        "an_0": dcol(v["attn_norm_2"][0]), "an_1": dcol(v["attn_norm_2"][1]),
        "mn_0": dcol(v["mlp_norm_2"][0]), "mn_1": dcol(v["mlp_norm_2"][1]),
        "lb": v["hgrn_lb_2"].reshape(3 * HC, P).T, "onorm": dcol(v["hgrn_onorm_2"][0]), "mu": dcol(v["rwkv_mu_2"][0]),
        "w0": dcol(v["rwkv_w0_2"][0]), "a0": dcol(v["rwkv_a0_2"][0]), "kk": dcol(v["rwkv_kk_2"][0]),
        "ka": dcol(v["rwkv_ka_2"][0]), "rk": dcol(v["rwkv_rk_2"][0]),
        "lnw": dcol(v["rwkv_ln_w_2"][0]), "lnb": dcol(v["rwkv_ln_b_2"][0]),
    }
    rows = {
        "qa": v["q_norm_a"][0], "ka": v["k_norm_a"][0], "qc": v["q_norm_c"][0], "kc": v["k_norm_c"][0],
        "q2": v["q_norm_2"][0], "k2": v["k_norm_2"][0], "sink": v["sink_c"][0],
        "rtb_0": np.concatenate([v["rt_grp_b"][0], v["rt_exp_b"][0]]),
        "rtb_1": np.concatenate([v["rt_grp_b"][1], v["rt_exp_b"][1]]),
    }
    out = {
        "cols": np.concatenate([cols[k] for k in COLS], 1),
        "rows": np.repeat(np.concatenate([rows[k] for k in ROWS])[None], P, 0),
        "mod_b": np.repeat(v["mod_b"][:, None], 2, 1),
        "rt_w": np.concatenate([v["rt_grp_w"], v["rt_exp_w"]], -1),
        "ple_rows": np.repeat(v["ple_norm_2"].reshape(1, -1), P, 0),
        "pT": v["p_2"][:, 0].transpose(0, 2, 1),
    }
    return {k: np.ascontiguousarray(a) for k, a in out.items()}


DIRECT = ["x", "ctx", "mod_w", "w_in_ab", "w_out_ab", "w_in_cd", "w_out_cd", "pool_w", "ex_gate", "ex_up",
          "ex_down", "w_in_ar_2", "w_out_ar_2", "rwkv_w2_2", "rwkv_a2_2", "rwkv_g2_2", "w_qkv_2", "w_o_attn_2",
          "w_up_2", "w_down_2", "ple_proj_2", "ple_gate_2"]


def kernel(**inputs):
    import concourse.bacc as bacc
    from concourse.bass_utils import run_bass_kernel_spmd as run

    nc = bacc.Bacc("TRN2", target_bir_lowering=False, num_devices=1)
    v = {k: np.asarray(a) for k, a in inputs.items()}
    consts, tables = shape_tables()
    arrays = {**{k: np.ascontiguousarray(v[k]) for k in DIRECT}, **layout(v), "consts": consts, "tables": tables}
    d = {k: nc.dram_tensor(f"in_{k}", a.shape, F32, kind="ExternalInput").ap() for k, a in arrays.items()}
    d["out"] = nc.dram_tensor("out_x", (1, SEQ, D), F32, kind="ExternalOutput").ap()
    build_program(nc, d)
    return run(nc, [{f"in_{k}": a for k, a in arrays.items()}], core_ids=[0]).results[0]["out_x"]
```
